# Optimizing a Trainium2 kernel written in Bass

```python
import math
import jax, jax.numpy as jnp
from jax import lax
import numpy as np

D_MODEL = 1024
BATCH = 1
SEQ = 512
DEPTH = 2
DEC_BATCH = 8
DEC_SEQ = 16
PAST_LEN = 512

CHUNK = 64
N_AB = (DEPTH + 1) // 2
N_ATT = DEPTH // 2
D_A = D_MODEL // 2
HEAD_A = 64
H_A = D_A // HEAD_A
DECAY_LORA = 64
AAA_LORA = 64
GATE_LORA = 128
A_COLS = 3 * D_A + DECAY_LORA + AAA_LORA + GATE_LORA
LNX_EPS = 64e-5
D_B = D_MODEL - D_A
GROUP_CH = 16
N_GROUPS = D_B // GROUP_CH
P_STATE = 64
AB_COLS = A_COLS + D_B
HEAD_DIM = 64
N_HEADS = D_MODEL // HEAD_DIM
N_KV = 4
GQ = N_HEADS // N_KV
WINDOW = 128
WIN_CHUNKS = WINDOW // CHUNK
WIN_BUF = min(WINDOW, PAST_LEN)
QKV_COLS = (N_HEADS + 2 * N_KV) * HEAD_DIM
SCALE = HEAD_DIM ** -0.5
D_FF = 4 * D_MODEL
RMS_EPS = 1e-6

kernel_name = 'hybrid_rwkv7_s5_swa_stream_step'

def rms_norm(x, g):
    xf = x.astype(jnp.float32)
    y = xf * lax.rsqrt(jnp.mean(xf * xf, axis=-1, keepdims=True) + RMS_EPS)
    return (y * g.astype(jnp.float32)).astype(x.dtype)

def rwkv7_mix(za, shift_prev, s0, p):
    bsz, t, _ = za.shape
    f32 = jnp.float32
    z_prev = jnp.concatenate([shift_prev[:, None].astype(za.dtype), za[:, :-1]], axis=1)
    zs = za + p['mu'] * (z_prev - za)
    cuts = [D_A, 2 * D_A, 3 * D_A, 3 * D_A + DECAY_LORA, 3 * D_A + DECAY_LORA + AAA_LORA]
    r, k, v, wl, al, gl = jnp.split(zs, cuts, axis=-1)
    w = -jax.nn.softplus(-(p['w0'] + jnp.tanh(wl) @ p['w2']).astype(f32)) - 0.5
    decay = jnp.exp(-jnp.exp(w))
    a = jax.nn.sigmoid((p['a0'] + al @ p['a2']).astype(f32))
    g = (jax.nn.sigmoid(gl) @ p['g2']).astype(f32)

    def heads(u):
        return u.astype(f32).reshape(bsz, t, H_A, HEAD_A)

    r, k, v, decay, a = heads(r), heads(k), heads(v), heads(decay), heads(a)
    kk = k * p['k_k'].astype(f32).reshape(H_A, HEAD_A)
    kk = kk / jnp.maximum(jnp.sqrt(jnp.sum(kk * kk, axis=-1, keepdims=True)), 1e-12)
    k = k * (1.0 + (a - 1.0) * p['k_a'].astype(f32).reshape(H_A, HEAD_A))
    b_vec = kk * a

    def step(S, inp):
        r_t, w_t, k_t, v_t, kk_t, b_t = inp
        sa = jnp.einsum('bhvk,bhk->bhv', S, -kk_t)
        S = S * w_t[:, :, None, :] + sa[..., None] * b_t[:, :, None, :] + v_t[..., None] * k_t[:, :, None, :]
        return S, jnp.einsum('bhvk,bhk->bhv', S, r_t)

    xs = tuple(jnp.moveaxis(u, 1, 0) for u in (r, decay, k, v, kk, b_vec))
    s_final, o = lax.scan(step, s0.astype(f32), xs)
    o = jnp.moveaxis(o, 0, 1)
    mu = jnp.mean(o, axis=-1, keepdims=True)
    var = jnp.mean(jnp.square(o - mu), axis=-1, keepdims=True)
    o = ((o - mu) * lax.rsqrt(var + LNX_EPS)).reshape(bsz, t, D_A) * p['lnx_w'] + p['lnx_b']
    bonus = jnp.sum(r * k * p['r_k'].astype(f32), axis=-1, keepdims=True) * v
    o = (o + bonus.reshape(bsz, t, D_A)) * g
    return o.astype(za.dtype), za[:, -1], s_final

def s5_mix(u, h0_re, h0_im, p):
    bsz, t, _ = u.shape
    f32 = jnp.float32
    lam = lax.complex(jnp.minimum(p['lam_re'].astype(f32), -1e-4), p['lam_im'].astype(f32))
    dt = jnp.exp(p['log_dt'].astype(f32))[:, None]
    lam_dt = lam * dt
    lam_bar = jnp.exp(lam_dt)
    b = lax.complex(p['b_re'].astype(f32), p['b_im'].astype(f32))
    b_bar = ((lam_bar - 1.0) / lam)[..., None] * b
    uf = u.astype(f32)
    bu = jnp.einsum('gpc,btgc->btgp', b_bar, uf.reshape(bsz, t, N_GROUPS, GROUP_CH))
    cnt = jnp.ones((1, t, 1, 1), f32)

    def combine(e1, e2):
        n1, b1 = e1
        n2, b2 = e2
        return n1 + n2, jnp.exp(n2 * lam_dt) * b1 + b2

    _, h = lax.associative_scan(combine, (cnt, bu), axis=1)
    if h0_re is not None:
        h0 = lax.complex(h0_re.astype(f32), h0_im.astype(f32))
        pos = jnp.arange(1, t + 1, dtype=f32)[None, :, None, None]
        h = h + jnp.exp(pos * lam_dt) * h0[:, None]
    c = lax.complex(p['c_re'].astype(f32), p['c_im'].astype(f32))
    y = jnp.real(jnp.einsum('gcp,btgp->btgc', c, h)).reshape(bsz, t, D_B) + p['d'].astype(f32) * uf
    y = jax.nn.gelu(y)
    y = y * jax.nn.sigmoid(y @ p['w_glu'].astype(f32))
    h_last = h[:, -1]
    return y.astype(u.dtype), jnp.real(h_last), jnp.imag(h_last)

def ab_layer(x, g_norm, p, shift_prev, s_rwkv, h_re, h_im):
    z = rms_norm(x, g_norm) @ p['w_in']
    oa, shift_new, s_new = rwkv7_mix(z[..., :A_COLS], shift_prev, s_rwkv, p)
    ob, hr, hi = s5_mix(z[..., A_COLS:], h_re, h_im, p)
    y = x + jnp.concatenate([oa, ob], axis=-1) @ p['w_out']
    return y, s_new, shift_new, hr, hi

def qkv_heads(x, g_norm, p):
    bsz, t, _ = x.shape
    qkv = rms_norm(x, g_norm) @ p['w_qkv']
    q, k, v = jnp.split(qkv, [N_HEADS * HEAD_DIM, (N_HEADS + N_KV) * HEAD_DIM], axis=-1)
    q = rms_norm(q.reshape(bsz, t, N_KV, GQ, HEAD_DIM), p['q_norm'])
    k = rms_norm(k.reshape(bsz, t, N_KV, HEAD_DIM), p['k_norm'])
    return q, k, v.reshape(bsz, t, N_KV, HEAD_DIM)

def sink_softmax(s, valid, sink):
    s = jnp.where(valid, s, -jnp.inf)
    m = jnp.maximum(jnp.max(s, axis=-1, keepdims=True), sink)
    e = jnp.exp(s - m)
    return e / (jnp.sum(e, axis=-1, keepdims=True) + jnp.exp(sink - m))

def band_chunks(u):
    nc = u.shape[1]
    up = jnp.concatenate([jnp.zeros_like(u[:, :WIN_CHUNKS - 1]), u], axis=1)
    return jnp.concatenate([up[:, j:j + nc] for j in range(WIN_CHUNKS)], axis=2)

def attn_prompt(x, g_norm, p):
    bsz, t, _ = x.shape
    nc = t // CHUNK
    f32 = jnp.float32
    q, k, v = qkv_heads(x, g_norm, p)
    qc = q.reshape(bsz, nc, CHUNK, N_KV, GQ, HEAD_DIM).astype(f32)
    kb = band_chunks(k.reshape(bsz, nc, CHUNK, N_KV, HEAD_DIM)).astype(f32)
    vb = band_chunks(v.reshape(bsz, nc, CHUNK, N_KV, HEAD_DIM)).astype(f32)
    s = jnp.einsum('bnqkgd,bnskd->bnkgqs', qc, kb) * SCALE
    key_chunk = jnp.arange(nc)[:, None] - (WIN_CHUNKS - 1) + (jnp.arange(WIN_CHUNKS * CHUNK) // CHUNK)[None, :]
    valid = (key_chunk >= 0)[None, :, None, None, None, :]
    sink = p['sinks'].astype(f32).reshape(N_KV, GQ)[:, :, None, None]
    pr = sink_softmax(s, valid, sink)
    o = jnp.einsum('bnkgqs,bnskd->bnqkgd', pr, vb).reshape(bsz, t, N_HEADS * HEAD_DIM)
    y = x + o.astype(x.dtype) @ p['w_out']
    return y, k[:, t - WIN_BUF:], v[:, t - WIN_BUF:]

def attn_sample(x, g_norm, p, ck, cv):
    bsz, t, _ = x.shape
    f32 = jnp.float32
    q, k, v = qkv_heads(x, g_norm, p)
    kf = jnp.concatenate([ck.astype(k.dtype), k], axis=1)
    vf = jnp.concatenate([cv.astype(v.dtype), v], axis=1)
    qpos = PAST_LEN + jnp.arange(t)
    kpos = PAST_LEN - WIN_BUF + jnp.arange(WIN_BUF + t)
    diff = qpos[:, None] // CHUNK - kpos[None, :] // CHUNK
    valid = (diff >= 0) & (diff < WIN_CHUNKS) & (kpos[None, :] >= 0)
    s = jnp.einsum('bqkgd,bskd->bkgqs', q.astype(f32), kf.astype(f32)) * SCALE
    sink = p['sinks'].astype(f32).reshape(N_KV, GQ)[:, :, None, None]
    pr = sink_softmax(s, valid, sink)
    o = jnp.einsum('bkgqs,bskd->bqkgd', pr, vf.astype(f32)).reshape(bsz, t, N_HEADS * HEAD_DIM)
    y = x + o.astype(x.dtype) @ p['w_out']
    return y, kf[:, t:], vf[:, t:]

def ffn(x, g_norm, w1, w2):
    h = jnp.square(jax.nn.relu(rms_norm(x, g_norm) @ w1))
    return x + h @ w2

def setup_inputs(seed: int = 0) -> dict:
    key = jax.random.key(seed)
    ks = iter(jax.random.split(key, 48))

    def nrm(shape, scale):
        return scale * jax.random.normal(next(ks), shape, jnp.float32)

    def uni(shape, lo, hi):
        return jax.random.uniform(next(ks), shape, jnp.float32, lo, hi)

    n_idx = jnp.arange(P_STATE, dtype=jnp.float32)[None, None, :]
    return {
        'x_prompt': nrm((BATCH, SEQ, D_MODEL), 1.0),
        'x_sample': nrm((DEC_BATCH, DEC_SEQ, D_MODEL), 1.0),
        'state_rwkv': nrm((N_AB, DEC_BATCH, H_A, HEAD_A, HEAD_A), 0.5),
        'state_shift': nrm((N_AB, DEC_BATCH, A_COLS), 1.0),
        'state_ssm_re': nrm((N_AB, DEC_BATCH, N_GROUPS, P_STATE), 0.1),
        'state_ssm_im': nrm((N_AB, DEC_BATCH, N_GROUPS, P_STATE), 0.1),
        'cache_k': nrm((N_ATT, DEC_BATCH, WIN_BUF, N_KV, HEAD_DIM), 1.0),
        'cache_v': nrm((N_ATT, DEC_BATCH, WIN_BUF, N_KV, HEAD_DIM), 1.0),
        'norm_mix': 1.0 + nrm((DEPTH, D_MODEL), 0.02),
        'norm_ffn': 1.0 + nrm((DEPTH, D_MODEL), 0.02),
        'ab_w_in': nrm((N_AB, D_MODEL, AB_COLS), D_MODEL ** -0.5),
        'ab_mu': uni((N_AB, A_COLS), 0.0, 1.0),
        'rwkv_w0': uni((N_AB, D_A), -6.0, 0.0),
        'rwkv_w2': nrm((N_AB, DECAY_LORA, D_A), 0.1 * DECAY_LORA ** -0.5),
        'rwkv_a0': nrm((N_AB, D_A), 0.1),
        'rwkv_a2': nrm((N_AB, AAA_LORA, D_A), 0.1 * AAA_LORA ** -0.5),
        'rwkv_g2': nrm((N_AB, GATE_LORA, D_A), GATE_LORA ** -0.5),
        'rwkv_k_k': 0.85 + nrm((N_AB, D_A), 0.02),
        'rwkv_k_a': 1.0 + nrm((N_AB, D_A), 0.02),
        'rwkv_r_k': nrm((N_AB, H_A, HEAD_A), 0.1),
        'rwkv_lnx_w': 1.0 + nrm((N_AB, D_A), 0.02),
        'rwkv_lnx_b': nrm((N_AB, D_A), 0.02),
        's5_lam_re': -0.5 + nrm((N_AB, N_GROUPS, P_STATE), 0.01),
        's5_lam_im': math.pi * n_idx + nrm((N_AB, N_GROUPS, P_STATE), 0.01),
        's5_log_dt': uni((N_AB, N_GROUPS), math.log(1e-3), math.log(1e-1)),
        's5_b_re': nrm((N_AB, N_GROUPS, P_STATE, GROUP_CH), (2 * GROUP_CH) ** -0.5),
        's5_b_im': nrm((N_AB, N_GROUPS, P_STATE, GROUP_CH), (2 * GROUP_CH) ** -0.5),
        's5_c_re': nrm((N_AB, N_GROUPS, GROUP_CH, P_STATE), (2 * P_STATE) ** -0.5),
        's5_c_im': nrm((N_AB, N_GROUPS, GROUP_CH, P_STATE), (2 * P_STATE) ** -0.5),
        's5_d': nrm((N_AB, D_B), 1.0),
        's5_w_glu': nrm((N_AB, D_B, D_B), D_B ** -0.5),
        'ab_w_out': nrm((N_AB, D_A + D_B, D_MODEL), (D_A + D_B) ** -0.5),
        'att_w_qkv': nrm((N_ATT, D_MODEL, QKV_COLS), D_MODEL ** -0.5),
        'att_q_norm': 1.0 + nrm((N_ATT, HEAD_DIM), 0.02),
        'att_k_norm': 1.0 + nrm((N_ATT, HEAD_DIM), 0.02),
        'att_sinks': nrm((N_ATT, N_HEADS), 0.5),
        'att_w_out': nrm((N_ATT, N_HEADS * HEAD_DIM, D_MODEL), (N_HEADS * HEAD_DIM) ** -0.5),
        'ffn_w1': nrm((DEPTH, D_MODEL, D_FF), D_MODEL ** -0.5),
        'ffn_w2': nrm((DEPTH, D_FF, D_MODEL), D_FF ** -0.5),
    }

def reference(x_prompt, x_sample, state_rwkv, state_shift, state_ssm_re, state_ssm_im, cache_k, cache_v,
              norm_mix, norm_ffn, ab_w_in, ab_mu, rwkv_w0, rwkv_w2, rwkv_a0, rwkv_a2, rwkv_g2,
              rwkv_k_k, rwkv_k_a, rwkv_r_k, rwkv_lnx_w, rwkv_lnx_b,
              s5_lam_re, s5_lam_im, s5_log_dt, s5_b_re, s5_b_im, s5_c_re, s5_c_im, s5_d, s5_w_glu,
              ab_w_out, att_w_qkv, att_q_norm, att_k_norm, att_sinks, att_w_out, ffn_w1, ffn_w2):
    xp, xs = x_prompt, x_sample
    bp = xp.shape[0]
    p_rwkv, p_shift, p_re, p_im, p_k, p_v = [], [], [], [], [], []
    s_rwkv, s_shift, s_re, s_im, s_k, s_v = [], [], [], [], [], []
    for layer in range(DEPTH):
        i = layer // 2
        if layer % 2 == 0:
            pab = dict(w_in=ab_w_in[i], w_out=ab_w_out[i], mu=ab_mu[i], w0=rwkv_w0[i], w2=rwkv_w2[i],
                       a0=rwkv_a0[i], a2=rwkv_a2[i], g2=rwkv_g2[i], k_k=rwkv_k_k[i], k_a=rwkv_k_a[i],
                       r_k=rwkv_r_k[i], lnx_w=rwkv_lnx_w[i], lnx_b=rwkv_lnx_b[i],
                       lam_re=s5_lam_re[i], lam_im=s5_lam_im[i], log_dt=s5_log_dt[i],
                       b_re=s5_b_re[i], b_im=s5_b_im[i], c_re=s5_c_re[i], c_im=s5_c_im[i],
                       d=s5_d[i], w_glu=s5_w_glu[i])
            zero_shift = jnp.zeros((bp, A_COLS), xp.dtype)
            zero_rwkv = jnp.zeros((bp, H_A, HEAD_A, HEAD_A), jnp.float32)
            xp, st, sh, hr, hi = ab_layer(xp, norm_mix[layer], pab, zero_shift, zero_rwkv, None, None)
            p_rwkv.append(st); p_shift.append(sh); p_re.append(hr); p_im.append(hi)
            xs, st, sh, hr, hi = ab_layer(xs, norm_mix[layer], pab, state_shift[i], state_rwkv[i],
                                          state_ssm_re[i], state_ssm_im[i])
            s_rwkv.append(st); s_shift.append(sh); s_re.append(hr); s_im.append(hi)
        else:
            pat = dict(w_qkv=att_w_qkv[i], q_norm=att_q_norm[i], k_norm=att_k_norm[i],
                       sinks=att_sinks[i], w_out=att_w_out[i])
            xp, kn, vn = attn_prompt(xp, norm_mix[layer], pat)
            p_k.append(kn); p_v.append(vn)
            xs, kn, vn = attn_sample(xs, norm_mix[layer], pat, cache_k[i], cache_v[i])
            s_k.append(kn); s_v.append(vn)
        xp = ffn(xp, norm_ffn[layer], ffn_w1[layer], ffn_w2[layer])
        xs = ffn(xs, norm_ffn[layer], ffn_w1[layer], ffn_w2[layer])
    return (xp, xs,
            jnp.stack(p_rwkv), jnp.stack(p_shift), jnp.stack(p_re), jnp.stack(p_im),
            jnp.stack(p_k), jnp.stack(p_v),
            jnp.stack(s_rwkv), jnp.stack(s_shift), jnp.stack(s_re), jnp.stack(s_im),
            jnp.stack(s_k), jnp.stack(s_v))


_drawn_inputs = setup_inputs


def setup_inputs(seed=0):
    import zlib

    import numpy as np

    out = dict(_drawn_inputs(seed))
    spreads = {}
    factors = {'rwkv_w2': 8.0,
     'rwkv_k_k': 2.832,
     'rwkv_k_a': 2.93,
     'rwkv_lnx_w': 7.08,
     'rwkv_lnx_b': 7.155,
     's5_lam_re': 14.989,
     's5_c_re': 3.239,
     's5_c_im': 3.207,
     'att_q_norm': 8.0,
     'att_k_norm': 3.349,
     'att_sinks': 64.0}
    for name, (base, spread) in spreads.items():
        noise = np.random.default_rng([zlib.crc32(name.encode()), seed]).standard_normal(out[name].shape)
        drawn = base * np.exp(spread * noise) if base else spread * noise
        out[name] = __import__('jax').numpy.asarray(drawn.astype(out[name].dtype))
    for name, factor in factors.items():
        out[name] = (out[name] * factor).astype(out[name].dtype)
    return out
```

```python
from contextlib import ExitStack

import concourse.bass as bass
from concourse import mybir

F32 = mybir.dt.float32
F32R = mybir.dt.float32r
ALU = mybir.AluOpType
ACT = mybir.ActivationFunctionType
AX = mybir.AxisListType

P = 128
D = 1024
KT = D // P
NP_TOK, NB, ST = 512, 8, 16
T = NP_TOK + NB * ST
HALF = T // 2
NPAIR = 4
A_TILES = 14
ZW = 1 + NP_TOK + NB * (1 + ST)
CH = 64
NCH = NP_TOK // CH
L5 = 8
NC5 = T // L5
NCP = NP_TOK // L5
NPR5 = 16
SLOT = 2048
FF_TILES = 16
KEYS = 80
EXPM05 = 0.6065306597126334
GELU_C = 0.7978845608028654
TWO_PI_HI, TWO_PI_LO = 6.28125, 0.0019353071795864769
ROUND = 12582912.0

N_IN, N_OUT, N_FF, N_QKV = 9, 4, 8, 6
SLOTS = N_IN + N_OUT + 4 * N_FF + N_QKV + N_OUT + 4 * N_FF
IN_TILES = [12, 13, 14, 15, 16, 17, 0, 1, 4, 5, 8, 9, 2, 3, 6, 7, 10, 11]

PRM = {}
_at = 0
for _name, _n in (("mu", 14), ("w0", 4), ("a0", 4), ("k_k", 4), ("k_a", 4), ("r_k", 4), ("lnw", 4), ("lnb", 4),
                  ("g", 32), ("qn", 1), ("kn", 1), ("eps", 1), ("eps_ln", 1), ("halfpi", 1), ("d5", 16), ("lre", 16),
                  ("lim", 16), ("ldt", 16), ("sinkp", 16), ("sinks", 2)):
    PRM[_name] = (_at, _n)
    _at += _n
PRM_COLS = _at
C_ID, C_ONE, C_BD, C_PS, C_PI, C_SS, C_SI, C_L1, C_U1, C_LV = 0, 1, 2, 3, 4, 5, 6, 7, 8, 9
CST_COLS = 14 * P + NB


def hybrid_step(nc, xT, w, prm, cst, shift, w2a2, g2, wglu, bc5, h05, s0, ckT, cv, cko, cvo,
                y, o_shift, o_srw, o_prw, o_s5p, o_s5s, o_kv, o_ck, o_cv):
    with ExitStack() as ctx:
        def sb(name, shape, dt=F32, c=ctx):
            return c.enter_context(nc.sbuf_tensor(name, shape, dt))

        PS = ctx.enter_context(nc.psum_tensor("PS", [P, 8, 512], F32))

        X = sb("X", [P, KT, T])
        WR = sb("WR", [P, 2, SLOT])
        WH = sb("WH", [P, 2, SLOT], F32R)
        WL = sb("WL", [P, 2, SLOT], F32R)
        PR = sb("PR", [P, PRM_COLS])
        CS = sb("CS", [P, CST_COLS])
        SC = sb("SC", [P, 4, T])
        ZL = sb("ZL", [P, A_TILES, 1 + NB])
        HP = sb("HP", [P, 8])
        SK = sb("SK", [P, 18])
        with ExitStack() as c1:
            HH = sb("HH", [P, FF_TILES, T], F32R, c1)
            HL = sb("HL", [P, FF_TILES, T], F32R, c1)
            XH = sb("XH", [P, KT, T], F32R, c1)
            XL = sb("XL", [P, KT, T], F32R, c1)
        with ExitStack() as c3:
            Z = sb("Z", [P, A_TILES, ZW], F32, c3)
            UF = sb("UF", [P, 4, L5, NC5], F32, c3)
            with ExitStack() as c4:
                UR = sb("UR", [P, 4, 4, 2 * NC5], F32, c4)
                TM = sb("TM", [P, 4, 576], F32, c4)
                PW = sb("PW", [P, 2, NPR5, L5 + 1], F32, c4)
                PV = sb("PV", [P, 2, NPR5, L5], F32, c4)
                BC = sb("BC", [P, 4, NPR5, 16], F32, c4)
                BB = sb("BB", [P, 2, NPR5, 16], F32, c4)
                S5 = sb("S5", [P, 16, NPR5], F32, c4)
                RHO = sb("RHO", [P, 4, NCP], F32, c4)
                HE = sb("HE", [P, 2, NPR5], F32, c4)
                HB = sb("HB", [P, 2, 3, NPR5, NB], F32, c4)
                M1T = sb("M1T", [P, 2, 4, L5, 32], F32, c4)
                M1 = sb("M1", [P, 2, 2, 4, P], F32, c4)
                CL = sb("CL", [P, 2, 4, L5 + 1, 32], F32, c4)
                TOE = sb("TOE", [P, 2, 4, P], F32, c4)
                ET = sb("ET", [P, 2, NPR5, NCP], F32, c4)
                XS = sb("XS", [P, 2, 4, NC5], F32, c4)
                HS = sb("HS", [P, 2, 4, NC5], F32, c4)
            tm_flat = TM[:, :, :].rearrange("p a c -> p (a c)")
            GQ, GT = [tm_flat[:, a * T:(a + 1) * T].rearrange("p (j c) -> p j c", j=4) for a in range(2)]
            HS4 = TM[:, 0:2, 4 * NCP:8 * NCP].rearrange("p a (j c) -> p a j c", j=4)
            with ExitStack() as c6:
                WG = sb("WG", [P, 4, 512], F32, c6)
                TG = sb("TG", [P, 4, T], F32, c6)
            with ExitStack() as c5:
                RKV = sb("RKV", [P, 3, T], F32, c5)
                TP = sb("TP", [P, 5, T], F32, c5)
                SG = sb("SG", [P, NCH + 1, P], F32, c5)
                GH = sb("GH", [P, 2, 8, P], F32, c5)
                AR = sb("AR", [P, 5, 2, P], F32, c5)
                BK = sb("BK", [P, 2, T], F32, c5)
                TOK = sb("TOK", [P, 2, 3, P], F32, c5)
                AW = sb("AW", [P, 2, 2, 2, 64], F32, c5)
                AU = sb("AU", [P, 2, 2, 2, 64], F32, c5)
                GM = sb("GM", [P, 2, 2, 4, P], F32, c5)
                TT = sb("TT", [P, 2, 2, 2, P], F32, c5)
                XM = sb("XM", [P, 2, 2, P], F32, c5)
                RT = sb("RT", [P, T], F32, c5)
                S0 = sb("S0", [P, NB, P], F32, c5)
                W2 = sb("W2", [P, 512], F32, c5)
                G2 = sb("G2", [P, 512], F32, c5)
                PEND = sb("PEND", [P, 16], F32, c5)
            TL, BO, O0 = SC[:, 0:2], SC[:, 2], SC[:, 3]
            TM3 = TP[:, :, :].rearrange("p a t -> p (a t)")[:, 0:3072].rearrange("p (a b t) -> p a b t", a=3, b=8)
        with ExitStack() as c7:
            Q = sb("Q", [P, 8, T], F32, c7)
            KR = sb("KR", [P, 2, T], F32, c7)
            VP = sb("VP", [P, 2, CH + T], F32, c7)
            KD = sb("KD", [P, 4, NP_TOK], F32, c7)
            KS = sb("KS", [P, 4, NB, KEYS], F32, c7)
            VW = sb("VW", [P, NCH, 256], F32, c7)
            VS = sb("VS", [P, NB, 256], F32, c7)
            EE = sb("EE", [P, 2, 4 * KEYS * 2], F32, c7)
            PT = sb("PT", [P, 8, P], F32, c7)
            SM = sb("SM", [P, 6, 16], F32, c7)

        qs_flat = SC[:, 2:4].rearrange("p a t -> p (a t)")[:, 0:1024]
        QS = qs_flat.rearrange("p (k b c) -> p k b c", k=4, b=NB)
        QSV = qs_flat.rearrange("p (k b a t) -> p k b a t", k=4, b=NB, a=2)

        def o_tiles(u, x):
            if u < 16:
                t, kv = u // 4, u % 4
                return PS[:, 3, 0:256].rearrange("p (a q) -> p a q", a=2), x[:, 2 * kv:2 * kv + 2, t * P:(t + 1) * P]
            a = NP_TOK + 64 * (u - 16)
            return PS[:, 3, :].rearrange("p (a q) -> p a q", a=8), x[:, :, a:a + 64]

        def prm_col(name, i=0):
            return PR[:, PRM[name][0] + i:PRM[name][0] + i + 1]

        def prm_cols(name):
            return PR[:, PRM[name][0]:PRM[name][0] + PRM[name][1]]

        def cstt(i):
            return CS[:, i * P:(i + 1) * P]

        IDN, ONES, BD = cstt(C_ID), cstt(C_ONE), cstt(C_BD)
        ROWM = CS[:, 14 * P:14 * P + NB]

        def prompt_cols(ap2d):
            return ap2d[:, 0:NP_TOK].rearrange("p (c t) -> p t c", t=L5)

        def sample_cols(ap2d, h):
            return ap2d[:, NP_TOK:T].rearrange("p (b h t) -> p h t b", h=2, t=L5)[:, h]

        def sem(name):
            return ctx.enter_context(nc.semaphore(name))

        params_in, x_in = sem("params_in"), sem("x_in")
        w_in = [sem("w_in0"), sem("w_in1")]
        w_split = sem("w_split")
        unit_done = sem("unit_done")
        unit_evac = sem("unit_evac")
        sq_ready, norm_sum, rms_ready = sem("sq_ready"), sem("norm_sum"), sem("rms_ready")
        xn_t, xn_hi, xn_lo = sem("xn_t"), sem("xn_hi"), sem("xn_lo")
        h_sq, h_hi, h_lo = sem("h_sq"), sem("h_hi"), sem("h_lo")
        dve_seq, act_seq = sem("dve_seq"), sem("act_seq")
        u_relayout, y_relayout, glu_w_in, s5_in = sem("u_relayout"), sem("y_relayout"), sem("glu_w_in"), sem("s5_in")
        s5_arg, s5_fn = sem("s5_arg"), sem("s5_fn")
        m1t_ready, m1_transposed, m1_ready = sem("m1t_ready"), sem("m1_transposed"), sem("m1_ready")
        cl_ready, toe_done, toe_ready = sem("cl_ready"), sem("toe_done"), sem("toe_ready")
        xs_done, xs_evac, hs_ready = sem("xs_done"), sem("xs_evac"), sem("hs_ready")
        y5_done, y5_sum, g_sq, g_arg, g_tanh, g_out = (sem("y5_done"), sem("y5_sum"), sem("g_sq"), sem("g_arg"),
                                                       sem("g_tanh"), sem("g_out"))
        glu_done, glu_tanh, glu_out = sem("glu_done"), sem("glu_tanh"), sem("glu_out")
        z_edge, zl_ready, lora_w_in, s0_in, st_stored = sem("z_edge"), sem("zl_ready"), sem("lora_w_in"), sem("s0_in"), sem("st_stored")
        mixed, lora_act, wa_done, wa_act = sem("mixed"), sem("lora_act"), sem("wa_done"), sem("wa_act")
        kk_sq, kk_sum, kk_norm = sem("kk_sq"), sem("kk_sum"), sem("kk_norm")
        cs_ready, decay_exp, feat_ready = sem("cs_ready"), sem("decay_exp"), sem("feat_ready")
        bonus_sum, bonus_ready = sem("bonus_sum"), sem("bonus_ready")
        tr_done, tok_ready, gram_done, gm_ready = sem("tr_done"), sem("tok_ready"), sem("gram_done"), sem("gm_ready")
        lv_done, aw_ready = sem("lak_v_done"), sem("aw_ready")
        lx_done, xm_ready, lt_done, tt_ready = sem("lx_done"), sem("xm_ready"), sem("lt_done"), sem("tt_ready")
        au_done, au_ready, ro_done, rt_ready, o0_ready = (sem("au_done"), sem("au_ready"), sem("ro_done"),
                                                          sem("rt_ready"), sem("o0_ready"))
        um_ready, gh_done, ghs_ready, gh_ready = sem("um_ready"), sem("gh_done"), sem("ghs_ready"), sem("gh_ready")
        st_done, st_ready = sem("st_done"), sem("st_ready")
        oo_done, o_ready, ln_sum, oc_ready, ln_sq, ln_sd, ab_out = (sem("oo_done"), sem("o_ready"), sem("ln_sum"),
                                                                   sem("oc_ready"), sem("ln_sq"), sem("ln_sd"),
                                                                   sem("ab_out"))
        qk_sq, qk_sum, qk_rms, qk_ready = sem("qk_sq"), sem("qk_sum"), sem("qk_rms"), sem("qk_ready")
        v_pad, kd_ready, cache_in, vw_tr, vw_ready = (sem("v_pad"), sem("kd_ready"), sem("cache_in"), sem("vw_tr"),
                                                      sem("vw_ready"))
        sc_done, sm_sub, sm_exp, sm_p = sem("sc_done"), sem("sm_sub"), sem("sm_exp"), sem("sm_p")
        pt_tr, pt_ready, pv_done, o_hi, o_lo = sem("pt_tr"), sem("pt_ready"), sem("pv_done"), sem("o_hi"), sem("o_lo")
        stored = sem("stored")

        block = ctx.enter_context(nc.Block())

        def sequencer(eng, s):
            n = [0]

            def o(ins):
                n[0] += 1
                ins.then_inc(s, 1)
                eng.wait_ge(s, n[0])
            return o

        stages, at = {}, 0
        for name, n in (("in", N_IN), ("out", N_OUT), ("up00", N_FF), ("dn00", N_FF), ("up01", N_FF), ("dn01", N_FF),
                        ("qkv", N_QKV), ("ao", N_OUT), ("up10", N_FF), ("dn10", N_FF), ("up11", N_FF), ("dn11", N_FF)):
            stages[name] = (at, n)
            at += n
        assert at == SLOTS

        def unit0(name):
            return 2 * stages[name][0]

        def end_unit(name):
            return 2 * sum(stages[name])

        NORM_UNIT = {1: lambda k: unit0("out") + k + 1, 2: lambda k: unit0("dn01") + 2 * k + 2,
                     3: lambda k: unit0("ao") + k + 1}
        ORDER = [4, 0, 1, 2, 3]

        def levels(t):
            return [2, 4, 8] if t == 4 else [2, 4, 8, 16, 32]

        LV_PAIR = sum(len(levels(t)) for t in ORDER)

        def lv(p, i):
            return p * LV_PAIR + sum(len(levels(t)) for t in ORDER[:i])

        @block.sync
        def _(sp):
            sp.dma_start(X[:, :, :], xT).then_inc(x_in, 16)
            sp.dma_start(PR[:, :], prm).then_inc(params_in, 16)
            sp.dma_start(CS[:, :], cst).then_inc(params_in, 16)
            for n in range(2):
                sp.dma_start(WR[:, n], w[n]).then_inc(w_in[n], 16)
            with sp.Fori(1, SLOTS // 2) as i:
                for r in range(2):
                    sp.wait_ge(w_split, 4 * i + (2 * r - 2))
                    sp.dma_start(WR[:, r], w[bass.ds(2 * i + r, 1)].rearrange("a p c -> p (a c)")).then_inc(w_in[r], 16)
            if SLOTS % 2:
                sp.wait_ge(w_split, 2 * (SLOTS - 2))
                sp.dma_start(WR[:, 0], w[SLOTS - 1]).then_inc(w_in[0], 16)

        @block.gpsimd
        def _(pool):
            def split(r, k, reused):
                pool.wait_ge(w_in[r], 16 * k + 16)
                if reused:
                    pool.wait_ge(unit_done, 4 * k + (2 * r - 2))
                nc.gpsimd.tensor_tensor(WH[:, r].rearrange("p (a c) -> p a c", c=P),
                                        WR[:, r].rearrange("p (a c) -> p a c", c=P),
                                        ONES.unsqueeze(1).broadcast_to((P, SLOT // P, P)), ALU.mult).then_inc(w_split, 1)
                pool.wait_ge(w_split, 4 * k + (2 * r + 1))
                nc.gpsimd.tensor_tensor(WL[:, r], WR[:, r], WH[:, r].bitcast(F32), ALU.subtract).then_inc(w_split, 1)

            pool.wait_ge(params_in, 32)
            split(0, 0, False)
            split(1, 0, False)
            with pool.Fori(1, SLOTS // 2) as i:
                for r in range(2):
                    split(r, i, True)
            if SLOTS % 2:
                split(0, SLOTS // 2, True)

        @block.tensor
        def _(pe):
            mm, tr = nc.tensor.matmul, nc.tensor.transpose

            def norm(L):
                for k in range(KT):
                    pe.wait_ge(sq_ready, L * KT + k + 1)
                    if L == 0 and k == 0:
                        pe.wait_ge(params_in, 32)
                    for h in range(2):
                        last = mm(PS[:, 4 + h, 0:HALF], ONES, SC[:, k % 2, h * HALF:(h + 1) * HALF],
                                  start=(k == 0), stop=(k == KT - 1))
                    last.then_inc(norm_sum, 1)

            def xn_wait(n):
                def wait(k):
                    pe.wait_ge(xn_hi, n * KT + k + 1)
                    pe.wait_ge(xn_lo, n * KT + k + 1)
                return wait

            def slot(name, i, u, xh, xl, kt, wait=None):
                s0 = stages[name][0]
                par = (s0 + u) % 2
                pe.wait_ge(w_split, 2 * i + 2 * (s0 + 1))
                wh = WH[:, par].rearrange("p (k c) -> p k c", k=kt)
                wl = WL[:, par].rearrange("p (k c) -> p k c", k=kt)
                for j in range(2):
                    if not isinstance(i, int) or 2 * (s0 + i) + j > 1:
                        pe.wait_ge(unit_evac, 2 * i + (2 * s0 + j - 1))
                    for h in (range(2) if kt == KT else [j]):
                        out = PS[:, 2 * j + (h if kt == KT else 0), 0:HALF]
                        cols = slice(h * HALF, (h + 1) * HALF)
                        wc = slice(j * P, (j + 1) * P) if kt == KT else slice(0, P)
                        for k in range(kt):
                            if wait and j == 0 and h == 0:
                                wait(k)
                            mm(out, wh[:, k, wc], xh[:, k, cols], start=(k == 0), stop=False)
                            mm(out, wh[:, k, wc], xl[:, k, cols], start=False, stop=False)
                            last = mm(out, wl[:, k, wc], xh[:, k, cols], start=False, stop=(k == kt - 1))
                    last.then_inc(unit_done, 1)

            def stage(name, xh, xl, kt, wait=None):
                if wait:
                    slot(name, 0, 0, xh, xl, kt, wait)
                    slot(name, 1, 1, xh, xl, kt)
                with pe.Fori(1 if wait else 0, stages[name][1] // 2) as i:
                    for u in range(2):
                        slot(name, 2 * i + u, u, xh, xl, kt)

            def s5(j5):
                pe.wait_ge(m1t_ready, j5 + 1)
                for i in range(4):
                    ri, t2 = i // 2, i % 2
                    if i < 2 and j5 > 0:
                        pe.wait_ge(xs_evac, 2 * j5)
                    if i >= 2:
                        pe.wait_ge(m1_ready, 4 * j5 + i - 1)
                    for j in range(4):
                        last = tr(PS[:, 4 + t2, j * P:(j + 1) * P],
                                  M1T[:, ri, j, 4 * t2:4 * t2 + 4, :].rearrange("p a b -> p (a b)"), IDN)
                    last.then_inc(m1_transposed, 1)
                pe.wait_ge(cl_ready, j5 + 1)
                if j5 > 0:
                    pe.wait_ge(y5_sum, j5)
                for j in range(4):
                    for ri in range(2):
                        mm(PS[:, 6, j * P:(j + 1) * P], M1T[:, ri, j, 4:8, :].rearrange("p a b -> p (a b)"),
                           CL[:, ri, j, 1:5, :].rearrange("p a b -> p (a b)"), start=(ri == 0), stop=(ri == 1))
                    for s in range(4):
                        for ri in range(2):
                            last = mm(PS[32 * s:32 * s + 32, 7, j * P + 32 * s:(j + 1) * P], M1T[:, ri, j, 7, :],
                                      CL[:, ri, j, 0:4 - s, :].rearrange("p a b -> p (a b)"),
                                      start=(ri == 0), stop=(ri == 1))
                last.then_inc(toe_done, 1)
                if j5 == 0:
                    pe.wait_ge(u_relayout, 16 * 16)
                pe.wait_ge(m1_ready, 4 * j5 + 4)
                for ri in range(2):
                    for j in range(4):
                        for t2 in range(2):
                            last = mm(PS[:, 4 + ri, j * NC5:(j + 1) * NC5], M1[:, ri, t2, j],
                                      UR[:, j, j5, t2 * NC5:(t2 + 1) * NC5], start=(t2 == 0), stop=(t2 == 1))
                    last.then_inc(xs_done, 1)
                pe.wait_ge(toe_ready, j5 + 1)
                pe.wait_ge(hs_ready, j5 + 1)
                for j in range(4):
                    at = (j % 2) * 2 * NC5
                    mm(PS[:, 6 + j // 2, at:at + 2 * NC5], TOE[:, 1, j], UR[:, j, j5, :], start=True, stop=False)
                    mm(PS[:, 6 + j // 2, at + NC5:at + 2 * NC5], TOE[:, 0, j], UR[:, j, j5, 0:NC5], start=False, stop=False)
                    for t2 in range(2):
                        for ri in range(2):
                            last = mm(PS[:, 6 + j // 2, at + t2 * NC5:at + (t2 + 1) * NC5],
                                      CL[:, ri, j, 1 + 4 * t2:5 + 4 * t2, :].rearrange("p a b -> p (a b)"),
                                      HS[:, ri, j, :], start=False, stop=(t2 == 1 and ri == 1))
                last.then_inc(y5_done, 1)

            def glu():
                pe.wait_ge(y_relayout, 16 * 16)
                pe.wait_ge(glu_w_in, 16)
                pe.wait_ge(unit_evac, 2 * N_IN)
                for j in range(4):
                    if j >= 2:
                        pe.wait_ge(glu_tanh, j - 1)
                    for h in range(2):
                        for k in range(4):
                            last = mm(PS[:, 2 * (j % 2) + h, 0:HALF], WG[:, k, j * P:(j + 1) * P],
                                      UF[:, k, 4 * h:4 * h + 4, :].rearrange("p t c -> p (t c)"),
                                      start=(k == 0), stop=(k == 3))
                    last.then_inc(glu_done, 1)

            def halves(bank, a, x):
                for h in range(2):
                    last = mm(PS[:, bank + h, 0:HALF], a, x[:, h * HALF:(h + 1) * HALF], start=True, stop=True)
                return last

            def rwkv(p):
                if p == 0:
                    pe.wait_ge(lora_act, 2)
                    pe.wait_ge(lora_w_in, 32)
                else:
                    pe.wait_ge(ab_out, p)
                halves(0, W2[0:64, p * P:(p + 1) * P], TL[0:64, 0]).then_inc(wa_done, 1)
                halves(2, W2[64:P, p * P:(p + 1) * P], TL[64:P, 0]).then_inc(wa_done, 1)
                pe.wait_ge(kk_sq, p + 1)
                halves(4, BD, TP[:, 4]).then_inc(kk_sum, 1)
                pe.wait_ge(feat_ready, p + 1)
                halves(6, BD, TP[:, 0]).then_inc(bonus_sum, 1)
                for i, t in enumerate(ORDER):
                    n = 5 * p + i
                    b = n % 2
                    cols = slice(t * P, (t + 1) * P)
                    if i == 0:
                        pe.wait_ge(wa_act, 2 * (p + 1))
                        pe.wait_ge(kk_norm, p + 1)
                    else:
                        pe.wait_ge(gh_ready, n)
                    tr(PS[:, 0, 0:P], BK[:, 0, cols], IDN)
                    tr(PS[:, 0, P:2 * P], BK[:, 1, cols], IDN)
                    tr(PS[:, 0, 2 * P:3 * P], RKV[:, 2, cols], IDN)
                    tr(PS[:, 0, 3 * P:4 * P], AR[:, t, 0], IDN).then_inc(tr_done, 1)
                    if i > 0:
                        pe.wait_ge(tt_ready, lv(p, i) + n)
                    for hh in range(2):
                        r = slice(64 * hh, 64 * hh + 64)
                        ar = AR[r, t].rearrange("p a t -> p (a t)")
                        mm(PS[:, 1 + hh, 0:2 * P], BK[r, 0, cols], ar, start=True, stop=True)
                        mm(PS[:, 1 + hh, 2 * P:4 * P], BK[r, 1, cols], ar, start=True, stop=True)
                    mm(PS[:, 3, 0:P], AR[0:64, t, 0], BK[0:64, 0, cols], start=True, stop=True)
                    mm(PS[:, 4, 0:P], AR[64:P, t, 0], BK[64:P, 0, cols], start=True, stop=True).then_inc(gram_done, 1)
                    pe.wait_ge(gm_ready, n + 1)
                    pe.wait_ge(tok_ready, n + 1)
                    if i > 0:
                        pe.wait_ge(au_ready, n)
                    for hh in range(2):
                        last = mm(PS[:, 5, hh * 64:hh * 64 + 64], GM[:, b, hh, 2], TOK[:, b, 2, 64 * hh:64 * hh + 64],
                                  start=True, stop=True)
                    last.then_inc(lv_done, 1)
                    for l, m in enumerate(levels(t)):
                        pe.wait_ge(tt_ready, lv(p, i) + n + l + 1)
                        for hh in range(2):
                            last = mm(PS[:, 3, hh * P:(hh + 1) * P], GM[:, b, hh, 0], TT[:, b, 0, hh], start=True, stop=True)
                        last.then_inc(lx_done, 1)
                        pe.wait_ge(xm_ready, lv(p, i) + l + 1)
                        for hh in range(2):
                            mm(PS[:, 4, hh * P:(hh + 1) * P], TT[:, b, 1, hh], XM[:, b, hh], start=True, stop=True)
                            last = mm(PS[:, 4, 256 + hh * P:256 + (hh + 1) * P], XM[:, b, hh], TT[:, b, 1, hh],
                                      start=True, stop=True)
                        last.then_inc(lt_done, 1)
                    pe.wait_ge(tt_ready, lv(p, i + 1) + n + 1)
                    pe.wait_ge(aw_ready, n + 1)
                    for hh in range(2):
                        last = mm(PS[:, 5, hh * P:(hh + 1) * P], TT[:, b, 1, hh], AW[:, b, hh].rearrange("p a k -> p (a k)"),
                                  start=True, stop=True)
                    last.then_inc(au_done, 1)
                    pe.wait_ge(au_ready, n + 1)
                    if i == 0:
                        pe.wait_ge(bonus_ready, p + 1)
                    else:
                        pe.wait_ge(rt_ready, n)
                        pe.wait_ge(o0_ready, n)
                    for hh in range(2):
                        r = slice(64 * hh, 64 * hh + 64)
                        mm(PS[r, 6, 0:P], AU[:, b, 0, hh], GM[:, b, hh, 1], start=True, stop=True)
                        mm(PS[r, 6, P:2 * P], AU[:, b, 1, hh], GM[:, b, hh, 1], start=True, stop=False)
                        last = mm(PS[r, 6, P:2 * P], TOK[:, b, 2, 64 * hh:64 * hh + 64], GM[:, b, hh, 3],
                                  start=False, stop=True)
                    last.then_inc(ro_done, 1)
                    At = AU[:, b, 0].rearrange("p h k -> p (h k)")
                    Ut = AU[:, b, 1].rearrange("p h k -> p (h k)")
                    if t == 4:
                        pe.wait_ge(um_ready, p + 1)
                        for h in range(2):
                            bm, um, vm = [TM3[:, a, 4 * h:4 * h + 4].rearrange("p b k -> p (b k)") for a in range(3)]
                            bank = (7, 0)[h]
                            mm(PS[:, bank, :], At, bm, start=True, stop=True).then_inc(gh_done, 1)
                            pe.wait_ge(ghs_ready, 4 * p + 2 * h + 1)
                            mm(PS[:, bank, :], TOK[:, b, 0], um, start=True, stop=False)
                            mm(PS[:, bank, :], TOK[:, b, 1], vm, start=False, stop=True).then_inc(gh_done, 1)
                        pe.wait_ge(ghs_ready, 4 * p + 4)
                        pe.wait_ge(s0_in, 16 * (p + 1))
                        for s in range(NB):
                            last = mm(PS[:, 1 + s // 4, (s % 4) * P:(s % 4 + 1) * P], GH[:, 0, s], S0[:, s],
                                      start=True, stop=True)
                        last.then_inc(st_done, 1)
                    else:
                        for c in range(2):
                            r = slice(64 * c, 64 * c + 64)
                            bank = (7, 0)[c]
                            mm(PS[:, bank, 0:P], At[r], TOK[r, b, 0], start=True, stop=True)
                            mm(PS[:, bank, P:2 * P], TOK[r, b, 0], Ut[r], start=True, stop=False)
                            mm(PS[:, bank, P:2 * P], TOK[r, b, 1], TOK[r, b, 2], start=False,
                               stop=True).then_inc(gh_done, 1)
                pe.wait_ge(gh_ready, 5 * p + 5)
                for c in range(NCH):
                    pe.wait_ge(st_ready, p * (NCH + 1) + 1 + c)
                    mm(PS[:, 1 + c % 2, 0:P], GH[:, 0, c], SG[:, c], start=True, stop=True).then_inc(st_done, 1)
                pe.wait_ge(rt_ready, 5 * p + 5)
                for c in range(NCH):
                    mm(PS[:, 3 + c // 5, (c % 5) * CH:(c % 5 + 1) * CH], SG[:, c], RT[:, c * CH:(c + 1) * CH],
                       start=True, stop=True)
                for s in range(NB):
                    a = NP_TOK + s * ST
                    last = mm(PS[:, 4, a - HALF:a - HALF + ST], S0[:, s], RT[:, a:a + ST], start=True, stop=True)
                last.then_inc(oo_done, 1)
                pe.wait_ge(o_ready, p + 1)
                halves(5, BD, TP[:, 0]).then_inc(ln_sum, 1)
                pe.wait_ge(ln_sq, p + 1)
                pe.wait_ge(st_ready, (p + 1) * (NCH + 1))
                halves(1, BD, TP[:, 2]).then_inc(ln_sum, 1)
                halves(3, G2[:, p * P:(p + 1) * P], TL[:, 1]).then_inc(ln_sum, 1)

            def attention():
                for j in range(10):
                    pe.wait_ge(qk_sq, j + 1)
                    if j >= 2:
                        pe.wait_ge(qk_rms, j - 1)
                    halves(4 + 2 * (j % 2), BD, SC[:, j % 2]).then_inc(qk_sum, 1)
                pe.wait_ge(v_pad, 1)
                pe.wait_ge(unit_evac, end_unit("qkv"))
                for n in range(NCH + NB):
                    if n >= 2:
                        pe.wait_ge(vw_ready, n - 1)
                    for i in range(2):
                        if n < NCH:
                            last = tr(PS[:, n % 2, i * P:(i + 1) * P], VP[:, i, n * CH:n * CH + P], IDN)
                        else:
                            a = CH + NP_TOK + (n - NCH) * ST
                            last = tr(PS[0:ST, n % 2, i * P:(i + 1) * P], VP[:, i, a:a + ST], IDN)
                    last.then_inc(vw_tr, 1)
                pe.wait_ge(kd_ready, 1)
                pe.wait_ge(cache_in, 32)
                pe.wait_ge(vw_ready, NCH + NB)
                u = 0
                for t in range(4):
                    for kv in range(4):
                        if u > 0:
                            pe.wait_ge(sm_sub, u)
                        for c in range(2):
                            n = 2 * t + c
                            for g in range(4):
                                half, t2 = g % 2, g // 2
                                r = slice(64 * half, 64 * half + 64)
                                q = Q[r, 2 * kv + t2, n * CH:(n + 1) * CH]
                                if n == 0:
                                    last = mm(PS[0:64, half, t2 * P + 64:t2 * P + P], q, KD[r, kv, 0:CH],
                                              start=True, stop=True)
                                else:
                                    last = mm(PS[64 * c:64 * c + 64, half, t2 * P:(t2 + 1) * P], q,
                                              KD[r, kv, (n - 1) * CH:(n + 1) * CH], start=True, stop=True)
                        last.then_inc(sc_done, 1)
                        pe.wait_ge(sm_p, u + 1)
                        if u > 0:
                            pe.wait_ge(pt_ready, u)
                        for g in range(4):
                            last = tr(PS[:, 2, g * P:(g + 1) * P], EE[:, u % 2, g * P:(g + 1) * P], IDN)
                        last.then_inc(pt_tr, 1)
                        pe.wait_ge(pt_ready, u + 1)
                        if u > 0:
                            pe.wait_ge(o_lo, u)
                        for c in range(2):
                            for half in range(2):
                                out = PS[64 * half:64 * half + 64, 3, 0:256].rearrange("p (a c q) -> p a c q", a=2, c=2)
                                last = mm(out[:, :, c], VW[:, 2 * t + c, kv * 64:kv * 64 + 64],
                                          PT[:, 2 * half:2 * half + 2, c * 64:c * 64 + 64], start=True, stop=True)
                        last.then_inc(pv_done, 1)
                        u += 1
                for bg in range(2):
                    pe.wait_ge(sm_sub, u)
                    for half in range(2):
                        r = slice(64 * half, 64 * half + 64)
                        for b4 in range(4):
                            for kv in range(4):
                                last = mm(PS[32 * kv:32 * kv + 32, half, b4 * KEYS:(b4 + 1) * KEYS],
                                          QS[r, kv, 4 * bg + b4], KS[r, kv, 4 * bg + b4], start=True, stop=True)
                    last.then_inc(sc_done, 1)
                    pe.wait_ge(sm_p, u + 1)
                    pe.wait_ge(pt_ready, u)
                    for g in range(8):
                        last = tr(PS[0:KEYS, (2, 4)[g // 4], (g % 4) * P:(g % 4 + 1) * P],
                                  EE[:, u % 2, g * KEYS:(g + 1) * KEYS], IDN)
                    last.then_inc(pt_tr, 1)
                    pe.wait_ge(pt_ready, u + 1)
                    pe.wait_ge(o_lo, u)
                    for b4 in range(4):
                        for half in range(2):
                            out = PS[64 * half:64 * half + 64, 3, :].rearrange("p (a b q) -> p a b q", a=8, b=4)
                            for kv in range(4):
                                last = mm(out[:, 2 * kv:2 * kv + 2, b4], VS[0:KEYS, 4 * bg + b4, kv * 64:kv * 64 + 64],
                                          PT[0:KEYS, half * 4 + b4, 32 * kv:32 * kv + 32], start=True, stop=True)
                    last.then_inc(pv_done, 1)
                    u += 1

            def mlp(l, n):
                stage(f"up{l}0", XH, XL, KT, xn_wait(n))
                for hf in range(2):
                    if hf:
                        stage(f"up{l}1", XH, XL, KT)
                    b = FF_TILES * (2 * l + hf)

                    def h_wait(k):
                        pe.wait_ge(h_hi, b + k + 1)
                        pe.wait_ge(h_lo, b + k + 1)
                    stage(f"dn{l}{hf}", HH, HL, FF_TILES, h_wait)

            norm(0)
            slot("in", 0, 0, XH, XL, KT, xn_wait(0))
            for i in range(1, N_IN):
                slot("in", i, i, XH, XL, KT)
            for j in range(4):
                s5(j)
            glu()
            for p in range(NPAIR):
                rwkv(p)
            stage("out", XH, XL, KT, xn_wait(1))
            norm(1)
            mlp(0, 2)
            norm(2)
            stage("qkv", XH, XL, KT, xn_wait(3))
            attention()

            def o_wait(k):
                if k == 0:
                    pe.wait_ge(o_lo, 18)
            stage("ao", XH, XL, KT, o_wait)
            norm(3)
            mlp(1, 4)

        @block.scalar
        def _(act):
            o = sequencer(act, act_seq)
            fn = nc.scalar.activation

            def halves(bank):
                return PS[:, bank:bank + 2, 0:HALF]

            def h2(ap):
                return ap.rearrange("p (h t) -> p h t", h=2)

            def norm(L, n):
                for k in range(KT):
                    if L == 0:
                        act.wait_ge(x_in, 16)
                    else:
                        act.wait_ge(unit_evac, NORM_UNIT[L](k))
                    if L * KT + k >= 2 and k >= 2:
                        act.wait_ge(norm_sum, L * KT + k - 1)
                    fn(SC[:, k % 2], X[:, k], ACT.Square).then_inc(sq_ready, 1)
                act.wait_ge(norm_sum, (L + 1) * KT)
                if L == 0:
                    act.wait_ge(params_in, 32)
                fn(h2(SC[:, 2]), halves(4), ACT.Sqrt, bias=prm_col("eps"), scale=1.0 / D).then_inc(rms_ready, 1)
                for k in range(KT):
                    act.wait_ge(xn_t, L * KT + k + 1)
                    fn(XH[:, k], SC[:, (3, 0)[k % 2]], ACT.Copy).then_inc(xn_hi, 1)

            def evac_in():
                for n in range(N_IN):
                    for j in range(2):
                        act.wait_ge(unit_done, 2 * n + j + 1)
                        tile = IN_TILES[2 * n + j]
                        ps = [PS[:, 2 * j, 0:HALF], PS[:, 2 * j + 1, 0:HALF]]
                        if tile < A_TILES:
                            fn(Z[:, tile, 1:1 + HALF], ps[0], ACT.Copy)
                            fn(Z[:, tile, 1 + HALF:1 + NP_TOK], ps[1][:, 0:NP_TOK - HALF], ACT.Copy)
                            zs = Z[:, tile, 1 + NP_TOK:ZW].rearrange("p (b t) -> p b t", b=NB)
                            last = fn(zs[:, :, 1:1 + ST], ps[1][:, NP_TOK - HALF:HALF].rearrange("p (b t) -> p b t", b=NB),
                                      ACT.Copy)
                        else:
                            uf = UF[:, tile - A_TILES]
                            c0 = HALF // L5
                            fn(uf[:, :, 0:c0], ps[0].rearrange("p (c t) -> p t c", t=L5), ACT.Copy)
                            fn(uf[:, :, c0:NCP], ps[1][:, 0:NP_TOK - HALF].rearrange("p (c t) -> p t c", t=L5), ACT.Copy)
                            us = ps[1][:, NP_TOK - HALF:HALF].rearrange("p (b h t) -> p h t b", h=2, t=L5)
                            for h in range(2):
                                last = fn(uf[:, :, NCP + h * NB:NCP + (h + 1) * NB], us[:, h], ACT.Copy)
                        last.then_inc(unit_evac, 1)
                    if n == 2:
                        act.wait_ge(unit_evac, 6)
                        for t4 in range(4):
                            for j in range(4):
                                src = UF[32 * j:32 * j + 32].rearrange("p a (b t) c -> p a b t c", t=4)[:, :, :, t4]
                                dst = UR[32 * t4:32 * t4 + 32, j].rearrange("p a (b c) -> p a b c", b=2)
                                act.dma_start(dst, src).then_inc(u_relayout, 16)

            def s5_scalars():
                act.wait_ge(params_in, 32)
                fn(S5[:, 0], prm_cols("ldt"), ACT.Exp).then_inc(s5_fn, 1)
                act.wait_ge(s5_arg, 1)
                fn(S5[:, 4], S5[:, 2], ACT.Exp)
                fn(S5[:, 10], S5[:, 2], ACT.Exp, scale=float(L5))
                fn(S5[:, 8], S5[:, 6], ACT.Sin)
                fn(S5[:, 9], S5[:, 7], ACT.Sin, bias=prm_col("halfpi"), scale=-1.0).then_inc(s5_fn, 1)

            def s5(j5):
                for i in range(4):
                    ri, t2 = i // 2, i % 2
                    act.wait_ge(m1_transposed, 4 * j5 + i + 1)
                    if j5 > 0:
                        act.wait_ge(xs_done, 2 * j5)
                    fn(M1[:, ri, t2].rearrange("p j c -> p (j c)"), PS[:, 4 + t2, :], ACT.Copy).then_inc(m1_ready, 1)
                act.wait_ge(toe_done, j5 + 1)
                if j5 == 0:
                    act.wait_ge(m1t_ready, 1)
                else:
                    act.wait_ge(y5_done, j5)
                fn(TOE[:, 0].rearrange("p j c -> p (j c)"), PS[:, 6, :], ACT.Copy)
                for s in range(4):
                    r = slice(32 * s, 32 * s + 32)
                    last = fn(TOE[r, 1, :, 32 * s:P], PS[r, 7, :].rearrange("p (j c) -> p j c", j=4)[:, :, 32 * s:P], ACT.Copy)
                last.then_inc(toe_ready, 1)
                for ri in range(2):
                    act.wait_ge(xs_done, 2 * j5 + ri + 1)
                    if j5 > 0:
                        act.wait_ge(hs_ready, j5)
                    fn(XS[:, ri].rearrange("p j c -> p (j c)"), PS[:, 4 + ri, 0:4 * NC5], ACT.Copy).then_inc(xs_evac, 1)
                act.wait_ge(y5_sum, j5 + 1)
                fn(GQ, UR[:, :, j5], ACT.Square).then_inc(g_sq, 1)
                act.wait_ge(g_arg, j5 + 1)
                fn(GT, GQ, ACT.Tanh, scale=GELU_C).then_inc(g_tanh, 1)

            def s5_finish():
                act.wait_ge(zl_ready, 1)
                act.dma_start(o_shift, ZL[:, :, :]).then_inc(stored, 16)
                act.wait_ge(g_out, 4)
                for t4 in range(4):
                    for j in range(4):
                        dst = UF[32 * j:32 * j + 32].rearrange("p a (b t) c -> p a b t c", t=4)[:, :, :, t4]
                        src = UR[32 * t4:32 * t4 + 32, j].rearrange("p a (b c) -> p a b c", b=2)
                        act.dma_start(dst, src).then_inc(y_relayout, 16)
                act.dma_start(o_s5p, HE[:, :, :]).then_inc(stored, 16)
                act.dma_start(o_s5s, HB[:, :, 2]).then_inc(stored, 16)
                act.wait_ge(y_relayout, 16 * 16)
                act.wait_ge(y5_done, 4)
                act.wait_ge(stored, 16 * 5)
                act.dma_start(WG[:, :, :], wglu).then_inc(glu_w_in, 16)
                for j in range(4):
                    act.wait_ge(glu_done, j + 1)
                    fn(h2(TG[:, j]), halves(2 * (j % 2)), ACT.Tanh, scale=0.25).then_inc(glu_tanh, 1)
                act.wait_ge(glu_out, 4)
                act.dma_start(W2[:, :], w2a2).then_inc(lora_w_in, 16)
                act.dma_start(G2[:, :], g2).then_inc(lora_w_in, 16)

            def rwkv(p):
                if p == 0:
                    act.wait_ge(mixed, 1)
                    fn(TL[0:64, 0], TL[0:64, 0], ACT.Tanh).then_inc(lora_act, 1)
                    o(fn(TL[:, 1], TL[:, 1], ACT.Tanh, scale=0.5))
                    fn(TL[:, 1], TL[:, 1], ACT.Copy, bias=0.5, scale=0.5).then_inc(lora_act, 1)
                if p > 0:
                    act.wait_ge(oo_done, p)
                act.dma_start(S0[:, :, :], s0[p]).then_inc(s0_in, 16)
                act.wait_ge(mixed, p + 2)
                fn(TP[:, 4], RKV[:, 1], ACT.Square, scale=prm_col("k_k", p)).then_inc(kk_sq, 1)
                act.wait_ge(wa_done, 2 * p + 1)
                fn(h2(TP[:, 0]), halves(0), ACT.Tanh, bias=HP[:, p:p + 1], scale=0.5).then_inc(wa_act, 1)
                act.wait_ge(wa_done, 2 * p + 2)
                fn(h2(TP[:, 3]), halves(2), ACT.Tanh, bias=HP[:, 4 + p:5 + p], scale=0.5).then_inc(wa_act, 1)
                act.wait_ge(kk_sum, p + 1)
                fn(h2(TP[:, 4]), halves(4), ACT.Sqrt).then_inc(kk_norm, 1)
                act.wait_ge(cs_ready, p + 1)
                fn(TP[:, 0], TP[:, 0], ACT.Exp)
                fn(TP[:, 2], TP[:, 1], ACT.Exp).then_inc(act_seq, 1)
                rwkv_seq[0] += 1
                act.wait_ge(act_seq, rwkv_seq[0])
                fn(TP[:, 1], TP[:, 1], ACT.Exp, scale=-1.0).then_inc(decay_exp, 1)
                for i, t in enumerate(ORDER):
                    n = 5 * p + i
                    b = n % 2
                    act.wait_ge(tr_done, n + 1)
                    if n >= 2:
                        act.wait_ge(ro_done, n - 1)
                        act.wait_ge(gh_ready, n - 1)
                    fn(AW[:, b, :, 0], PS[:, 0, 3 * P:4 * P].rearrange("p (h k) -> p h k", h=2), ACT.Copy)
                    fn(TOK[:, b].rearrange("p a c -> p (a c)"), PS[:, 0, 0:3 * P], ACT.Copy).then_inc(tok_ready, 1)
                    act.wait_ge(lv_done, n + 1)
                    fn(AW[:, b, :, 1], PS[:, 5, 0:P].rearrange("p (h k) -> p h k", h=2), ACT.Copy).then_inc(aw_ready, 1)
                    act.wait_ge(au_done, n + 1)
                    fn(AU[:, b].rearrange("p a h k -> p h a k"), PS[:, 5, 0:2 * P].rearrange("p (h a k) -> p h a k", h=2, a=2),
                       ACT.Copy).then_inc(au_ready, 1)
                    act.wait_ge(rt_ready, n + 1)
                    fn(O0[:, t * P:(t + 1) * P], PS[:, 6, P:2 * P], ACT.Copy).then_inc(o0_ready, 1)
                    if t == 4:
                        act.wait_ge(st_ready, p * (NCH + 1) + 1)
                        act.dma_start(o_srw[p], GH[:, 0]).then_inc(st_stored, 16)
                act.wait_ge(st_ready, (p + 1) * (NCH + 1))
                act.dma_start(o_prw[p], SG[:, NCH]).then_inc(st_stored, 16)
                act.wait_ge(oc_ready, p + 1)
                fn(TP[:, 2], TP[:, 1], ACT.Square).then_inc(ln_sq, 1)
                act.wait_ge(ln_sum, 3 * p + 2)
                fn(h2(TP[:, 3]), halves(1), ACT.Sqrt, bias=prm_col("eps_ln"), scale=1.0 / 64).then_inc(ln_sd, 1)

            def ab_high():
                for k in range(KT):
                    if k < 4:
                        act.wait_ge(ab_out, 4)
                        fn(XH[:, k], Z[:, k, 0:T], ACT.Copy).then_inc(xn_hi, 1)
                    else:
                        act.wait_ge(glu_out, 4)
                        fn(prompt_cols(XH[:, k]), UF[:, k - 4, :, 0:NCP], ACT.Copy, scale=0.25)
                        for h in range(2):
                            last = fn(sample_cols(XH[:, k], h), UF[:, k - 4, :, NCP + h * NB:NCP + (h + 1) * NB], ACT.Copy,
                                      scale=0.25)
                        last.then_inc(xn_hi, 1)

            def hidden(name, hidx):
                u0, b = unit0(name), FF_TILES * hidx
                if hidx % 2 == 1:
                    act.wait_ge(unit_done, u0)
                act.wait_ge(unit_evac, u0)
                with act.Fori(0, FF_TILES // 2) as i:
                    for j in range(2):
                        act.wait_ge(unit_done, 2 * i + (u0 + j + 1))
                        fn(h2(SC[:, j]), halves(2 * j), ACT.Relu).then_inc(unit_evac, 1)
                        act.wait_ge(h_sq, 2 * i + (b + j + 1))
                        fn(HH[:, bass.ds(2 * i + j, 1)].rearrange("p a t -> p (a t)"), SC[:, 2 + j], ACT.Copy).then_inc(h_hi, 1)

            def attention():
                u0 = unit0("qkv")
                act.wait_ge(unit_done, u0)
                act.dma_start(KS[:, :, :, 0:CH], ckT).then_inc(cache_in, 16)
                act.dma_start(VS[0:CH, :, :], cv).then_inc(cache_in, 16)
                act.wait_ge(unit_evac, u0)
                for j in range(12):
                    act.wait_ge(unit_done, u0 + j + 1)
                    dst = Q[:, j] if j < 8 else (KR[:, j - 8] if j < 10 else VP[:, j - 10, CH:CH + T])
                    fn(h2(dst), halves(2 * (j % 2)), ACT.Copy).then_inc(unit_evac, 1)
                for j in range(10):
                    src = Q[:, j] if j < 8 else KR[:, j - 8]
                    if j == 0:
                        act.wait_ge(unit_evac, u0 + 12)
                        act.wait_ge(xn_lo, 4 * KT)
                    if j >= 2:
                        act.wait_ge(qk_sum, j - 1)
                    fn(SC[:, j % 2], src, ACT.Square).then_inc(qk_sq, 1)
                    act.wait_ge(qk_sum, j + 1)
                    if j >= 2:
                        act.wait_ge(qk_ready, j - 1)
                    fn(h2(SC[:, 2 + j % 2]), halves(4 + 2 * (j % 2)), ACT.Sqrt, bias=prm_col("eps"),
                       scale=1.0 / 64).then_inc(qk_rms, 1)
                for n in range(NCH + NB):
                    act.wait_ge(vw_tr, n + 1)
                    if n < NCH:
                        fn(VW[:, n], PS[:, n % 2, 0:256], ACT.Copy).then_inc(vw_ready, 1)
                    else:
                        fn(VS[CH:KEYS, n - NCH], PS[0:ST, n % 2, 0:256], ACT.Copy).then_inc(vw_ready, 1)
                act.wait_ge(qk_ready, 10)
                act.dma_start(o_kv[:, 0], KR[:, :, T - 256:T]).then_inc(stored, 16)
                act.dma_start(o_kv[:, 1], VP[:, :, CH + T - 256:CH + T]).then_inc(stored, 16)
                for u in range(18):
                    w_, ng = (512, 4) if u < 16 else (8 * KEYS, 8)
                    act.wait_ge(sm_sub, u + 1)
                    fn(SM[:, 3, 0:ng], SM[:, 2, 0:ng], ACT.Exp, scale=0.125)
                    fn(EE[:, u % 2, 0:w_], EE[:, u % 2, 0:w_], ACT.Exp, scale=0.125).then_inc(sm_exp, 1)
                    act.wait_ge(pt_tr, u + 1)
                    if u > 0:
                        act.wait_ge(pv_done, u)
                    if u < 16:
                        fn(PT[:, 0:4].rearrange("p g q -> p (g q)"), PS[:, 2, :], ACT.Copy).then_inc(pt_ready, 1)
                    else:
                        fn(PT[0:KEYS, 0:4].rearrange("p g q -> p (g q)"), PS[0:KEYS, 2, :], ACT.Copy)
                        fn(PT[0:KEYS, 4:8].rearrange("p g q -> p (g q)"), PS[0:KEYS, 4, :], ACT.Copy).then_inc(pt_ready, 1)
                    act.wait_ge(pv_done, u + 1)
                    ps, dst = o_tiles(u, XH)
                    fn(dst, ps, ACT.Copy).then_inc(o_hi, 1)

            act.dma_start(BC[:, :, :, :], bc5).then_inc(s5_in, 16)
            act.dma_start(HB[:, :, 0], h05).then_inc(s5_in, 16)
            act.dma_start(ZL[:, :, :], shift).then_inc(z_edge, 16)
            act.dma_start(o_ck, cko).then_inc(stored, 16)
            act.dma_start(o_cv, cvo).then_inc(stored, 16)
            rwkv_seq = [1]
            norm(0, 0)
            evac_in()
            s5_scalars()
            for j in range(4):
                s5(j)
            s5_finish()
            for p in range(NPAIR):
                rwkv(p)
            act.wait_ge(st_stored, 32 * NPAIR)
            ab_high()
            norm(1, 2)
            hidden("up00", 0)
            hidden("up01", 1)
            norm(2, 3)
            attention()
            norm(3, 4)
            act.wait_ge(stored, 16 * 7)
            hidden("up10", 2)
            hidden("up11", 3)
            for k in range(KT):
                act.wait_ge(unit_evac, unit0("dn11") + 2 * k + 2)
                act.dma_start(y[:, k], X[:, k]).then_inc(stored, 16)
            act.wait_ge(stored, 16 * (KT + 2 + 2 + 2 + 1))

        @block.vector
        def _(dve):
            o = sequencer(dve, dve_seq)
            v = nc.vector
            tt, ts, stt = v.tensor_tensor, v.tensor_scalar, v.scalar_tensor_tensor
            M, A, S_ = ALU.mult, ALU.add, ALU.subtract

            def h2(ap):
                return ap.rearrange("p (h t) -> p h t", h=2)

            def halves(bank):
                return PS[:, bank:bank + 2, 0:HALF]

            def norm(L, n):
                dve.wait_ge(rms_ready, L + 1)
                o(v.reciprocal(SC[:, 2], SC[:, 2]))
                for k in range(KT):
                    tb = SC[:, (3, 0)[k % 2]]
                    if k == 0:
                        dve.wait_ge(norm_sum, (L + 1) * KT)
                    if k >= 2:
                        dve.wait_ge(xn_lo, n * KT + k - 1)
                    stt(tb, X[:, k], prm_col("g", 8 * L + k), SC[:, 2], M, M).then_inc(xn_t, 1)
                    dve.wait_ge(xn_hi, n * KT + k + 1)
                    tt(XL[:, k], tb, XH[:, k].bitcast(F32), S_).then_inc(xn_lo, 1)

            def cmul(outs, a, b, tmp):
                tt(tmp[0], a[0], b[0], M)
                tt(tmp[1], a[1], b[1], M)
                tt(tmp[2], a[0], b[1], M)
                o(tt(tmp[3], a[1], b[0], M))
                for r_out, i_out, pick in outs:
                    tt(r_out, pick(tmp[0]), pick(tmp[1]), S_)
                    o(tt(i_out, pick(tmp[2]), pick(tmp[3]), A))

            def tmps(shape):
                n = 1
                for x in shape:
                    n *= x
                out = []
                for a in range(4):
                    ap = TM[:, a, 0:n]
                    if len(shape) == 2:
                        ap = ap.rearrange("p (a b) -> p a b", a=shape[0])
                    if len(shape) == 3:
                        ap = ap.rearrange("p (a b c) -> p a b c", a=shape[0], b=shape[1])
                    out.append(ap)
                return out

            ident = lambda ap: ap

            def s5_scalars():
                s = [S5[:, i] for i in range(16)]
                dve.wait_ge(params_in, 32)
                dve.wait_ge(s5_in, 32)
                dve.wait_ge(s5_fn, 1)
                o(ts(s[1], prm_cols("lre"), -1e-4, None, ALU.min))
                o(tt(s[2], s[1], s[0], M))
                o(tt(s[3], prm_cols("lim"), s[0], M))
                o(ts(s[5], s[3], 1.0 / 6.283185307179586, ROUND, M, A))
                o(ts(s[5], s[5], -ROUND, None, A))
                o(stt(s[6], s[5], -TWO_PI_HI, s[3], M, A))
                o(stt(s[6], s[5], -TWO_PI_LO, s[6], M, A))
                o(ts(s[6], s[6], 3.1415925, -3.1415925, ALU.min, ALU.max))
                stt(s[7], s[6], -1.0, s[6], M, ALU.max).then_inc(s5_arg, 1)
                dve.wait_ge(s5_fn, 2)
                v.memset(PW[:, 0, :, 0:1], 1.0)
                o(v.memset(PW[:, 1, :, 0:1], 0.0))
                o(tt(PW[:, 0, :, 1], s[4], s[9], M))
                o(tt(PW[:, 1, :, 1], s[4], s[8], M))
                for k in (1, 2, 4):
                    a = [PW[:, ri, :, 1:k + 1] for ri in range(2)]
                    b = [PW[:, ri, :, k:k + 1].broadcast_to((P, NPR5, k)) for ri in range(2)]
                    cmul([(PW[:, 0, :, k + 1:2 * k + 1], PW[:, 1, :, k + 1:2 * k + 1], ident)], a, b, tmps((NPR5, k)))
                for ri in range(2):
                    for n in range(L5):
                        v.tensor_copy(PV[:, ri, :, n:n + 1], PW[:, ri, :, L5 - 1 - n:L5 - n])
                o(ts(s[11], PW[:, 0, :, 1], -1.0, None, A))
                ni, lr, li = PW[:, 1, :, 1], s[1], prm_cols("lim")
                tt(s[12], lr, lr, M)
                o(tt(s[13], li, li, M))
                o(tt(s[12], s[12], s[13], A))
                o(v.reciprocal(s[12], s[12]))
                tt(s[13], s[11], lr, M)
                o(tt(s[14], ni, li, M))
                o(tt(s[13], s[13], s[14], A))
                tt(s[14], ni, lr, M)
                o(tt(s[15], s[11], li, M))
                o(tt(s[14], s[14], s[15], S_))
                tt(s[13], s[13], s[12], M)
                o(tt(s[14], s[14], s[12], M))
                coef = [s[13].unsqueeze(2).broadcast_to((P, NPR5, 16)), s[14].unsqueeze(2).broadcast_to((P, NPR5, 16))]
                cmul([(BB[:, 0], BB[:, 1], ident)], coef, [BC[:, 0], BC[:, 1]], tmps((NPR5, 16)))
                dve.wait_ge(unit_done, 2 * N_IN)
                for _ in range(3):
                    cmul([(s[9], s[8], ident)], [s[9], s[8]], [s[9], s[8]], tmps((NPR5,)))
                v.memset(ET[:, 0, :, 0:1], 1.0)
                o(v.memset(ET[:, 1, :, 0:1], 0.0))
                k = 1
                while k < NCP:
                    b = [x.unsqueeze(2).broadcast_to((P, NPR5, k)) for x in (s[9], s[8])]
                    cmul([(ET[:, 0, :, k:2 * k], ET[:, 1, :, k:2 * k], ident)], [ET[:, ri, :, 0:k] for ri in range(2)], b,
                         tmps((NPR5, k)))
                    cmul([(s[9], s[8], ident)], [s[9], s[8]], [s[9], s[8]], tmps((NPR5,)))
                    k *= 2
                v.memset(M1T[:, :, :, :, :], 0.0)
                v.memset(CL[:, :, :, :, :], 0.0)
                v.memset(HS[:, :, :, 0:1], 0.0)
                o(v.memset(TOE[:, :, :, :], 0.0))

            def s5(j5):
                pr = slice(4 * j5, 4 * j5 + 4)

                def blocks(dst):
                    return [(dst[64 * g:64 * g + 64, 0, :, :, 16 * g:16 * g + 16],
                             dst[64 * g:64 * g + 64, 1, :, :, 16 * g:16 * g + 16],
                             lambda ap, g=g: ap[64 * g:64 * g + 64]) for g in range(2)]

                if j5 > 0:
                    dve.wait_ge(toe_done, j5)
                    dve.wait_ge(g_out, j5)
                shape = (P, 4, L5, 16)
                a = [PV[:, ri, pr].unsqueeze(3).broadcast_to(shape) for ri in range(2)]
                b = [BB[:, ri, pr].unsqueeze(2).broadcast_to(shape) for ri in range(2)]
                cmul(blocks(M1T), a, b, tmps((4, L5, 16)))
                v.tensor_copy(RHO[:, :, :], S5[:, 10, pr].unsqueeze(2).broadcast_to((P, 4, NCP))).then_inc(m1t_ready, 1)
                if j5 > 0:
                    dve.wait_ge(y5_done, j5)
                shape = (P, 4, L5 + 1, 16)
                a = [PW[:, ri, pr].unsqueeze(3).broadcast_to(shape) for ri in range(2)]
                b = [BC[:, 2 + ri, pr].unsqueeze(2).broadcast_to(shape) for ri in range(2)]
                t = tmps((4, L5 + 1, 16))
                tt(t[0], a[0], b[0], M)
                tt(t[1], a[1], b[1], M)
                tt(t[2], a[0], b[1], M)
                o(tt(t[3], a[1], b[0], M))
                o(tt(t[2], t[2], t[3], A))
                for g in range(2):
                    q = slice(64 * g, 64 * g + 64)
                    tt(CL[q, 0, :, :, 16 * g:16 * g + 16], t[0][q], t[1][q], S_)
                    last = ts(CL[q, 1, :, :, 16 * g:16 * g + 16], t[2][q], -1.0, None, M)
                last.then_inc(cl_ready, 1)
                v.memset(RHO[:, :, 0:1], 0.0)
                dve.wait_ge(xs_evac, 2 * j5 + 2)
                t = tmps((4, NCP))
                e = [ET[:, ri, pr] for ri in range(2)]
                x = [XS[:, ri, :, 0:NCP] for ri in range(2)]
                tt(t[0], x[0], e[0], M)
                tt(t[1], x[1], e[1], M)
                tt(t[2], x[1], e[0], M)
                o(tt(t[3], x[0], e[1], M))
                tt(t[0], t[0], t[1], A)
                o(tt(t[2], t[2], t[3], S_))
                rho = RHO[:, :, :].rearrange("p j c -> p (j c)")
                for a_ in (0, 2):
                    last = v.tensor_tensor_scan(TM[:, a_ + 1, 0:4 * NCP], rho, TM[:, a_, 0:4 * NCP], 0.0, M, A)
                o(last)
                tt(t[0], t[1], e[0], M)
                tt(t[2], t[3], e[1], M)
                o(tt(HS4[:, 0], t[1], e[1], M))
                o(tt(HS4[:, 1], t[3], e[0], M))
                tt(t[0], t[0], t[2], S_)
                o(tt(t[1], HS4[:, 0], HS4[:, 1], A))
                for ri in range(2):
                    v.tensor_copy(HS[:, ri, :, 1:NCP], t[ri][:, :, 0:NCP - 1])
                    v.tensor_copy(HE[:, ri, pr], t[ri][:, :, NCP - 1])
                p8 = [PW[:, ri, pr, L5:L5 + 1].broadcast_to((P, 4, NB)) for ri in range(2)]
                for h in range(2):
                    hin = [HB[:, ri, h, pr] for ri in range(2)]
                    for ri in range(2):
                        v.tensor_copy(HS[:, ri, :, NCP + h * NB:NCP + (h + 1) * NB], hin[ri])
                    t = [TM[:, a_, 256:256 + 4 * NB].rearrange("p (a b) -> p a b", a=4) for a_ in range(4)]
                    tt(t[0], p8[0], hin[0], M)
                    tt(t[1], p8[1], hin[1], M)
                    tt(t[2], p8[0], hin[1], M)
                    o(tt(t[3], p8[1], hin[0], M))
                    tt(t[0], t[0], t[1], S_)
                    o(tt(t[2], t[2], t[3], A))
                    c = slice(NCP + h * NB, NCP + (h + 1) * NB)
                    tt(HB[:, 0, h + 1, pr], t[0], XS[:, 0, :, c], A)
                    o(tt(HB[:, 1, h + 1, pr], t[2], XS[:, 1, :, c], A))
                v.engine_nop().then_inc(hs_ready, 1)
                dve.wait_ge(y5_done, j5 + 1)
                for j in range(4):
                    a_ = (j % 2) * 2 * NC5
                    last = stt(UR[:, j, j5], UR[:, j, j5], prm_col("d5", 4 * j5 + j), PS[:, 6 + j // 2, a_:a_ + 2 * NC5], M, A)
                last.then_inc(y5_sum, 1)
                yv = UR[:, :, j5]
                dve.wait_ge(g_sq, j5 + 1)
                o(ts(GQ, GQ, 0.044715, 1.0, M, A))
                tt(GQ, GQ, yv, M).then_inc(g_arg, 1)
                dve.wait_ge(g_tanh, j5 + 1)
                stt(yv, GT, 1.0, yv, A, M).then_inc(g_out, 1)

            def glu():
                for j in range(4):
                    dve.wait_ge(glu_done, 4)
                    dve.wait_ge(glu_tanh, j + 1)
                    yv = UF[:, j].rearrange("p t c -> p (t c)")
                    stt(yv, TG[:, j], 1.0, yv, A, M).then_inc(glu_out, 1)

            def mix(tile, dst):
                d = TP[:, 0]
                zp = Z[:, tile, 1 + NP_TOK:ZW].rearrange("p (b t) -> p b t", b=NB)
                ds_ = d[:, NP_TOK:T].rearrange("p (b t) -> p b t", b=NB)
                tt(d[:, 0:NP_TOK], Z[:, tile, 0:NP_TOK], Z[:, tile, 1:1 + NP_TOK], S_)
                o(tt(ds_, zp[:, :, 0:ST], zp[:, :, 1:1 + ST], S_))
                stt(dst[:, 0:NP_TOK], d[:, 0:NP_TOK], prm_col("mu", tile), Z[:, tile, 1:1 + NP_TOK], M, A)
                o(stt(dst[:, NP_TOK:T].rearrange("p (b t) -> p b t", b=NB), ds_, prm_col("mu", tile),
                      zp[:, :, 1:1 + ST], M, A))

            def rwkv(p):
                R, K, V = RKV[:, 0], RKV[:, 1], RKV[:, 2]
                T1, T2, T3, T4, T5 = [TP[:, a] for a in range(5)]
                if p == 0:
                    dve.wait_ge(glu_out, 4)
                    mix(12, TL[:, 0])
                    mix(13, TL[:, 1])
                    v.memset(SG[:, 0], 0.0).then_inc(mixed, 1)
                for a in range(3):
                    mix(4 * a + p, RKV[:, a])
                v.engine_nop().then_inc(mixed, 1)
                dve.wait_ge(wa_act, 2 * p + 1)
                o(ts(T1, T1, 1.0, -0.5 * EXPM05, A, M))
                for c in range(NCH + NB):
                    a = slice(c * CH, (c + 1) * CH) if c < NCH else slice(NP_TOK + (c - NCH) * ST, NP_TOK + (c - NCH + 1) * ST)
                    last = v.tensor_tensor_scan(T2[:, a], ONES[:, 0:a.stop - a.start], T1[:, a], 0.0, M, A)
                o(last)
                tt(T1, T2, T1, S_).then_inc(cs_ready, 1)
                dve.wait_ge(kk_norm, p + 1)
                o(ts(T5, T5, 1e-12, None, ALU.max))
                o(v.reciprocal(T5, T5))
                o(stt(T5, K, prm_col("k_k", p), T5, M, M))
                dve.wait_ge(wa_act, 2 * p + 2)
                o(ts(T4, T4, 0.5, 0.5, M, A))
                o(ts(BK[:, 0], T4, -1.0, prm_col("k_a", p), A, M))
                stt(K, BK[:, 0], 1.0, K, A, M)
                o(tt(T4, T5, T4, M))
                dve.wait_ge(decay_exp, p + 1)
                five = lambda ap: ap.rearrange("p (a t) -> p a t", a=5)
                stt(AR[:, :, 0], five(T5), -1.0, five(T1), M, M)
                tt(AR[:, :, 1], five(R), five(T3), M)
                tt(BK[:, 0], T4, T2, M)
                tt(BK[:, 1], K, T2, M)
                v.tensor_copy(PEND[:, 0:NCH], T3[:, CH - 1:NP_TOK:CH])
                o(v.tensor_copy(PEND[:, NCH:NCH + NB], T3[:, NP_TOK + ST - 1:T:ST]))
                stt(T1, R, prm_col("r_k", p), K, M, M).then_inc(feat_ready, 1)
                dve.wait_ge(bonus_sum, p + 1)
                tt(h2(BO), halves(6), h2(V), M).then_inc(bonus_ready, 1)
                for i, t in enumerate(ORDER):
                    n = 5 * p + i
                    b = n % 2
                    cst0 = C_SS if t == 4 else C_PS
                    dve.wait_ge(gram_done, n + 1)
                    mask = CS[:, cst0 * P:(cst0 + 2) * P].unsqueeze(1).broadcast_to((P, 2, 2 * P))
                    for hh in range(2):
                        last = tt(GM[:, b, hh].rearrange("p (a c) t -> p a (c t)", a=2),
                                  PS[:, 1 + hh, :].rearrange("p (a c) -> p a c", a=2), mask, M)
                    last.then_inc(gm_ready, 1)
                    dve.wait_ge(gm_ready, n + 1)
                    for hh in range(2):
                        tt(TT[:, b, 0, hh], PS[:, 3 + hh, 0:P], cstt(C_L1), M)
                    o(tt(TT[:, b, 1], GM[:, b, :, 0], cstt(C_U1).unsqueeze(1).broadcast_to((P, 2, P)), M))
                    tv = TT[:, b].rearrange("p a h t -> p (a h) t")
                    tt(tv, tv, IDN.unsqueeze(1).broadcast_to((P, 4, P)), A).then_inc(tt_ready, 1)
                    for l, m in enumerate(levels(t)):
                        dve.wait_ge(lx_done, lv(p, i) + l + 1)
                        tt(XM[:, b], PS[:, 3, 0:256].rearrange("p (h t) -> p h t", h=2),
                           cstt(C_LV + l).unsqueeze(1).broadcast_to((P, 2, P)), M).then_inc(xm_ready, 1)
                        dve.wait_ge(lt_done, lv(p, i) + l + 1)
                        tf = TT[:, b].rearrange("p a h t -> p (a h t)")
                        tt(tf, tf, PS[:, 4, :], A).then_inc(tt_ready, 1)
                    dve.wait_ge(ro_done, n + 1)
                    tt(RT[:, t * P:(t + 1) * P], PS[:, 6, 0:P], AR[:, t, 1], A).then_inc(rt_ready, 1)
                    if t == 4:
                        dve.wait_ge(tok_ready, n + 1)
                        dve.wait_ge(au_ready, n + 1)
                        rows = ROWM.unsqueeze(2).broadcast_to((P, NB, P))
                        for a, src in enumerate((TOK[:, b, 0], AU[:, b, 1].rearrange("p h k -> p (h k)"), TOK[:, b, 2])):
                            last = tt(TM3[:, a], src.unsqueeze(1).broadcast_to((P, NB, P)), rows, M)
                        last.then_inc(um_ready, 1)
                        if p > 0:
                            dve.wait_ge(st_done, 9 * p)
                        for h in range(2):
                            bank = (7, 0)[h]
                            q = slice(4 * h, 4 * h + 4)
                            ps = PS[:, bank, :].rearrange("p (b c) -> p b c", b=4)
                            dve.wait_ge(gh_done, 12 * p + 2 * h + 1)
                            o(tt(GH[:, 0, q], ps, BD.unsqueeze(1).broadcast_to((P, 4, P)), M))
                            tt(GH[:, 0, q], GH[:, 0, q], IDN.unsqueeze(1).broadcast_to((P, 4, P)), A).then_inc(ghs_ready, 1)
                            dve.wait_ge(gh_done, 12 * p + 2 * h + 2)
                            pe_ = PEND[:, NCH + 4 * h:NCH + 4 * h + 4].unsqueeze(2).broadcast_to((P, 4, P))
                            o(tt(GH[:, 1, q], ps, pe_, M))
                            tt(GH[:, 1, q], GH[:, 1, q], BD.unsqueeze(1).broadcast_to((P, 4, P)), M).then_inc(ghs_ready, 1)
                        dve.wait_ge(st_done, p * (NCH + 1) + 1)
                        for h in range(2):
                            q = slice(4 * h, 4 * h + 4)
                            pe_ = PEND[:, NCH + 4 * h:NCH + 4 * h + 4].unsqueeze(2).broadcast_to((P, 4, P))
                            o(tt(GH[:, 0, q], PS[:, 1 + h, :].rearrange("p (b c) -> p b c", b=4), pe_, M))
                        o(tt(GH[:, 0], GH[:, 0], GH[:, 1], A))
                        v.engine_nop().then_inc(st_ready, 1)
                        v.engine_nop().then_inc(gh_ready, 1)
                    else:
                        if i == 1:
                            dve.wait_ge(st_stored, 32 * p + 16)
                        for c in range(2):
                            bank, ch = (7, 0)[c], 2 * t + c
                            dve.wait_ge(gh_done, 12 * p + 4 + 2 * (i - 1) + c + 1)
                            o(tt(GH[:, 0, ch], PS[:, bank, 0:P], BD, M))
                            tt(GH[:, 0, ch], GH[:, 0, ch], IDN, A)
                            last = stt(GH[:, 1, ch], PS[:, bank, P:2 * P], PEND[:, ch:ch + 1], BD, M, M)
                        last.then_inc(gh_ready, 1)
                dve.wait_ge(gh_ready, 5 * p + 5)
                for c in range(NCH):
                    dve.wait_ge(st_done, p * (NCH + 1) + 2 + c)
                    stt(SG[:, c + 1], PS[:, 1 + c % 2, 0:P], PEND[:, c:c + 1], GH[:, 1, c], M, A).then_inc(st_ready, 1)
                dve.wait_ge(oo_done, p + 1)
                dve.wait_ge(o0_ready, 5 * p + 5)
                tt(h2(T1), halves(3), h2(O0), A).then_inc(o_ready, 1)
                dve.wait_ge(ln_sum, 3 * p + 1)
                stt(h2(T2), halves(5), -1.0 / 64, h2(T1), M, A).then_inc(oc_ready, 1)
                dve.wait_ge(ln_sd, p + 1)
                o(v.reciprocal(T4, T4))
                o(tt(T2, T2, T4, M))
                o(ts(T2, T2, prm_col("lnw", p), prm_col("lnb", p), M, A))
                o(tt(T2, T2, BO, A))
                dve.wait_ge(ln_sum, 3 * p + 3)
                tt(Z[:, p, 0:T].rearrange("p (h t) -> p h t", h=2), halves(3), h2(T2), M).then_inc(ab_out, 1)

            def ab_low():
                for k in range(KT):
                    dve.wait_ge(xn_hi, KT + k + 1)
                    if k < 4:
                        dve.wait_ge(ab_out, 4)
                        tt(XL[:, k], Z[:, k, 0:T], XH[:, k].bitcast(F32), S_).then_inc(xn_lo, 1)
                    else:
                        if k == 4:
                            dve.wait_ge(glu_out, 4)
                        hi = XH[:, k].bitcast(F32)
                        stt(prompt_cols(XL[:, k]), UF[:, k - 4, :, 0:NCP], 0.25, prompt_cols(hi), M, S_)
                        for h in range(2):
                            last = stt(sample_cols(XL[:, k], h), UF[:, k - 4, :, NCP + h * NB:NCP + (h + 1) * NB], 0.25,
                                       sample_cols(hi, h), M, S_)
                        last.then_inc(xn_lo, 1)

            def add_tiles(name):
                dve.wait_ge(unit_evac, unit0(name))
                for k in range(KT):
                    u = unit0(name) + k
                    dve.wait_ge(unit_done, u + 1)
                    xk = h2(X[:, k])
                    tt(xk, halves(2 * (k % 2)), xk, A).then_inc(unit_evac, 1)

            def add_halves(name):
                u0 = unit0(name)
                dve.wait_ge(unit_evac, u0)
                with dve.Fori(0, KT) as i:
                    for j in range(2):
                        dve.wait_ge(unit_done, 2 * i + (u0 + j + 1))
                        xk = X[:, bass.ds(i, 1), j * HALF:(j + 1) * HALF].rearrange("p a t -> p (a t)")
                        tt(xk, PS[:, 2 * j, 0:HALF], xk, A).then_inc(unit_evac, 1)

            def hidden(name, hidx):
                u0, b = unit0(name), FF_TILES * hidx
                with dve.Fori(0, FF_TILES // 2) as i:
                    for j in range(2):
                        dve.wait_ge(unit_evac, 2 * i + (u0 + j + 1))
                        tt(SC[:, 2 + j], SC[:, j], SC[:, j], M).then_inc(h_sq, 1)
                        dve.wait_ge(h_hi, 2 * i + (b + j + 1))
                        m = bass.ds(2 * i + j, 1)
                        tt(HL[:, m].rearrange("p a t -> p (a t)"), SC[:, 2 + j],
                           HH[:, m].rearrange("p a t -> p (a t)").bitcast(F32), S_).then_inc(h_lo, 1)

            def attention():
                dve.wait_ge(unit_done, unit0("qkv"))
                v.memset(VP[:, :, 0:CH], 0.0).then_inc(v_pad, 1)
                for j in range(10):
                    src = Q[:, j] if j < 8 else KR[:, j - 8]
                    dve.wait_ge(qk_rms, j + 1)
                    r = SC[:, 2 + j % 2]
                    o(v.reciprocal(r, r))
                    stt(src, src, prm_col("qn" if j < 8 else "kn"), r, M, M).then_inc(qk_ready, 1)
                dve.wait_ge(qk_ready, 10)
                for kv in range(4):
                    i, src = kv // 2, slice(64 * (kv % 2), 64 * (kv % 2) + 64)
                    for half in range(2):
                        r = slice(64 * half, 64 * half + 64)
                        v.tensor_copy(KD[r, kv], KR[src, i, 0:NP_TOK])
                        v.tensor_copy(KS[r, kv, :, CH:KEYS], KR[src, i, NP_TOK:T].rearrange("p (b t) -> p b t", b=NB))
                    last = v.tensor_copy(QSV[:, kv].rearrange("p b a t -> p a b t"),
                                         Q[:, 2 * kv:2 * kv + 2, NP_TOK:T].rearrange("p a (b t) -> p a b t", b=NB))
                last.then_inc(kd_ready, 1)
                for u in range(18):
                    t, kv = u // 4, u % 4
                    dve.wait_ge(sc_done, u + 1)
                    if u < 16:
                        g1, kk, ng = 2, P, 4
                        sink = SK[:, 4 * kv:4 * kv + 4].rearrange("p (a b) -> p a b", a=2)
                        if t == 0:
                            for half in range(2):
                                pv = PS[0:64, half, 0:256].rearrange("p (a k) -> p a k", a=2)
                                last = v.memset(pv[:, :, 0:64], -1e30)
                            o(last)
                    else:
                        g1, kk, ng = 4, KEYS, 8
                        sink = SK[:, 16:18].unsqueeze(2).broadcast_to((P, 2, 4))
                    ps = PS[:, 0:2, 0:g1 * kk].rearrange("p h (a k) -> p h a k", a=g1)
                    sm = [SM[:, a, 0:ng].rearrange("p (h a) -> p h a", h=2) for a in range(6)]
                    e = EE[:, u % 2, 0:ng * kk].rearrange("p (h a k) -> p h a k", h=2, a=g1)
                    o(v.tensor_reduce(sm[0], ps, AX.X, ALU.max))
                    o(tt(sm[1], sm[0], sink, ALU.max))
                    tt(sm[2], sink, sm[1], S_)
                    tt(e, ps, sm[1].unsqueeze(3).broadcast_to((P, 2, g1, kk)), S_).then_inc(sm_sub, 1)
                    dve.wait_ge(sm_exp, u + 1)
                    o(v.tensor_reduce(sm[4], e, AX.X, A))
                    o(tt(sm[4], sm[4], sm[3], A))
                    o(v.reciprocal(sm[5], sm[4]))
                    tt(e, e, sm[5].unsqueeze(3).broadcast_to((P, 2, g1, kk)), M).then_inc(sm_p, 1)
                    dve.wait_ge(o_hi, u + 1)
                    ps, dst = o_tiles(u, XL)
                    _, hi = o_tiles(u, XH)
                    tt(dst, ps, hi.bitcast(F32), S_).then_inc(o_lo, 1)

            dve.wait_ge(z_edge, 16)
            v.tensor_copy(Z[:, :, 0:1], ZL[:, :, 0:1])
            zt = Z[:, :, 1 + NP_TOK:ZW].rearrange("p a (b t) -> p a b t", b=NB)
            v.tensor_copy(zt[:, :, :, 0], ZL[:, :, 1:1 + NB])
            dve.wait_ge(params_in, 32)
            o(ts(HP[:, :], PR[:, PRM["w0"][0]:PRM["w0"][0] + 8], 0.5, None, M))
            o(ts(SK[:, :], PR[:, PRM["sinkp"][0]:PRM["sinkp"][0] + 18], 8.0, None, M))
            norm(0, 0)
            s5_scalars()
            for j in range(4):
                s5(j)
            dve.wait_ge(unit_evac, 2 * N_IN)
            v.tensor_copy(ZL[:, :, 0:1], Z[:, :, NP_TOK:NP_TOK + 1])
            o(v.tensor_copy(ZL[:, :, 1:1 + NB], Z[:, :, 1 + NP_TOK:ZW].rearrange("p a (b t) -> p a b t", b=NB)[:, :, :, ST]))
            v.engine_nop().then_inc(zl_ready, 1)
            glu()
            for p in range(NPAIR):
                rwkv(p)
            ab_low()
            add_tiles("out")
            norm(1, 2)
            for hf in range(2):
                hidden(f"up0{hf}", hf)
                add_halves(f"dn0{hf}")
            norm(2, 3)
            attention()
            add_tiles("ao")
            norm(3, 4)
            for hf in range(2):
                hidden(f"up1{hf}", 2 + hf)
                add_halves(f"dn1{hf}")


SHAPES = [(P, KT, T), (P, A_TILES, 1 + NB), (NPAIR, P, NB, P), (NPAIR, P, P), (P, 2, NPR5), (P, 2, NPR5, NB),
          (P, 2, 2, 256), (NB, 112 * 256), (NB, 112 * 256)]


def constants():
    import numpy as np
    r, c = np.arange(P)[:, None], np.arange(P)[None, :]
    tiles = [r == c, r >= 0 * c, r // 64 == c // 64]
    for ch in (CH, ST):
        same = r // ch == c // ch
        tiles += [same & (r < c), same & (r <= c)]
    pair = (r // 2 == c // 2)
    tiles += [pair & (r > c), pair & (r < c)]
    for m in (2, 4, 8, 16, 32):
        tiles.append((r // (2 * m) == c // (2 * m)) & (r % (2 * m) >= m) & (c % (2 * m) < m))
    tiles = [np.broadcast_to(x, (P, P)) for x in tiles]
    tiles.append(r // ST == np.arange(NB)[None, :])
    return np.concatenate(tiles, axis=1).astype(np.float32)


def cols(a):
    return a.reshape(-1, P).T


def kernel(**inputs):
    import numpy as np
    import concourse.bacc as bacc
    from concourse.bass_utils import run_bass_kernel_spmd

    x = {k: np.asarray(v) for k, v in inputs.items()}
    f = np.float32
    tok = np.concatenate([x["x_prompt"].reshape(NP_TOK, D), x["x_sample"].reshape(NB * ST, D)], axis=0)

    def up(wm):
        n = wm.shape[1] // 256
        return wm.reshape(KT, P, n, 256).transpose(2, 1, 0, 3).reshape(n, P, SLOT)

    def down(wm):
        n = wm.shape[1] // P
        return wm.reshape(FF_TILES, P, n, P).transpose(2, 1, 0, 3).reshape(n, P, SLOT)

    w_in = up(x["ab_w_in"][0])[[6, 7, 8, 0, 2, 4, 1, 3, 5]]
    slots = [w_in, up(x["ab_w_out"][0])]
    for l in range(2):
        if l:
            slots += [up(x["att_w_qkv"][0]), up(x["att_w_out"][0])]
        for h in range(2):
            slots += [up(x["ffn_w1"][l][:, h * 2048:(h + 1) * 2048]), down(x["ffn_w2"][l][h * 2048:(h + 1) * 2048])]
    w = np.concatenate(slots, axis=0)

    def pairs(a):
        return np.moveaxis(a.reshape((NPR5, P) + a.shape[2:]), 1, 0)

    def const(v):
        return np.full((P, 1), v, f)

    d5 = np.broadcast_to(x["s5_d"][0].reshape(NPR5, 1, 32), (NPR5, 4, 32)).reshape(NPR5, P).T
    sinks = x["att_sinks"][0].reshape(4, 2, 2)
    parts = [cols(x["ab_mu"][0])]
    parts += [cols(x[n][0]) for n in ("rwkv_w0", "rwkv_a0", "rwkv_k_k", "rwkv_k_a")]
    parts += [cols(x["rwkv_r_k"][0].reshape(-1)), cols(x["rwkv_lnx_w"][0]), cols(x["rwkv_lnx_b"][0])]
    parts += [cols(x[n][l]) for l in range(2) for n in ("norm_mix", "norm_ffn")]
    parts += [np.tile(x["att_q_norm"][0], 2)[:, None], np.tile(x["att_k_norm"][0], 2)[:, None]]
    parts += [const(1e-6), const(64e-5), const(np.pi / 2), d5, pairs(x["s5_lam_re"][0]), pairs(x["s5_lam_im"][0]),
              pairs(np.broadcast_to(x["s5_log_dt"][0][:, None], (32, 64)))]
    parts += [np.broadcast_to(sinks.transpose(0, 2, 1).reshape(1, 16), (P, 16)),
              np.broadcast_to(sinks[:, :, None, :], (4, 2, ST, 2)).reshape(P, 2)]
    prm = np.concatenate(parts, axis=1)
    bc5 = np.stack([pairs(x["s5_b_re"][0]), pairs(x["s5_b_im"][0]), pairs(x["s5_c_re"][0].transpose(0, 2, 1)),
                    pairs(x["s5_c_im"][0].transpose(0, 2, 1))], axis=1)
    h05 = np.stack([pairs(x[n][0].transpose(1, 2, 0)) for n in ("state_ssm_re", "state_ssm_im")], axis=1)
    s0 = np.zeros((NPAIR, 2, 64, NB, 2, 64), f)
    st = x["state_rwkv"][0].reshape(NB, NPAIR, 2, 64, 64)
    for hh in range(2):
        s0[:, hh, :, :, hh] = st[:, :, hh].transpose(1, 3, 0, 2)
    shift = np.zeros((P, A_TILES, 1 + NB), f)
    shift[:, :, 1:] = x["state_shift"][0].reshape(NB, A_TILES, P).transpose(2, 1, 0)
    ck, cv = x["cache_k"][0], x["cache_v"][0]
    ckT = np.tile(ck[:, 64:].transpose(3, 2, 0, 1), (2, 1, 1, 1))
    arrays = dict(
        xT=tok.T.reshape(KT, P, T).transpose(1, 0, 2), w=w, prm=prm, cst=constants(), shift=shift,
        w2a2=np.concatenate([x["rwkv_w2"][0], x["rwkv_a2"][0]], axis=0), g2=x["rwkv_g2"][0],
        wglu=x["s5_w_glu"][0].reshape(4, P, 512).transpose(1, 0, 2), bc5=bc5, h05=h05,
        s0=s0.reshape(NPAIR, P, NB, P), ckT=ckT, cv=cv[:, 64:].reshape(NB, 64, 256).transpose(1, 0, 2),
        cko=ck[:, ST:].reshape(NB, 112 * 256), cvo=cv[:, ST:].reshape(NB, 112 * 256))

    nc = bacc.Bacc("TRN2", target_bir_lowering=False, num_devices=1)
    ins = {f"in_{n}": np.ascontiguousarray(a) for n, a in arrays.items()}
    args = [nc.dram_tensor(n, a.shape, mybir.dt.from_np(a.dtype), kind="ExternalInput").ap() for n, a in ins.items()]
    args += [nc.dram_tensor(f"out_{i}", s, F32, kind="ExternalOutput").ap() for i, s in enumerate(SHAPES)]
    hybrid_step(nc, *args)
    r = run_bass_kernel_spmd(nc, [ins], core_ids=[0])
    y, shift_o, srw, prw, s5p, s5s, kv, cko, cvo = [r.results[0][f"out_{i}"] for i in range(len(SHAPES))]

    yt = y.transpose(1, 0, 2).reshape(D, T).T
    sh = shift_o.transpose(2, 1, 0).reshape(1 + NB, A_TILES * P)

    def heads(a):
        a = a.reshape(NPAIR, 2, 64, -1, 2, 64)
        d = np.stack([a[:, h, :, :, h] for h in range(2)], axis=1)
        return d.transpose(3, 0, 1, 4, 2).reshape(-1, 8, 64, 64)

    def ungroup(a):
        return np.moveaxis(a, 1, 0).reshape((32, 64) + a.shape[2:])

    def frames(i, lo, n):
        return kv[:, i, :, lo:lo + n].transpose(2, 1, 0).reshape(n, 4, 64)

    def cache(old, i):
        return np.concatenate([old.reshape(NB, 112, 4, 64), frames(i, 128, 128).reshape(NB, ST, 4, 64)], axis=1)[None]

    return (yt[:NP_TOK].reshape(1, NP_TOK, D), yt[NP_TOK:].reshape(NB, ST, D),
            heads(prw)[None], sh[None, 0:1], ungroup(s5p[:, 0])[None, None], ungroup(s5p[:, 1])[None, None],
            frames(0, 0, 128)[None, None], frames(1, 0, 128)[None, None],
            heads(srw)[None], sh[None, 1:], ungroup(s5s[:, 0]).transpose(2, 0, 1)[None],
            ungroup(s5s[:, 1]).transpose(2, 0, 1)[None], cache(cko, 0), cache(cvo, 1))
```

```python
from contextlib import ExitStack

import concourse.bass as bass
from concourse import mybir

F32 = mybir.dt.float32
F32R = mybir.dt.float32r
ALU = mybir.AluOpType
ACT = mybir.ActivationFunctionType
AX = mybir.AxisListType

P = 128
D = 1024
KT = D // P
NP_TOK, NB, ST = 512, 8, 16
T = NP_TOK + NB * ST
HALF = T // 2
NPAIR = 4
A_TILES = 14
ZW = 1 + NP_TOK + NB * (1 + ST)
CH = 64
NCH = NP_TOK // CH
L5 = 8
NC5 = T // L5
NCP = NP_TOK // L5
NPR5 = 16
SLOT = 2048
FF_TILES = 16
KEYS = 80
EXPM05 = 0.6065306597126334
GELU_C = 0.7978845608028654
TWO_PI_HI, TWO_PI_LO = 6.28125, 0.0019353071795864769
ROUND = 12582912.0

N_IN, N_OUT, N_FF, N_QKV = 9, 4, 8, 6
SLOTS = N_IN + N_OUT + 4 * N_FF + N_QKV + N_OUT + 4 * N_FF
IN_TILES = [12, 13, 14, 15, 16, 17, 0, 1, 4, 5, 8, 9, 2, 3, 6, 7, 10, 11]

PRM = {}
_at = 0
for _name, _n in (("mu", 14), ("w0", 4), ("a0", 4), ("k_k", 4), ("k_a", 4), ("r_k", 4), ("lnw", 4), ("lnb", 4),
                  ("g", 32), ("qn", 1), ("kn", 1), ("eps", 1), ("eps_ln", 1), ("halfpi", 1), ("d5", 16), ("lre", 16),
                  ("lim", 16), ("ldt", 16), ("sinkp", 16), ("sinks", 2)):
    PRM[_name] = (_at, _n)
    _at += _n
PRM_COLS = _at
C_ID, C_ONE, C_BD, C_PS, C_PI, C_SS, C_SI, C_L1, C_U1, C_LV = 0, 1, 2, 3, 4, 5, 6, 7, 8, 9
CST_COLS = 14 * P + NB


def hybrid_step(nc, xT, w, prm, cst, shift, w2a2, g2, wglu, bc5, h05, s0, ckT, cv, cko, cvo,
                y, o_shift, o_srw, o_prw, o_s5p, o_s5s, o_kv, o_ck, o_cv):
    with ExitStack() as ctx:
        def sb(name, shape, dt=F32, c=ctx):
            return c.enter_context(nc.sbuf_tensor(name, shape, dt))

        PS = ctx.enter_context(nc.psum_tensor("PS", [P, 8, 512], F32))

        X = sb("X", [P, KT, T])
        WR = sb("WR", [P, 2, SLOT])
        PR = sb("PR", [P, PRM_COLS])
        CS = sb("CS", [P, CST_COLS])
        SC = sb("SC", [P, 4, T])
        ZL = sb("ZL", [P, A_TILES, 1 + NB])
        HP = sb("HP", [P, 8])
        SK = sb("SK", [P, 18])
        with ExitStack() as c0:
            GM = sb("GM", [P, 5, 2, 4, P], F32, c0)
            TT = sb("TT", [P, 5, 2, 2, P], F32, c0)
            W2 = sb("W2", [P, 512], F32, c0)
        WH = sb("WH", [P, 2, SLOT], F32R)
        WL = sb("WL", [P, 2, SLOT], F32R)
        with ExitStack() as c1:
            HH = sb("HH", [P, FF_TILES, T], F32R, c1)
            HL = sb("HL", [P, FF_TILES, T], F32R, c1)
            XH = sb("XH", [P, KT, T], F32R, c1)
            XL = sb("XL", [P, KT, T], F32R, c1)
        with ExitStack() as c3:
            Z = sb("Z", [P, A_TILES, ZW], F32, c3)
            UF = sb("UF", [P, 4, L5, NC5], F32, c3)
            with ExitStack() as c4:
                UR = sb("UR", [P, 4, 4, 2 * NC5], F32, c4)
                TM = sb("TM", [P, 4, 576], F32, c4)
                PW = sb("PW", [P, 2, NPR5, L5 + 1], F32, c4)
                PV = sb("PV", [P, 2, NPR5, L5], F32, c4)
                BC = sb("BC", [P, 4, NPR5, 16], F32, c4)
                BB = sb("BB", [P, 2, NPR5, 16], F32, c4)
                S5 = sb("S5", [P, 16, NPR5], F32, c4)
                RHO = sb("RHO", [P, 4, NCP], F32, c4)
                HE = sb("HE", [P, 2, NPR5], F32, c4)
                HB = sb("HB", [P, 2, 3, NPR5, NB], F32, c4)
                M1T = sb("M1T", [P, 2, 4, L5, 32], F32, c4)
                M1 = sb("M1", [P, 2, 2, 4, P], F32, c4)
                CL = sb("CL", [P, 2, 4, L5 + 1, 32], F32, c4)
                TOE = sb("TOE", [P, 2, 4, P], F32, c4)
                ET = sb("ET", [P, 2, NPR5, NCP], F32, c4)
                XS = sb("XS", [P, 2, 4, NC5], F32, c4)
                HS = sb("HS", [P, 2, 4, NC5], F32, c4)
            tm_flat = TM[:, :, :].rearrange("p a c -> p (a c)")
            GQ, GT = [tm_flat[:, a * T:(a + 1) * T].rearrange("p (j c) -> p j c", j=4) for a in range(2)]
            HS4 = TM[:, 0:2, 4 * NCP:8 * NCP].rearrange("p a (j c) -> p a j c", j=4)
            with ExitStack() as c6:
                WG = sb("WG", [P, 4, 512], F32, c6)
                TG = sb("TG", [P, 4, T], F32, c6)
            with ExitStack() as c5:
                RKV = sb("RKV", [P, 3, T], F32, c5)
                TP = sb("TP", [P, 5, T], F32, c5)
                SG = sb("SG", [P, NCH + 1, P], F32, c5)
                GH = sb("GH", [P, 2, 8, P], F32, c5)
                AR = sb("AR", [P, 5, 2, 2, P], F32, c5)
                BETA = sb("BETA", [P, T], F32, c5)[:, :]
                TOK = sb("TOK", [P, 5, 3, P], F32, c5)
                AW = sb("AW", [P, 5, 2, 2, 64], F32, c5)
                AU = sb("AU", [P, 5, 2, 2, 64], F32, c5)
                XM = sb("XM", [P, 5, 2, P], F32, c5)
                S0 = sb("S0", [P, NB, P], F32, c5)
                G2 = sb("G2", [P, 512], F32, c5)
                PEND = sb("PEND", [P, 2, 16], F32, c5)
            TL, BO, O0 = SC[:, 0:2], [SC[:, 2], Z[:, 12, 0:T]], SC[:, 3]
            TM3 = TP[:, :, :].rearrange("p a t -> p (a t)")[:, 0:3072].rearrange("p (a b t) -> p a b t", a=3, b=8)

            def RT(p):
                return Z[:, 4 + p, 0:T]

            def KAPPA(p):
                return Z[:, 8 + p, 0:T]
        with ExitStack() as c7:
            Q = sb("Q", [P, 8, T], F32, c7)
            KR = sb("KR", [P, 2, T], F32, c7)
            VP = sb("VP", [P, 2, CH + T], F32, c7)
            KD = sb("KD", [P, 4, NP_TOK], F32, c7)
            KS = sb("KS", [P, 4, NB, KEYS], F32, c7)
            VW = sb("VW", [P, NCH, 256], F32, c7)
            VS = sb("VS", [P, NB, 256], F32, c7)
            EE = sb("EE", [P, 2, 4 * KEYS * 2], F32, c7)
            PT = sb("PT", [P, 8, P], F32, c7)
            SM = sb("SM", [P, 6, 16], F32, c7)

        qs_flat = SC[:, 2:4].rearrange("p a t -> p (a t)")[:, 0:1024]
        QS = qs_flat.rearrange("p (k b c) -> p k b c", k=4, b=NB)
        QSV = qs_flat.rearrange("p (k b a t) -> p k b a t", k=4, b=NB, a=2)

        def o_tiles(u, x):
            if u < 16:
                t, kv = u // 4, u % 4
                return PS[:, 3, 0:256].rearrange("p (a q) -> p a q", a=2), x[:, 2 * kv:2 * kv + 2, t * P:(t + 1) * P]
            a = NP_TOK + 64 * (u - 16)
            return PS[:, 3, :].rearrange("p (a q) -> p a q", a=8), x[:, :, a:a + 64]

        def prm_col(name, i=0):
            return PR[:, PRM[name][0] + i:PRM[name][0] + i + 1]

        def prm_cols(name):
            return PR[:, PRM[name][0]:PRM[name][0] + PRM[name][1]]

        def cstt(i):
            return CS[:, i * P:(i + 1) * P]

        IDN, ONES, BD = cstt(C_ID), cstt(C_ONE), cstt(C_BD)
        ROWM = CS[:, 14 * P:14 * P + NB]

        def prompt_cols(ap2d):
            return ap2d[:, 0:NP_TOK].rearrange("p (c t) -> p t c", t=L5)

        def sample_cols(ap2d, h):
            return ap2d[:, NP_TOK:T].rearrange("p (b h t) -> p h t b", h=2, t=L5)[:, h]

        def sem(name):
            return ctx.enter_context(nc.semaphore(name))

        params_in, x_in = sem("params_in"), sem("x_in")
        w_in = [sem("w_in0"), sem("w_in1")]
        w_split = sem("w_split")
        unit_done = sem("unit_done")
        unit_evac = sem("unit_evac")
        sq_ready, norm_sum, rms_ready = sem("sq_ready"), sem("norm_sum"), sem("rms_ready")
        xn_t, xn_hi, xn_lo = sem("xn_t"), sem("xn_hi"), sem("xn_lo")
        h_sq, h_hi, h_lo = sem("h_sq"), sem("h_hi"), sem("h_lo")
        dve_seq, act_seq = sem("dve_seq"), sem("act_seq")
        u_relayout, y_relayout, glu_w_in, s5_in = sem("u_relayout"), sem("y_relayout"), sem("glu_w_in"), sem("s5_in")
        s5_arg, s5_fn = sem("s5_arg"), sem("s5_fn")
        m1t_ready, m1_transposed, m1_ready = sem("m1t_ready"), sem("m1_transposed"), sem("m1_ready")
        cl_ready, toe_done, toe_ready = sem("cl_ready"), sem("toe_done"), sem("toe_ready")
        xs_done, xs_evac, hs_ready = sem("xs_done"), sem("xs_evac"), sem("hs_ready")
        y5_done, y5_sum, g_sq, g_arg, g_tanh, g_out = (sem("y5_done"), sem("y5_sum"), sem("g_sq"), sem("g_arg"),
                                                       sem("g_tanh"), sem("g_out"))
        glu_done, glu_tanh, glu_out = sem("glu_done"), sem("glu_tanh"), sem("glu_out")
        z_edge, zl_ready, lora_w_in, s0_in = sem("z_edge"), sem("zl_ready"), sem("lora_w_in"), sem("s0_in")
        srw_stored, prw_stored = sem("srw_stored"), sem("prw_stored")
        mixed, lora_act, wa_done, wa_act = sem("mixed"), sem("lora_act"), sem("wa_done"), sem("wa_act")
        kk_sq, kk_sum, kk_norm = sem("kk_sq"), sem("kk_sum"), sem("kk_norm")
        cs_ready, decay_exp, feat_ready = sem("cs_ready"), sem("decay_exp"), sem("feat_ready")
        bonus_sum, bonus_ready = sem("bonus_sum"), sem("bonus_ready")
        tr_done, tok_ready, gram_done, gm_ready = sem("tr_done"), sem("tok_ready"), sem("gram_done"), sem("gm_ready")
        lv_done, aw_ready = sem("lak_v_done"), sem("aw_ready")
        lx_done, xm_ready, lt_done = sem("lx_done"), sem("xm_ready"), sem("lt_done")
        tt_first, tt_ready = sem("tt_first"), sem("tt_ready")
        au_done, au_ready, ro_done, rt_ready, o0_ready = (sem("au_done"), sem("au_ready"), sem("ro_done"),
                                                          sem("rt_ready"), sem("o0_ready"))
        um_ready, gh_done, ghs_ready, gh_ready = sem("um_ready"), sem("gh_done"), sem("ghs_ready"), sem("gh_ready")
        st_done, st_ready = sem("st_done"), sem("st_ready")
        oo_done, o_ready, ln_sum, oc_ready, ln_sq, ln_sd, ab_out = (sem("oo_done"), sem("o_ready"), sem("ln_sum"),
                                                                   sem("oc_ready"), sem("ln_sq"), sem("ln_sd"),
                                                                   sem("ab_out"))
        qk_sq, qk_sum, qk_rms, qk_ready = sem("qk_sq"), sem("qk_sum"), sem("qk_rms"), sem("qk_ready")
        v_pad, kd_ready, cache_in, vw_tr, vw_ready = (sem("v_pad"), sem("kd_ready"), sem("cache_in"), sem("vw_tr"),
                                                      sem("vw_ready"))
        sc_done, sm_sub, sm_exp, sm_p = sem("sc_done"), sem("sm_sub"), sem("sm_exp"), sem("sm_p")
        pt_tr, pt_ready, pv_done, o_hi, o_lo = sem("pt_tr"), sem("pt_ready"), sem("pv_done"), sem("o_hi"), sem("o_lo")
        stored = sem("stored")

        block = ctx.enter_context(nc.Block())

        def sequencer(eng, s):
            n = [0]

            def o(ins):
                n[0] += 1
                ins.then_inc(s, 1)
                eng.wait_ge(s, n[0])
            return o

        stages, at = {}, 0
        for name, n in (("in", N_IN), ("out", N_OUT), ("up00", N_FF), ("dn00", N_FF), ("up01", N_FF), ("dn01", N_FF),
                        ("qkv", N_QKV), ("ao", N_OUT), ("up10", N_FF), ("dn10", N_FF), ("up11", N_FF), ("dn11", N_FF)):
            stages[name] = (at, n)
            at += n
        assert at == SLOTS

        def unit0(name):
            return 2 * stages[name][0]

        def end_unit(name):
            return 2 * sum(stages[name])

        NORM_UNIT = {1: lambda k: unit0("out") + k + 1, 2: lambda k: unit0("dn01") + 2 * k + 2,
                     3: lambda k: unit0("ao") + k + 1}
        ORDER = [4, 0, 1, 2, 3]

        def levels(t):
            return [2, 4, 8] if t == 4 else [2, 4, 8, 16, 32]

        LEVELS = [3, 5, 5, 5, 5]
        LV_PAIR = sum(LEVELS)
        GH_PAIR = 4 + 2 * 4

        def active(l):
            return [i for i in range(5) if LEVELS[i] > l]

        def lvn(p, l, i):
            return p * LV_PAIR + sum(len(active(m)) for m in range(l)) + active(l).index(i)

        @block.sync
        def _(sp):
            sp.dma_start(X[:, :, :], xT).then_inc(x_in, 16)
            sp.dma_start(PR[:, :], prm).then_inc(params_in, 16)
            sp.dma_start(CS[:, :], cst).then_inc(params_in, 16)
            for n in range(2):
                sp.dma_start(WR[:, n], w[n]).then_inc(w_in[n], 16)
            with sp.Fori(1, SLOTS // 2) as i:
                for r in range(2):
                    sp.wait_ge(w_split, 4 * i + (2 * r - 2))
                    sp.dma_start(WR[:, r], w[bass.ds(2 * i + r, 1)].rearrange("a p c -> p (a c)")).then_inc(w_in[r], 16)
            if SLOTS % 2:
                sp.wait_ge(w_split, 2 * (SLOTS - 2))
                sp.dma_start(WR[:, 0], w[SLOTS - 1]).then_inc(w_in[0], 16)

        @block.gpsimd
        def _(pool):
            def split(r, k, reused):
                pool.wait_ge(w_in[r], 16 * k + 16)
                if reused:
                    pool.wait_ge(unit_done, 4 * k + (2 * r - 2))
                nc.gpsimd.tensor_tensor(WH[:, r].rearrange("p (a c) -> p a c", c=P),
                                        WR[:, r].rearrange("p (a c) -> p a c", c=P),
                                        ONES.unsqueeze(1).broadcast_to((P, SLOT // P, P)), ALU.mult).then_inc(w_split, 1)
                pool.wait_ge(w_split, 4 * k + (2 * r + 1))
                nc.gpsimd.tensor_tensor(WL[:, r], WR[:, r], WH[:, r].bitcast(F32), ALU.subtract).then_inc(w_split, 1)

            pool.wait_ge(params_in, 32)
            split(0, 0, False)
            split(1, 0, False)
            with pool.Fori(1, N_IN // 2) as i:
                for r in range(2):
                    split(r, i, True)
            split(0, N_IN // 2, True)
            pool.wait_ge(gh_done, GH_PAIR * NPAIR)
            split(1, N_IN // 2, True)
            with pool.Fori(N_IN // 2 + 1, SLOTS // 2) as i:
                for r in range(2):
                    split(r, i, True)
            if SLOTS % 2:
                split(0, SLOTS // 2, True)

        @block.tensor
        def _(pe):
            mm, tr = nc.tensor.matmul, nc.tensor.transpose

            def norm(L):
                for k in range(KT):
                    pe.wait_ge(sq_ready, L * KT + k + 1)
                    if L == 0 and k == 0:
                        pe.wait_ge(params_in, 32)
                    for h in range(2):
                        last = mm(PS[:, 4 + h, 0:HALF], ONES, SC[:, k % 2, h * HALF:(h + 1) * HALF],
                                  start=(k == 0), stop=(k == KT - 1))
                    last.then_inc(norm_sum, 1)

            def xn_wait(n):
                def wait(k):
                    pe.wait_ge(xn_hi, n * KT + k + 1)
                    pe.wait_ge(xn_lo, n * KT + k + 1)
                return wait

            def slot(name, i, u, xh, xl, kt, wait=None):
                s0 = stages[name][0]
                par = (s0 + u) % 2
                pe.wait_ge(w_split, 2 * i + 2 * (s0 + 1))
                wh = WH[:, par].rearrange("p (k c) -> p k c", k=kt)
                wl = WL[:, par].rearrange("p (k c) -> p k c", k=kt)
                for j in range(2):
                    if not isinstance(i, int) or 2 * (s0 + i) + j > 1:
                        pe.wait_ge(unit_evac, 2 * i + (2 * s0 + j - 1))
                    for h in (range(2) if kt == KT else [j]):
                        out = PS[:, 2 * j + (h if kt == KT else 0), 0:HALF]
                        cols = slice(h * HALF, (h + 1) * HALF)
                        wc = slice(j * P, (j + 1) * P) if kt == KT else slice(0, P)
                        for k in range(kt):
                            if wait and j == 0 and h == 0:
                                wait(k)
                            mm(out, wh[:, k, wc], xh[:, k, cols], start=(k == 0), stop=False)
                            mm(out, wh[:, k, wc], xl[:, k, cols], start=False, stop=False)
                            last = mm(out, wl[:, k, wc], xh[:, k, cols], start=False, stop=(k == kt - 1))
                    last.then_inc(unit_done, 1)

            def stage(name, xh, xl, kt, wait=None):
                if wait:
                    slot(name, 0, 0, xh, xl, kt, wait)
                    slot(name, 1, 1, xh, xl, kt)
                with pe.Fori(1 if wait else 0, stages[name][1] // 2) as i:
                    for u in range(2):
                        slot(name, 2 * i + u, u, xh, xl, kt)

            def s5(j5):
                pe.wait_ge(m1t_ready, j5 + 1)
                for i in range(4):
                    ri, t2 = i // 2, i % 2
                    if i < 2 and j5 > 0:
                        pe.wait_ge(xs_evac, 2 * j5)
                    if i >= 2:
                        pe.wait_ge(m1_ready, 4 * j5 + i - 1)
                    for j in range(4):
                        last = tr(PS[:, 4 + t2, j * P:(j + 1) * P],
                                  M1T[:, ri, j, 4 * t2:4 * t2 + 4, :].rearrange("p a b -> p (a b)"), IDN)
                    last.then_inc(m1_transposed, 1)
                pe.wait_ge(cl_ready, j5 + 1)
                if j5 > 0:
                    pe.wait_ge(y5_sum, j5)
                for j in range(4):
                    for ri in range(2):
                        mm(PS[:, 6, j * P:(j + 1) * P], M1T[:, ri, j, 4:8, :].rearrange("p a b -> p (a b)"),
                           CL[:, ri, j, 1:5, :].rearrange("p a b -> p (a b)"), start=(ri == 0), stop=(ri == 1))
                    for s in range(4):
                        for ri in range(2):
                            last = mm(PS[32 * s:32 * s + 32, 7, j * P + 32 * s:(j + 1) * P], M1T[:, ri, j, 7, :],
                                      CL[:, ri, j, 0:4 - s, :].rearrange("p a b -> p (a b)"),
                                      start=(ri == 0), stop=(ri == 1))
                last.then_inc(toe_done, 1)
                if j5 == 0:
                    pe.wait_ge(u_relayout, 16 * 16)
                pe.wait_ge(m1_ready, 4 * j5 + 4)
                for ri in range(2):
                    for j in range(4):
                        for t2 in range(2):
                            last = mm(PS[:, 4 + ri, j * NC5:(j + 1) * NC5], M1[:, ri, t2, j],
                                      UR[:, j, j5, t2 * NC5:(t2 + 1) * NC5], start=(t2 == 0), stop=(t2 == 1))
                    last.then_inc(xs_done, 1)
                pe.wait_ge(toe_ready, j5 + 1)
                pe.wait_ge(hs_ready, j5 + 1)
                for j in range(4):
                    at = (j % 2) * 2 * NC5
                    mm(PS[:, 6 + j // 2, at:at + 2 * NC5], TOE[:, 1, j], UR[:, j, j5, :], start=True, stop=False)
                    mm(PS[:, 6 + j // 2, at + NC5:at + 2 * NC5], TOE[:, 0, j], UR[:, j, j5, 0:NC5], start=False, stop=False)
                    for t2 in range(2):
                        for ri in range(2):
                            last = mm(PS[:, 6 + j // 2, at + t2 * NC5:at + (t2 + 1) * NC5],
                                      CL[:, ri, j, 1 + 4 * t2:5 + 4 * t2, :].rearrange("p a b -> p (a b)"),
                                      HS[:, ri, j, :], start=False, stop=(t2 == 1 and ri == 1))
                last.then_inc(y5_done, 1)

            def glu():
                pe.wait_ge(y_relayout, 16 * 16)
                pe.wait_ge(glu_w_in, 16)
                pe.wait_ge(unit_evac, 2 * N_IN)
                for j in range(4):
                    if j >= 2:
                        pe.wait_ge(glu_tanh, j - 1)
                    for h in range(2):
                        for k in range(4):
                            last = mm(PS[:, 2 * (j % 2) + h, 0:HALF], WG[:, k, j * P:(j + 1) * P],
                                      UF[:, k, 4 * h:4 * h + 4, :].rearrange("p t c -> p (t c)"),
                                      start=(k == 0), stop=(k == 3))
                    last.then_inc(glu_done, 1)

            def halves(bank, a, x):
                for h in range(2):
                    last = mm(PS[:, bank + h, 0:HALF], a, x[:, h * HALF:(h + 1) * HALF], start=True, stop=True)
                return last

            def wa(p):
                if p == 0:
                    pe.wait_ge(lora_act, 2)
                    pe.wait_ge(lora_w_in, 32)
                else:
                    pe.wait_ge(gh_ready, 5 * p)
                halves(0, W2[0:64, p * P:(p + 1) * P], TL[0:64, 0]).then_inc(wa_done, 1)
                halves(2, W2[64:P, p * P:(p + 1) * P], TL[64:P, 0]).then_inc(wa_done, 1)

            def kk(p):
                pe.wait_ge(kk_sq, p + 1)
                pe.wait_ge(wa_act, 2 * p + 1)
                halves(0, BD, TP[:, 4]).then_inc(kk_sum, 1)

            def bonus(p):
                pe.wait_ge(feat_ready, p + 1)
                halves(2, BD, TP[:, 0]).then_inc(bonus_sum, 1)

            def chain(p, c):
                if c == 0:
                    pe.wait_ge(gh_ready, 5 * p + 5)
                    if p > 0:
                        pe.wait_ge(ab_out, p)
                pe.wait_ge(st_ready, p * (NCH + 1) + 1 + c)
                mm(PS[:, (5, 7)[c % 2], 0:P], GH[:, 0, c], SG[:, c], start=True, stop=True).then_inc(st_done, 1)

            def outputs(p):
                for c in range(NCH):
                    mm(PS[:, 5 + c // 5, (c % 5) * CH:(c % 5 + 1) * CH], SG[:, c], RT(p)[:, c * CH:(c + 1) * CH],
                       start=True, stop=True)
                for s in range(NB):
                    a = NP_TOK + s * ST
                    last = mm(PS[:, 6, a - HALF:a - HALF + ST], S0[:, s], RT(p)[:, a:a + ST], start=True, stop=True)
                last.then_inc(oo_done, 1)

            def tile_au(p, i):
                pe.wait_ge(tt_ready, lvn(p, LEVELS[i] - 1, i) + 1)
                for hh in range(2):
                    last = mm(PS[:, i, hh * P:(hh + 1) * P], TT[:, i, 1, hh], AW[:, i, hh].rearrange("p a k -> p (a k)"),
                              start=True, stop=True)
                last.then_inc(au_done, 1)

            def tile_ro(p, i):
                pe.wait_ge(au_ready, 5 * p + i + 1)
                for hh in range(2):
                    r = slice(64 * hh, 64 * hh + 64)
                    mm(PS[r, i, 0:P], AU[:, i, 0, hh], GM[:, i, hh, 1], start=True, stop=True)
                    mm(PS[r, i, P:2 * P], AU[:, i, 1, hh], GM[:, i, hh, 1], start=True, stop=False)
                    last = mm(PS[r, i, P:2 * P], TOK[:, i, 2, 64 * hh:64 * hh + 64], GM[:, i, hh, 3],
                              start=False, stop=True)
                last.then_inc(ro_done, 1)

            def level(p, l):
                for i in active(l):
                    pe.wait_ge(*((tt_first, 5 * p + i + 1) if l == 0 else (tt_ready, lvn(p, l - 1, i) + 1)))
                    for hh in range(2):
                        last = mm(PS[:, i, hh * P:(hh + 1) * P], GM[:, i, hh, 0], TT[:, i, 0, hh], start=True, stop=True)
                    last.then_inc(lx_done, 1)
                for i in active(l):
                    pe.wait_ge(xm_ready, lvn(p, l, i) + 1)
                    for hh in range(2):
                        if l + 1 < LEVELS[i]:
                            mm(PS[:, i, hh * P:(hh + 1) * P], TT[:, i, 1, hh], XM[:, i, hh], start=True, stop=True)
                        last = mm(PS[:, i, 256 + hh * P:256 + (hh + 1) * P], XM[:, i, hh], TT[:, i, 1, hh],
                                  start=True, stop=True)
                    last.then_inc(lt_done, 1)

            def tiles(p):
                pe.wait_ge(bonus_ready, p + 1)
                pe.wait_ge(kk_norm, p + 1)
                for i, t in enumerate(ORDER):
                    cols = slice(t * P, (t + 1) * P)
                    tr(PS[:, i, 0:P], BETA[:, cols], IDN)
                    tr(PS[:, i, P:2 * P], KAPPA(p)[:, cols], IDN)
                    tr(PS[:, i, 2 * P:3 * P], RKV[:, 2, cols], IDN)
                    for hh in range(2):
                        last = mm(PS[:, i, 3 * P + 64 * hh:3 * P + 64 * hh + 64], AR[:, t, hh, 0],
                                  IDN[:, 64 * hh:64 * hh + 64], start=True, stop=True)
                    last.then_inc(tr_done, 1)
                if p > 0:
                    pe.wait_ge(o_ready, p)
                    halves(5, BD, TP[:, 0]).then_inc(ln_sum, 1)
                for hh in range(2):
                    for i, t in enumerate(ORDER):
                        cols = slice(t * P, (t + 1) * P)
                        if hh == 0:
                            pe.wait_ge(tok_ready, 5 * p + i + 1)
                        else:
                            pe.wait_ge(gm_ready, 10 * p + i + 1)
                        ar = AR[:, t, hh].rearrange("p a t -> p (a t)")
                        mm(PS[:, i, 0:2 * P], BETA[:, cols], ar, start=True, stop=True)
                        mm(PS[:, i, 2 * P:4 * P], KAPPA(p)[:, cols], ar, start=True, stop=True).then_inc(gram_done, 1)
                if p > 0:
                    pe.wait_ge(ln_sq, p)
                    halves(5, BD, TP[:, 2]).then_inc(ln_sum, 1)
                for i, t in enumerate(ORDER):
                    cols = slice(t * P, (t + 1) * P)
                    pe.wait_ge(gm_ready, 10 * p + 5 + i + 1)
                    for hh in range(2):
                        mm(PS[:, i, hh * P:(hh + 1) * P], AR[:, t, hh, 0], BETA[:, cols], start=True, stop=True)
                        last = mm(PS[:, i, 256 + hh * 64:256 + hh * 64 + 64], GM[:, i, hh, 2],
                                  TOK[:, i, 2, 64 * hh:64 * hh + 64], start=True, stop=True)
                    last.then_inc(lv_done, 1)
                if p > 0:
                    pe.wait_ge(ln_sd, p)
                    halves(5, G2[:, (p - 1) * P:p * P], TL[:, 1]).then_inc(ln_sum, 1)
                level(p, 0)
                level(p, 1)
                level(p, 2)
                tile_au(p, 0)
                level(p, 3)
                tile_ro(p, 0)
                level(p, 4)
                pe.wait_ge(um_ready, p + 1)
                At = [AU[:, i, 0].rearrange("p h k -> p (h k)") for i in range(5)]
                Ut = [AU[:, i, 1].rearrange("p h k -> p (h k)") for i in range(5)]
                masked = [[TM3[:, a, 4 * h:4 * h + 4].rearrange("p b k -> p (b k)") for a in range(3)] for h in range(2)]
                mm(PS[:, 7, :], At[0], masked[0][0], start=True, stop=True).then_inc(gh_done, 1)
                pe.wait_ge(rt_ready, 5 * p + 1)
                pe.wait_ge(o0_ready, 5 * p + 1)
                mm(PS[:, 0, :], At[0], masked[1][0], start=True, stop=True).then_inc(gh_done, 1)
                for i in range(1, 5):
                    tile_au(p, i)
                for h in range(2):
                    pe.wait_ge(ghs_ready, 4 * p + h + 1)
                    mm(PS[:, (7, 0)[h], :], TOK[:, 0, 0], masked[h][1], start=True, stop=False)
                    mm(PS[:, (7, 0)[h], :], TOK[:, 0, 1], masked[h][2], start=False, stop=True).then_inc(gh_done, 1)
                for i in range(1, 5):
                    tile_ro(p, i)
                pe.wait_ge(s0_in, 16 * (p + 1))
                for s in range(NB):
                    if s % 4 == 0:
                        pe.wait_ge(ghs_ready, 4 * p + 2 + s // 4 + 1)
                    last = mm(PS[:, (7, 0)[s // 4], (s % 4) * P:(s % 4 + 1) * P], GH[:, 0, s], S0[:, s],
                              start=True, stop=True)
                last.then_inc(st_done, 1)
                for c in range(2):
                    r, at = slice(64 * c, 64 * c + 64), 256 * c
                    for i in range(1, 5):
                        if c == 0:
                            pe.wait_ge(rt_ready, 5 * p + i + 1)
                            pe.wait_ge(o0_ready, 5 * p + i + 1)
                        else:
                            pe.wait_ge(gh_done, GH_PAIR * p + 4 + i)
                        mm(PS[:, i, at:at + P], At[i][r], TOK[r, i, 0], start=True, stop=True)
                        mm(PS[:, i, at + P:at + 2 * P], TOK[r, i, 0], Ut[i][r], start=True, stop=False)
                        mm(PS[:, i, at + P:at + 2 * P], TOK[r, i, 1], TOK[r, i, 2], start=False,
                           stop=True).then_inc(gh_done, 1)

            def rwkv():
                wa(0)
                kk(0)
                bonus(0)
                for p in range(NPAIR):
                    tiles(p)
                    if p + 1 < NPAIR:
                        wa(p + 1)
                    for c in range(NCH):
                        chain(p, c)
                        if c == 3 and p + 1 < NPAIR:
                            kk(p + 1)
                    outputs(p)
                    if p + 1 < NPAIR:
                        bonus(p + 1)
                pe.wait_ge(o_ready, NPAIR)
                halves(5, BD, TP[:, 0]).then_inc(ln_sum, 1)
                pe.wait_ge(ln_sq, NPAIR)
                halves(5, BD, TP[:, 2]).then_inc(ln_sum, 1)
                pe.wait_ge(ln_sd, NPAIR)
                halves(5, G2[:, (NPAIR - 1) * P:NPAIR * P], TL[:, 1]).then_inc(ln_sum, 1)

            def attention():
                for j in range(10):
                    pe.wait_ge(qk_sq, j + 1)
                    if j >= 2:
                        pe.wait_ge(qk_rms, j - 1)
                    halves(4 + 2 * (j % 2), BD, SC[:, j % 2]).then_inc(qk_sum, 1)
                pe.wait_ge(v_pad, 1)
                pe.wait_ge(unit_evac, end_unit("qkv"))
                for n in range(NCH + NB):
                    if n >= 2:
                        pe.wait_ge(vw_ready, n - 1)
                    for i in range(2):
                        if n < NCH:
                            last = tr(PS[:, n % 2, i * P:(i + 1) * P], VP[:, i, n * CH:n * CH + P], IDN)
                        else:
                            a = CH + NP_TOK + (n - NCH) * ST
                            last = tr(PS[0:ST, n % 2, i * P:(i + 1) * P], VP[:, i, a:a + ST], IDN)
                    last.then_inc(vw_tr, 1)
                pe.wait_ge(kd_ready, 1)
                pe.wait_ge(cache_in, 32)
                pe.wait_ge(vw_ready, NCH + NB)
                u = 0
                for t in range(4):
                    for kv in range(4):
                        if u > 0:
                            pe.wait_ge(sm_sub, u)
                        for c in range(2):
                            n = 2 * t + c
                            for g in range(4):
                                half, t2 = g % 2, g // 2
                                r = slice(64 * half, 64 * half + 64)
                                q = Q[r, 2 * kv + t2, n * CH:(n + 1) * CH]
                                if n == 0:
                                    last = mm(PS[0:64, half, t2 * P + 64:t2 * P + P], q, KD[r, kv, 0:CH],
                                              start=True, stop=True)
                                else:
                                    last = mm(PS[64 * c:64 * c + 64, half, t2 * P:(t2 + 1) * P], q,
                                              KD[r, kv, (n - 1) * CH:(n + 1) * CH], start=True, stop=True)
                        last.then_inc(sc_done, 1)
                        pe.wait_ge(sm_p, u + 1)
                        if u > 0:
                            pe.wait_ge(pt_ready, u)
                        for g in range(4):
                            last = tr(PS[:, 2, g * P:(g + 1) * P], EE[:, u % 2, g * P:(g + 1) * P], IDN)
                        last.then_inc(pt_tr, 1)
                        pe.wait_ge(pt_ready, u + 1)
                        if u > 0:
                            pe.wait_ge(o_lo, u)
                        for c in range(2):
                            for half in range(2):
                                out = PS[64 * half:64 * half + 64, 3, 0:256].rearrange("p (a c q) -> p a c q", a=2, c=2)
                                last = mm(out[:, :, c], VW[:, 2 * t + c, kv * 64:kv * 64 + 64],
                                          PT[:, 2 * half:2 * half + 2, c * 64:c * 64 + 64], start=True, stop=True)
                        last.then_inc(pv_done, 1)
                        u += 1
                for bg in range(2):
                    pe.wait_ge(sm_sub, u)
                    for half in range(2):
                        r = slice(64 * half, 64 * half + 64)
                        for b4 in range(4):
                            for kv in range(4):
                                last = mm(PS[32 * kv:32 * kv + 32, half, b4 * KEYS:(b4 + 1) * KEYS],
                                          QS[r, kv, 4 * bg + b4], KS[r, kv, 4 * bg + b4], start=True, stop=True)
                    last.then_inc(sc_done, 1)
                    pe.wait_ge(sm_p, u + 1)
                    pe.wait_ge(pt_ready, u)
                    for g in range(8):
                        last = tr(PS[0:KEYS, (2, 4)[g // 4], (g % 4) * P:(g % 4 + 1) * P],
                                  EE[:, u % 2, g * KEYS:(g + 1) * KEYS], IDN)
                    last.then_inc(pt_tr, 1)
                    pe.wait_ge(pt_ready, u + 1)
                    pe.wait_ge(o_lo, u)
                    for b4 in range(4):
                        for half in range(2):
                            out = PS[64 * half:64 * half + 64, 3, :].rearrange("p (a b q) -> p a b q", a=8, b=4)
                            for kv in range(4):
                                last = mm(out[:, 2 * kv:2 * kv + 2, b4], VS[0:KEYS, 4 * bg + b4, kv * 64:kv * 64 + 64],
                                          PT[0:KEYS, half * 4 + b4, 32 * kv:32 * kv + 32], start=True, stop=True)
                    last.then_inc(pv_done, 1)
                    u += 1

            def mlp(l, n):
                stage(f"up{l}0", XH, XL, KT, xn_wait(n))
                for hf in range(2):
                    if hf:
                        stage(f"up{l}1", XH, XL, KT)
                    b = FF_TILES * (2 * l + hf)

                    def h_wait(k):
                        pe.wait_ge(h_hi, b + k + 1)
                        pe.wait_ge(h_lo, b + k + 1)
                    stage(f"dn{l}{hf}", HH, HL, FF_TILES, h_wait)

            norm(0)
            slot("in", 0, 0, XH, XL, KT, xn_wait(0))
            for i in range(1, N_IN):
                slot("in", i, i, XH, XL, KT)
            for j in range(4):
                s5(j)
            glu()
            rwkv()
            stage("out", XH, XL, KT, xn_wait(1))
            norm(1)
            mlp(0, 2)
            norm(2)
            stage("qkv", XH, XL, KT, xn_wait(3))
            attention()

            def o_wait(k):
                if k == 0:
                    pe.wait_ge(o_lo, 18)
            stage("ao", XH, XL, KT, o_wait)
            norm(3)
            mlp(1, 4)

        @block.scalar
        def _(act):
            o = sequencer(act, act_seq)
            fn = nc.scalar.activation

            def halves(bank):
                return PS[:, bank:bank + 2, 0:HALF]

            def h2(ap):
                return ap.rearrange("p (h t) -> p h t", h=2)

            def norm(L, n):
                for k in range(KT):
                    if L == 0:
                        act.wait_ge(x_in, 16)
                    else:
                        act.wait_ge(unit_evac, NORM_UNIT[L](k))
                    if L * KT + k >= 2 and k >= 2:
                        act.wait_ge(norm_sum, L * KT + k - 1)
                    fn(SC[:, k % 2], X[:, k], ACT.Square).then_inc(sq_ready, 1)
                act.wait_ge(norm_sum, (L + 1) * KT)
                if L == 0:
                    act.wait_ge(params_in, 32)
                fn(h2(SC[:, 2]), halves(4), ACT.Sqrt, bias=prm_col("eps"), scale=1.0 / D).then_inc(rms_ready, 1)
                for k in range(KT):
                    act.wait_ge(xn_t, L * KT + k + 1)
                    fn(XH[:, k], SC[:, (3, 0)[k % 2]], ACT.Copy).then_inc(xn_hi, 1)

            def evac_in():
                for n in range(N_IN):
                    for j in range(2):
                        act.wait_ge(unit_done, 2 * n + j + 1)
                        tile = IN_TILES[2 * n + j]
                        ps = [PS[:, 2 * j, 0:HALF], PS[:, 2 * j + 1, 0:HALF]]
                        if tile < A_TILES:
                            fn(Z[:, tile, 1:1 + HALF], ps[0], ACT.Copy)
                            fn(Z[:, tile, 1 + HALF:1 + NP_TOK], ps[1][:, 0:NP_TOK - HALF], ACT.Copy)
                            zs = Z[:, tile, 1 + NP_TOK:ZW].rearrange("p (b t) -> p b t", b=NB)
                            last = fn(zs[:, :, 1:1 + ST], ps[1][:, NP_TOK - HALF:HALF].rearrange("p (b t) -> p b t", b=NB),
                                      ACT.Copy)
                        else:
                            uf = UF[:, tile - A_TILES]
                            c0 = HALF // L5
                            fn(uf[:, :, 0:c0], ps[0].rearrange("p (c t) -> p t c", t=L5), ACT.Copy)
                            fn(uf[:, :, c0:NCP], ps[1][:, 0:NP_TOK - HALF].rearrange("p (c t) -> p t c", t=L5), ACT.Copy)
                            us = ps[1][:, NP_TOK - HALF:HALF].rearrange("p (b h t) -> p h t b", h=2, t=L5)
                            for h in range(2):
                                last = fn(uf[:, :, NCP + h * NB:NCP + (h + 1) * NB], us[:, h], ACT.Copy)
                        last.then_inc(unit_evac, 1)
                    if n == 2:
                        act.wait_ge(unit_evac, 6)
                        for t4 in range(4):
                            for j in range(4):
                                src = UF[32 * j:32 * j + 32].rearrange("p a (b t) c -> p a b t c", t=4)[:, :, :, t4]
                                dst = UR[32 * t4:32 * t4 + 32, j].rearrange("p a (b c) -> p a b c", b=2)
                                act.dma_start(dst, src).then_inc(u_relayout, 16)

            def s5_scalars():
                act.wait_ge(params_in, 32)
                fn(S5[:, 0], prm_cols("ldt"), ACT.Exp).then_inc(s5_fn, 1)
                act.wait_ge(s5_arg, 1)
                fn(S5[:, 4], S5[:, 2], ACT.Exp)
                fn(S5[:, 10], S5[:, 2], ACT.Exp, scale=float(L5))
                fn(S5[:, 8], S5[:, 6], ACT.Sin)
                fn(S5[:, 9], S5[:, 7], ACT.Sin, bias=prm_col("halfpi"), scale=-1.0).then_inc(s5_fn, 1)

            def s5(j5):
                for i in range(4):
                    ri, t2 = i // 2, i % 2
                    act.wait_ge(m1_transposed, 4 * j5 + i + 1)
                    if j5 > 0:
                        act.wait_ge(xs_done, 2 * j5)
                    fn(M1[:, ri, t2].rearrange("p j c -> p (j c)"), PS[:, 4 + t2, :], ACT.Copy).then_inc(m1_ready, 1)
                act.wait_ge(toe_done, j5 + 1)
                if j5 == 0:
                    act.wait_ge(m1t_ready, 1)
                else:
                    act.wait_ge(y5_done, j5)
                fn(TOE[:, 0].rearrange("p j c -> p (j c)"), PS[:, 6, :], ACT.Copy)
                for s in range(4):
                    r = slice(32 * s, 32 * s + 32)
                    last = fn(TOE[r, 1, :, 32 * s:P], PS[r, 7, :].rearrange("p (j c) -> p j c", j=4)[:, :, 32 * s:P], ACT.Copy)
                last.then_inc(toe_ready, 1)
                for ri in range(2):
                    act.wait_ge(xs_done, 2 * j5 + ri + 1)
                    if j5 > 0:
                        act.wait_ge(hs_ready, j5)
                    fn(XS[:, ri].rearrange("p j c -> p (j c)"), PS[:, 4 + ri, 0:4 * NC5], ACT.Copy).then_inc(xs_evac, 1)
                act.wait_ge(y5_sum, j5 + 1)
                fn(GQ, UR[:, :, j5], ACT.Square).then_inc(g_sq, 1)
                act.wait_ge(g_arg, j5 + 1)
                fn(GT, GQ, ACT.Tanh, scale=GELU_C).then_inc(g_tanh, 1)

            def s5_finish():
                act.wait_ge(zl_ready, 1)
                act.dma_start(o_shift, ZL[:, :, :]).then_inc(stored, 16)
                act.wait_ge(g_out, 4)
                for t4 in range(4):
                    for j in range(4):
                        dst = UF[32 * j:32 * j + 32].rearrange("p a (b t) c -> p a b t c", t=4)[:, :, :, t4]
                        src = UR[32 * t4:32 * t4 + 32, j].rearrange("p a (b c) -> p a b c", b=2)
                        act.dma_start(dst, src).then_inc(y_relayout, 16)
                act.dma_start(o_s5p, HE[:, :, :]).then_inc(stored, 16)
                act.dma_start(o_s5s, HB[:, :, 2]).then_inc(stored, 16)
                act.wait_ge(y_relayout, 16 * 16)
                act.wait_ge(y5_done, 4)
                act.wait_ge(stored, 16 * 5)
                act.dma_start(WG[:, :, :], wglu).then_inc(glu_w_in, 16)
                for j in range(4):
                    act.wait_ge(glu_done, j + 1)
                    fn(h2(TG[:, j]), halves(2 * (j % 2)), ACT.Tanh, scale=0.25).then_inc(glu_tanh, 1)
                act.wait_ge(glu_out, 4)
                act.dma_start(W2[:, :], w2a2).then_inc(lora_w_in, 16)
                act.dma_start(G2[:, :], g2).then_inc(lora_w_in, 16)

            def features(p):
                if p == 0:
                    act.wait_ge(mixed, 1)
                    fn(TL[0:64, 0], TL[0:64, 0], ACT.Tanh).then_inc(lora_act, 1)
                    o(fn(TL[:, 1], TL[:, 1], ACT.Tanh, scale=0.5))
                    fn(TL[:, 1], TL[:, 1], ACT.Copy, bias=0.5, scale=0.5).then_inc(lora_act, 1)
                act.wait_ge(mixed, 2 * p + 2)
                fn(TP[:, 4], RKV[:, 1], ACT.Square, scale=prm_col("k_k", p)).then_inc(kk_sq, 1)
                act.wait_ge(wa_done, 2 * p + 1)
                fn(h2(TP[:, 2]), halves(0), ACT.Tanh, bias=HP[:, p:p + 1], scale=0.5).then_inc(wa_act, 1)
                act.wait_ge(wa_done, 2 * p + 2)
                fn(h2(TP[:, 3]), halves(2), ACT.Tanh, bias=HP[:, 4 + p:5 + p], scale=0.5).then_inc(wa_act, 1)
                act.wait_ge(kk_sum, p + 1)
                fn(h2(TP[:, 4]), halves(0), ACT.Sqrt).then_inc(kk_norm, 1)
                act.wait_ge(cs_ready, p + 1)
                fn(TP[:, 0], TP[:, 0], ACT.Exp)
                o(fn(TP[:, 2], TP[:, 1], ACT.Exp))
                fn(TP[:, 1], TP[:, 1], ACT.Exp, scale=-1.0).then_inc(decay_exp, 1)

            def tile_au(p, i):
                act.wait_ge(au_done, 5 * p + i + 1)
                fn(AU[:, i].rearrange("p a h k -> p h a k"), PS[:, i, 0:2 * P].rearrange("p (h a k) -> p h a k", h=2, a=2),
                   ACT.Copy).then_inc(au_ready, 1)

            def tile_o0(p, i):
                t = ORDER[i]
                act.wait_ge(rt_ready, 5 * p + i + 1)
                fn(O0[:, t * P:(t + 1) * P], PS[:, i, P:2 * P], ACT.Copy).then_inc(o0_ready, 1)

            def finish_sq(p):
                act.wait_ge(oc_ready, p + 1)
                fn(TP[:, 2], TP[:, 1], ACT.Square).then_inc(ln_sq, 1)

            def finish_sd(p):
                act.wait_ge(ln_sum, 3 * p + 2)
                fn(h2(TP[:, 3]), halves(5), ACT.Sqrt, bias=prm_col("eps_ln"), scale=1.0 / 64).then_inc(ln_sd, 1)

            def tiles(p):
                if p > 0:
                    act.wait_ge(oo_done, p)
                act.dma_start(S0[:, :, :], s0[p]).then_inc(s0_in, 16)
                for i in range(5):
                    act.wait_ge(tr_done, 5 * p + i + 1)
                    fn(AW[:, i, :, 0], PS[:, i, 3 * P:4 * P].rearrange("p (h k) -> p h k", h=2), ACT.Copy)
                    fn(TOK[:, i].rearrange("p a c -> p (a c)"), PS[:, i, 0:3 * P], ACT.Copy).then_inc(tok_ready, 1)
                if p > 0:
                    finish_sq(p - 1)
                    finish_sd(p - 1)
                tile_au(p, 0)
                tile_o0(p, 0)
                for i in range(1, 5):
                    tile_au(p, i)
                for i in range(1, 5):
                    tile_o0(p, i)
                act.wait_ge(st_ready, p * (NCH + 1) + 1)
                act.dma_start(o_srw[p], TM3[:, 0]).then_inc(srw_stored, 16)

            def rwkv():
                features(0)
                for p in range(NPAIR):
                    tiles(p)
                    if p + 1 < NPAIR:
                        features(p + 1)
                    act.wait_ge(st_ready, (p + 1) * (NCH + 1))
                    act.dma_start(o_prw[p], SG[:, NCH]).then_inc(prw_stored, 16)
                finish_sq(NPAIR - 1)
                finish_sd(NPAIR - 1)

            def ab_high():
                for k in range(KT):
                    if k < 4:
                        act.wait_ge(ab_out, 4)
                        fn(XH[:, k], Z[:, k, 0:T], ACT.Copy).then_inc(xn_hi, 1)
                    else:
                        act.wait_ge(glu_out, 4)
                        fn(prompt_cols(XH[:, k]), UF[:, k - 4, :, 0:NCP], ACT.Copy, scale=0.25)
                        for h in range(2):
                            last = fn(sample_cols(XH[:, k], h), UF[:, k - 4, :, NCP + h * NB:NCP + (h + 1) * NB], ACT.Copy,
                                      scale=0.25)
                        last.then_inc(xn_hi, 1)

            def hidden(name, hidx):
                u0, b = unit0(name), FF_TILES * hidx
                if hidx % 2 == 1:
                    act.wait_ge(unit_done, u0)
                act.wait_ge(unit_evac, u0)
                with act.Fori(0, FF_TILES // 2) as i:
                    for j in range(2):
                        act.wait_ge(unit_done, 2 * i + (u0 + j + 1))
                        fn(h2(SC[:, j]), halves(2 * j), ACT.Relu).then_inc(unit_evac, 1)
                        act.wait_ge(h_sq, 2 * i + (b + j + 1))
                        fn(HH[:, bass.ds(2 * i + j, 1)].rearrange("p a t -> p (a t)"), SC[:, 2 + j], ACT.Copy).then_inc(h_hi, 1)

            def attention():
                u0 = unit0("qkv")
                act.wait_ge(unit_done, u0)
                act.dma_start(KS[:, :, :, 0:CH], ckT).then_inc(cache_in, 16)
                act.dma_start(VS[0:CH, :, :], cv).then_inc(cache_in, 16)
                act.wait_ge(unit_evac, u0)
                for j in range(12):
                    act.wait_ge(unit_done, u0 + j + 1)
                    dst = Q[:, j] if j < 8 else (KR[:, j - 8] if j < 10 else VP[:, j - 10, CH:CH + T])
                    fn(h2(dst), halves(2 * (j % 2)), ACT.Copy).then_inc(unit_evac, 1)
                for j in range(10):
                    src = Q[:, j] if j < 8 else KR[:, j - 8]
                    if j == 0:
                        act.wait_ge(unit_evac, u0 + 12)
                        act.wait_ge(xn_lo, 4 * KT)
                    if j >= 2:
                        act.wait_ge(qk_sum, j - 1)
                    fn(SC[:, j % 2], src, ACT.Square).then_inc(qk_sq, 1)
                    act.wait_ge(qk_sum, j + 1)
                    if j >= 2:
                        act.wait_ge(qk_ready, j - 1)
                    fn(h2(SC[:, 2 + j % 2]), halves(4 + 2 * (j % 2)), ACT.Sqrt, bias=prm_col("eps"),
                       scale=1.0 / 64).then_inc(qk_rms, 1)
                for n in range(NCH + NB):
                    act.wait_ge(vw_tr, n + 1)
                    if n < NCH:
                        fn(VW[:, n], PS[:, n % 2, 0:256], ACT.Copy).then_inc(vw_ready, 1)
                    else:
                        fn(VS[CH:KEYS, n - NCH], PS[0:ST, n % 2, 0:256], ACT.Copy).then_inc(vw_ready, 1)
                act.wait_ge(qk_ready, 10)
                act.dma_start(o_kv[:, 0], KR[:, :, T - 256:T]).then_inc(stored, 16)
                act.dma_start(o_kv[:, 1], VP[:, :, CH + T - 256:CH + T]).then_inc(stored, 16)
                for u in range(18):
                    w_, ng = (512, 4) if u < 16 else (8 * KEYS, 8)
                    act.wait_ge(sm_sub, u + 1)
                    fn(SM[:, 3, 0:ng], SM[:, 2, 0:ng], ACT.Exp, scale=0.125)
                    fn(EE[:, u % 2, 0:w_], EE[:, u % 2, 0:w_], ACT.Exp, scale=0.125).then_inc(sm_exp, 1)
                    act.wait_ge(pt_tr, u + 1)
                    if u > 0:
                        act.wait_ge(pv_done, u)
                    if u < 16:
                        fn(PT[:, 0:4].rearrange("p g q -> p (g q)"), PS[:, 2, :], ACT.Copy).then_inc(pt_ready, 1)
                    else:
                        fn(PT[0:KEYS, 0:4].rearrange("p g q -> p (g q)"), PS[0:KEYS, 2, :], ACT.Copy)
                        fn(PT[0:KEYS, 4:8].rearrange("p g q -> p (g q)"), PS[0:KEYS, 4, :], ACT.Copy).then_inc(pt_ready, 1)
                    act.wait_ge(pv_done, u + 1)
                    ps, dst = o_tiles(u, XH)
                    fn(dst, ps, ACT.Copy).then_inc(o_hi, 1)

            act.dma_start(BC[:, :, :, :], bc5).then_inc(s5_in, 16)
            act.dma_start(HB[:, :, 0], h05).then_inc(s5_in, 16)
            act.dma_start(ZL[:, :, :], shift).then_inc(z_edge, 16)
            act.dma_start(o_ck, cko).then_inc(stored, 16)
            act.dma_start(o_cv, cvo).then_inc(stored, 16)
            norm(0, 0)
            evac_in()
            s5_scalars()
            for j in range(4):
                s5(j)
            s5_finish()
            rwkv()
            act.wait_ge(srw_stored, 16 * NPAIR)
            act.wait_ge(prw_stored, 16 * NPAIR)
            ab_high()
            norm(1, 2)
            hidden("up00", 0)
            hidden("up01", 1)
            norm(2, 3)
            attention()
            norm(3, 4)
            act.wait_ge(stored, 16 * 7)
            hidden("up10", 2)
            hidden("up11", 3)
            for k in range(KT):
                act.wait_ge(unit_evac, unit0("dn11") + 2 * k + 2)
                act.dma_start(y[:, k], X[:, k]).then_inc(stored, 16)
            act.wait_ge(stored, 16 * (KT + 2 + 2 + 2 + 1))

        @block.vector
        def _(dve):
            o = sequencer(dve, dve_seq)
            v = nc.vector
            tt, ts, stt = v.tensor_tensor, v.tensor_scalar, v.scalar_tensor_tensor
            M, A, S_ = ALU.mult, ALU.add, ALU.subtract

            def h2(ap):
                return ap.rearrange("p (h t) -> p h t", h=2)

            def halves(bank):
                return PS[:, bank:bank + 2, 0:HALF]

            def norm(L, n):
                dve.wait_ge(rms_ready, L + 1)
                o(v.reciprocal(SC[:, 2], SC[:, 2]))
                for k in range(KT):
                    tb = SC[:, (3, 0)[k % 2]]
                    if k == 0:
                        dve.wait_ge(norm_sum, (L + 1) * KT)
                    if k >= 2:
                        dve.wait_ge(xn_lo, n * KT + k - 1)
                    stt(tb, X[:, k], prm_col("g", 8 * L + k), SC[:, 2], M, M).then_inc(xn_t, 1)
                    dve.wait_ge(xn_hi, n * KT + k + 1)
                    tt(XL[:, k], tb, XH[:, k].bitcast(F32), S_).then_inc(xn_lo, 1)

            def cmul(outs, a, b, tmp):
                tt(tmp[0], a[0], b[0], M)
                tt(tmp[1], a[1], b[1], M)
                tt(tmp[2], a[0], b[1], M)
                o(tt(tmp[3], a[1], b[0], M))
                for r_out, i_out, pick in outs:
                    tt(r_out, pick(tmp[0]), pick(tmp[1]), S_)
                    o(tt(i_out, pick(tmp[2]), pick(tmp[3]), A))

            def tmps(shape):
                n = 1
                for x in shape:
                    n *= x
                out = []
                for a in range(4):
                    ap = TM[:, a, 0:n]
                    if len(shape) == 2:
                        ap = ap.rearrange("p (a b) -> p a b", a=shape[0])
                    if len(shape) == 3:
                        ap = ap.rearrange("p (a b c) -> p a b c", a=shape[0], b=shape[1])
                    out.append(ap)
                return out

            ident = lambda ap: ap

            def s5_scalars():
                s = [S5[:, i] for i in range(16)]
                dve.wait_ge(params_in, 32)
                dve.wait_ge(s5_in, 32)
                dve.wait_ge(s5_fn, 1)
                o(ts(s[1], prm_cols("lre"), -1e-4, None, ALU.min))
                o(tt(s[2], s[1], s[0], M))
                o(tt(s[3], prm_cols("lim"), s[0], M))
                o(ts(s[5], s[3], 1.0 / 6.283185307179586, ROUND, M, A))
                o(ts(s[5], s[5], -ROUND, None, A))
                o(stt(s[6], s[5], -TWO_PI_HI, s[3], M, A))
                o(stt(s[6], s[5], -TWO_PI_LO, s[6], M, A))
                o(ts(s[6], s[6], 3.1415925, -3.1415925, ALU.min, ALU.max))
                stt(s[7], s[6], -1.0, s[6], M, ALU.max).then_inc(s5_arg, 1)
                dve.wait_ge(s5_fn, 2)
                v.memset(PW[:, 0, :, 0:1], 1.0)
                o(v.memset(PW[:, 1, :, 0:1], 0.0))
                o(tt(PW[:, 0, :, 1], s[4], s[9], M))
                o(tt(PW[:, 1, :, 1], s[4], s[8], M))
                for k in (1, 2, 4):
                    a = [PW[:, ri, :, 1:k + 1] for ri in range(2)]
                    b = [PW[:, ri, :, k:k + 1].broadcast_to((P, NPR5, k)) for ri in range(2)]
                    cmul([(PW[:, 0, :, k + 1:2 * k + 1], PW[:, 1, :, k + 1:2 * k + 1], ident)], a, b, tmps((NPR5, k)))
                for ri in range(2):
                    for n in range(L5):
                        v.tensor_copy(PV[:, ri, :, n:n + 1], PW[:, ri, :, L5 - 1 - n:L5 - n])
                o(ts(s[11], PW[:, 0, :, 1], -1.0, None, A))
                ni, lr, li = PW[:, 1, :, 1], s[1], prm_cols("lim")
                tt(s[12], lr, lr, M)
                o(tt(s[13], li, li, M))
                o(tt(s[12], s[12], s[13], A))
                o(v.reciprocal(s[12], s[12]))
                tt(s[13], s[11], lr, M)
                o(tt(s[14], ni, li, M))
                o(tt(s[13], s[13], s[14], A))
                tt(s[14], ni, lr, M)
                o(tt(s[15], s[11], li, M))
                o(tt(s[14], s[14], s[15], S_))
                tt(s[13], s[13], s[12], M)
                o(tt(s[14], s[14], s[12], M))
                coef = [s[13].unsqueeze(2).broadcast_to((P, NPR5, 16)), s[14].unsqueeze(2).broadcast_to((P, NPR5, 16))]
                cmul([(BB[:, 0], BB[:, 1], ident)], coef, [BC[:, 0], BC[:, 1]], tmps((NPR5, 16)))
                dve.wait_ge(unit_done, 2 * N_IN)
                for _ in range(3):
                    cmul([(s[9], s[8], ident)], [s[9], s[8]], [s[9], s[8]], tmps((NPR5,)))
                v.memset(ET[:, 0, :, 0:1], 1.0)
                o(v.memset(ET[:, 1, :, 0:1], 0.0))
                k = 1
                while k < NCP:
                    b = [x.unsqueeze(2).broadcast_to((P, NPR5, k)) for x in (s[9], s[8])]
                    cmul([(ET[:, 0, :, k:2 * k], ET[:, 1, :, k:2 * k], ident)], [ET[:, ri, :, 0:k] for ri in range(2)], b,
                         tmps((NPR5, k)))
                    cmul([(s[9], s[8], ident)], [s[9], s[8]], [s[9], s[8]], tmps((NPR5,)))
                    k *= 2
                v.memset(M1T[:, :, :, :, :], 0.0)
                v.memset(CL[:, :, :, :, :], 0.0)
                v.memset(HS[:, :, :, 0:1], 0.0)
                o(v.memset(TOE[:, :, :, :], 0.0))

            def s5(j5):
                pr = slice(4 * j5, 4 * j5 + 4)

                def blocks(dst):
                    return [(dst[64 * g:64 * g + 64, 0, :, :, 16 * g:16 * g + 16],
                             dst[64 * g:64 * g + 64, 1, :, :, 16 * g:16 * g + 16],
                             lambda ap, g=g: ap[64 * g:64 * g + 64]) for g in range(2)]

                if j5 > 0:
                    dve.wait_ge(toe_done, j5)
                    dve.wait_ge(g_out, j5)
                shape = (P, 4, L5, 16)
                a = [PV[:, ri, pr].unsqueeze(3).broadcast_to(shape) for ri in range(2)]
                b = [BB[:, ri, pr].unsqueeze(2).broadcast_to(shape) for ri in range(2)]
                cmul(blocks(M1T), a, b, tmps((4, L5, 16)))
                v.tensor_copy(RHO[:, :, :], S5[:, 10, pr].unsqueeze(2).broadcast_to((P, 4, NCP))).then_inc(m1t_ready, 1)
                if j5 > 0:
                    dve.wait_ge(y5_done, j5)
                shape = (P, 4, L5 + 1, 16)
                a = [PW[:, ri, pr].unsqueeze(3).broadcast_to(shape) for ri in range(2)]
                b = [BC[:, 2 + ri, pr].unsqueeze(2).broadcast_to(shape) for ri in range(2)]
                t = tmps((4, L5 + 1, 16))
                tt(t[0], a[0], b[0], M)
                tt(t[1], a[1], b[1], M)
                tt(t[2], a[0], b[1], M)
                o(tt(t[3], a[1], b[0], M))
                o(tt(t[2], t[2], t[3], A))
                for g in range(2):
                    q = slice(64 * g, 64 * g + 64)
                    tt(CL[q, 0, :, :, 16 * g:16 * g + 16], t[0][q], t[1][q], S_)
                    last = ts(CL[q, 1, :, :, 16 * g:16 * g + 16], t[2][q], -1.0, None, M)
                last.then_inc(cl_ready, 1)
                v.memset(RHO[:, :, 0:1], 0.0)
                dve.wait_ge(xs_evac, 2 * j5 + 2)
                t = tmps((4, NCP))
                e = [ET[:, ri, pr] for ri in range(2)]
                x = [XS[:, ri, :, 0:NCP] for ri in range(2)]
                tt(t[0], x[0], e[0], M)
                tt(t[1], x[1], e[1], M)
                tt(t[2], x[1], e[0], M)
                o(tt(t[3], x[0], e[1], M))
                tt(t[0], t[0], t[1], A)
                o(tt(t[2], t[2], t[3], S_))
                rho = RHO[:, :, :].rearrange("p j c -> p (j c)")
                for a_ in (0, 2):
                    last = v.tensor_tensor_scan(TM[:, a_ + 1, 0:4 * NCP], rho, TM[:, a_, 0:4 * NCP], 0.0, M, A)
                o(last)
                tt(t[0], t[1], e[0], M)
                tt(t[2], t[3], e[1], M)
                o(tt(HS4[:, 0], t[1], e[1], M))
                o(tt(HS4[:, 1], t[3], e[0], M))
                tt(t[0], t[0], t[2], S_)
                o(tt(t[1], HS4[:, 0], HS4[:, 1], A))
                for ri in range(2):
                    v.tensor_copy(HS[:, ri, :, 1:NCP], t[ri][:, :, 0:NCP - 1])
                    v.tensor_copy(HE[:, ri, pr], t[ri][:, :, NCP - 1])
                p8 = [PW[:, ri, pr, L5:L5 + 1].broadcast_to((P, 4, NB)) for ri in range(2)]
                for h in range(2):
                    hin = [HB[:, ri, h, pr] for ri in range(2)]
                    for ri in range(2):
                        v.tensor_copy(HS[:, ri, :, NCP + h * NB:NCP + (h + 1) * NB], hin[ri])
                    t = [TM[:, a_, 256:256 + 4 * NB].rearrange("p (a b) -> p a b", a=4) for a_ in range(4)]
                    tt(t[0], p8[0], hin[0], M)
                    tt(t[1], p8[1], hin[1], M)
                    tt(t[2], p8[0], hin[1], M)
                    o(tt(t[3], p8[1], hin[0], M))
                    tt(t[0], t[0], t[1], S_)
                    o(tt(t[2], t[2], t[3], A))
                    c = slice(NCP + h * NB, NCP + (h + 1) * NB)
                    tt(HB[:, 0, h + 1, pr], t[0], XS[:, 0, :, c], A)
                    o(tt(HB[:, 1, h + 1, pr], t[2], XS[:, 1, :, c], A))
                v.engine_nop().then_inc(hs_ready, 1)
                dve.wait_ge(y5_done, j5 + 1)
                for j in range(4):
                    a_ = (j % 2) * 2 * NC5
                    last = stt(UR[:, j, j5], UR[:, j, j5], prm_col("d5", 4 * j5 + j), PS[:, 6 + j // 2, a_:a_ + 2 * NC5], M, A)
                last.then_inc(y5_sum, 1)
                yv = UR[:, :, j5]
                dve.wait_ge(g_sq, j5 + 1)
                o(ts(GQ, GQ, 0.044715, 1.0, M, A))
                tt(GQ, GQ, yv, M).then_inc(g_arg, 1)
                dve.wait_ge(g_tanh, j5 + 1)
                stt(yv, GT, 1.0, yv, A, M).then_inc(g_out, 1)

            def glu():
                for j in range(4):
                    dve.wait_ge(glu_done, 4)
                    dve.wait_ge(glu_tanh, j + 1)
                    yv = UF[:, j].rearrange("p t c -> p (t c)")
                    stt(yv, TG[:, j], 1.0, yv, A, M).then_inc(glu_out, 1)

            def mix(tile, dst, between=lambda: None):
                d = TP[:, 0]
                zp = Z[:, tile, 1 + NP_TOK:ZW].rearrange("p (b t) -> p b t", b=NB)
                ds_ = d[:, NP_TOK:T].rearrange("p (b t) -> p b t", b=NB)
                tt(d[:, 0:NP_TOK], Z[:, tile, 0:NP_TOK], Z[:, tile, 1:1 + NP_TOK], S_)
                o(tt(ds_, zp[:, :, 0:ST], zp[:, :, 1:1 + ST], S_))
                between()
                stt(dst[:, 0:NP_TOK], d[:, 0:NP_TOK], prm_col("mu", tile), Z[:, tile, 1:1 + NP_TOK], M, A)
                o(stt(dst[:, NP_TOK:T].rearrange("p (b t) -> p b t", b=NB), ds_, prm_col("mu", tile),
                      zp[:, :, 1:1 + ST], M, A))
                between()

            def features(p, between):
                R, K, V, kappa = RKV[:, 0], RKV[:, 1], RKV[:, 2], KAPPA(p)
                T1, T2, T3, T4, T5 = [TP[:, a] for a in range(5)]
                if p == 0:
                    dve.wait_ge(glu_out, 4)
                    mix(12, TL[:, 0])
                    mix(13, TL[:, 1])
                    v.memset(AR[0:64, :, 1], 0.0)
                    v.memset(AR[64:P, :, 0], 0.0)
                    v.memset(SG[:, 0], 0.0).then_inc(mixed, 1)
                else:
                    dve.wait_ge(srw_stored, 16 * p)
                    v.engine_nop().then_inc(mixed, 1)
                mix(4 + p, K, between)
                v.engine_nop().then_inc(mixed, 1)
                mix(p, R, between)
                mix(8 + p, V, between)
                dve.wait_ge(wa_act, 2 * p + 1)
                o(ts(T1, T3, 1.0, -0.5 * EXPM05, A, M))
                for c in range(NCH + NB):
                    a = slice(c * CH, (c + 1) * CH) if c < NCH else slice(NP_TOK + (c - NCH) * ST, NP_TOK + (c - NCH + 1) * ST)
                    last = v.tensor_tensor_scan(T2[:, a], ONES[:, 0:a.stop - a.start], T1[:, a], 0.0, M, A)
                    if c % 4 == 3:
                        between()
                o(last)
                tt(T1, T2, T1, S_).then_inc(cs_ready, 1)
                between()
                dve.wait_ge(wa_act, 2 * p + 2)
                o(ts(T4, T4, 0.5, 0.5, M, A))
                ts(kappa, K, prm_col("k_k", p), None, M)
                between()
                o(ts(BETA, T4, -1.0, prm_col("k_a", p), A, M))
                stt(K, BETA, 1.0, K, A, M)
                between()
                dve.wait_ge(kk_norm, p + 1)
                o(ts(T5, T5, 1e-12, None, ALU.max))
                o(v.reciprocal(T5, T5))
                o(tt(T5, T5, kappa, M))
                tt(T4, T5, T4, M)
                dve.wait_ge(decay_exp, p + 1)
                five = lambda ap: ap.rearrange("p (a t) -> p a t", a=5)
                for hh in range(2):
                    r = slice(64 * hh, 64 * hh + 64)
                    stt(AR[r, :, hh, 0], five(T5)[r], -1.0, five(T1)[r], M, M)
                    last = tt(AR[r, :, hh, 1], five(R)[r], five(T3)[r], M)
                o(last)
                tt(BETA, T4, T2, M)
                tt(kappa, K, T2, M)
                v.tensor_copy(PEND[:, p % 2, 0:NCH], T3[:, CH - 1:NP_TOK:CH])
                v.tensor_copy(PEND[:, p % 2, NCH:NCH + NB], T3[:, NP_TOK + ST - 1:T:ST])
                stt(T1, R, prm_col("r_k", p), K, M, M).then_inc(feat_ready, 1)
                dve.wait_ge(bonus_sum, p + 1)
                tt(h2(BO[p % 2]), halves(2), h2(V), M).then_inc(bonus_ready, 1)

            def finish_1(p):
                T1 = TP[:, 0]
                dve.wait_ge(oo_done, p + 1)
                dve.wait_ge(o0_ready, 5 * p + 5)
                tt(h2(T1), halves(5), h2(O0), A).then_inc(o_ready, 1)

            def finish_2(p):
                dve.wait_ge(ln_sum, 3 * p + 1)
                stt(h2(TP[:, 1]), halves(5), -1.0 / 64, h2(TP[:, 0]), M, A).then_inc(oc_ready, 1)

            def finish_3(p):
                T2, T4 = TP[:, 1], TP[:, 3]
                dve.wait_ge(ln_sd, p + 1)
                o(v.reciprocal(T4, T4))
                o(tt(T2, T2, T4, M))
                o(ts(T2, T2, prm_col("lnw", p), prm_col("lnb", p), M, A))
                o(tt(T2, T2, BO[p % 2], A))
                dve.wait_ge(ln_sum, 3 * p + 3)
                tt(Z[:, p, 0:T].rearrange("p (h t) -> p h t", h=2), halves(5), h2(T2), M).then_inc(ab_out, 1)

            def tile_gm(p, i, hh):
                dve.wait_ge(gram_done, 10 * p + 5 * hh + i + 1)
                mask = CS[:, (C_SS if i == 0 else C_PS) * P:((C_SS if i == 0 else C_PS) + 2) * P]
                tt(GM[:, i, hh].rearrange("p (a c) t -> p a (c t)", a=2), PS[:, i, :].rearrange("p (a c) -> p a c", a=2),
                   mask.unsqueeze(1).broadcast_to((P, 2, 2 * P)), M).then_inc(gm_ready, 1)

            def tile_first(p, i):
                dve.wait_ge(lv_done, 5 * p + i + 1)
                tt(TT[:, i, 0], PS[:, i, 0:256].rearrange("p (h t) -> p h t", h=2),
                   cstt(C_L1).unsqueeze(1).broadcast_to((P, 2, P)), M)
                tt(TT[:, i, 1], GM[:, i, :, 0], cstt(C_U1).unsqueeze(1).broadcast_to((P, 2, P)), M)
                o(v.tensor_copy(AW[:, i, :, 1], PS[:, i, 256:384].rearrange("p (h k) -> p h k", h=2)))
                tv = TT[:, i].rearrange("p a h t -> p (a h) t")
                tt(tv, tv, IDN.unsqueeze(1).broadcast_to((P, 4, P)), A).then_inc(tt_first, 1)

            def level(p, l):
                for i in active(l):
                    dve.wait_ge(lx_done, lvn(p, l, i) + 1)
                    tt(XM[:, i], PS[:, i, 0:256].rearrange("p (h t) -> p h t", h=2),
                       cstt(C_LV + l).unsqueeze(1).broadcast_to((P, 2, P)), M).then_inc(xm_ready, 1)
                for i in active(l):
                    dve.wait_ge(lt_done, lvn(p, l, i) + 1)
                    if l + 1 < LEVELS[i]:
                        tf = TT[:, i].rearrange("p a h t -> p (a h t)")
                        tt(tf, tf, PS[:, i, :], A).then_inc(tt_ready, 1)
                    else:
                        tf = TT[:, i, 1].rearrange("p h t -> p (h t)")
                        tt(tf, tf, PS[:, i, 256:512], A).then_inc(tt_ready, 1)

            def tile_rt(p, i):
                t = ORDER[i]
                dve.wait_ge(ro_done, 5 * p + i + 1)
                for hh in range(2):
                    r = slice(64 * hh, 64 * hh + 64)
                    last = tt(RT(p)[r, t * P:(t + 1) * P], PS[r, i, 0:P], AR[r, t, hh, 1], A)
                last.then_inc(rt_ready, 1)

            def masked(a, src):
                return tt(TM3[:, a], src.unsqueeze(1).broadcast_to((P, NB, P)), ROWM.unsqueeze(2).broadcast_to((P, NB, P)), M)

            def tiles(p):
                if p > 0:
                    finish_1(p - 1)
                for i in range(5):
                    tile_gm(p, i, 0)
                if p > 0:
                    finish_2(p - 1)
                for i in range(5):
                    tile_gm(p, i, 1)
                for i in range(5):
                    tile_first(p, i)
                if p > 0:
                    finish_3(p - 1)
                    dve.wait_ge(ab_out, p)
                level(p, 0)
                dve.wait_ge(tok_ready, 5 * p + 1)
                masked(0, TOK[:, 0, 0])
                level(p, 1)
                masked(2, TOK[:, 0, 2])
                level(p, 2)
                level(p, 3)
                tile_rt(p, 0)
                dve.wait_ge(au_ready, 5 * p + 1)
                masked(1, AU[:, 0, 1].rearrange("p h k -> p (h k)")).then_inc(um_ready, 1)
                level(p, 4)

                def quarter(h):
                    q = slice(4 * h, 4 * h + 4)
                    pend = PEND[:, p % 2, NCH + 4 * h:NCH + 4 * h + 4].unsqueeze(2).broadcast_to((P, 4, P))
                    return q, PS[:, (7, 0)[h], :].rearrange("p (b c) -> p b c", b=4), pend
                four = (P, 4, P)
                for h in range(2):
                    q, ps, pend = quarter(h)
                    dve.wait_ge(gh_done, GH_PAIR * p + h + 1)
                    o(tt(GH[:, 0, q], ps, BD.unsqueeze(1).broadcast_to(four), M))
                    tt(GH[:, 0, q], GH[:, 0, q], IDN.unsqueeze(1).broadcast_to(four), A).then_inc(ghs_ready, 1)
                for h in range(2):
                    q, ps, pend = quarter(h)
                    dve.wait_ge(gh_done, GH_PAIR * p + 2 + h + 1)
                    o(tt(GH[:, 1, q], ps, pend, M))
                    tt(GH[:, 1, q], GH[:, 1, q], BD.unsqueeze(1).broadcast_to(four), M).then_inc(ghs_ready, 1)
                for i in range(1, 5):
                    tile_rt(p, i)
                dve.wait_ge(st_done, p * (NCH + 1) + 1)
                dve.wait_ge(ghs_ready, 4 * p + 4)
                for h in range(2):
                    q, ps, pend = quarter(h)
                    o(tt(TM3[:, 0, q], ps, pend, M))
                o(tt(TM3[:, 0], TM3[:, 0], GH[:, 1], A))
                v.engine_nop().then_inc(st_ready, 1)
                v.engine_nop().then_inc(gh_ready, 1)
                for i in range(1, 5):
                    ch = 2 * ORDER[i]
                    ps = PS[:, i, :].rearrange("p (c a k) -> p c a k", c=2, a=2)
                    two = (P, 2, P)
                    dve.wait_ge(gh_done, GH_PAIR * p + 8 + i)
                    tt(GH[:, 0, ch:ch + 2], ps[:, :, 0], BD.unsqueeze(1).broadcast_to(two), M)
                    for c in range(2):
                        last = stt(GH[:, 1, ch + c], ps[:, c, 1], PEND[:, p % 2, ch + c:ch + c + 1], BD, M, M)
                    o(last)
                    tt(GH[:, 0, ch:ch + 2], GH[:, 0, ch:ch + 2], IDN.unsqueeze(1).broadcast_to(two), A).then_inc(gh_ready, 1)

            def chain(p, c):
                if c == 0 and p > 0:
                    dve.wait_ge(prw_stored, 16 * p)
                dve.wait_ge(st_done, p * (NCH + 1) + 2 + c)
                stt(SG[:, c + 1], PS[:, (5, 7)[c % 2], 0:P], PEND[:, p % 2, c:c + 1], GH[:, 1, c], M, A).then_inc(st_ready, 1)

            def rwkv():
                features(0, lambda: None)
                for p in range(NPAIR):
                    tiles(p)
                    left = list(range(NCH))
                    if p + 1 < NPAIR:
                        features(p + 1, lambda: left and chain(p, left.pop(0)))
                    while left:
                        chain(p, left.pop(0))
                dve.wait_ge(srw_stored, 16 * NPAIR)
                finish_1(NPAIR - 1)
                finish_2(NPAIR - 1)
                finish_3(NPAIR - 1)

            def ab_low():
                for k in range(KT):
                    dve.wait_ge(xn_hi, KT + k + 1)
                    if k < 4:
                        dve.wait_ge(ab_out, 4)
                        tt(XL[:, k], Z[:, k, 0:T], XH[:, k].bitcast(F32), S_).then_inc(xn_lo, 1)
                    else:
                        if k == 4:
                            dve.wait_ge(glu_out, 4)
                        hi = XH[:, k].bitcast(F32)
                        stt(prompt_cols(XL[:, k]), UF[:, k - 4, :, 0:NCP], 0.25, prompt_cols(hi), M, S_)
                        for h in range(2):
                            last = stt(sample_cols(XL[:, k], h), UF[:, k - 4, :, NCP + h * NB:NCP + (h + 1) * NB], 0.25,
                                       sample_cols(hi, h), M, S_)
                        last.then_inc(xn_lo, 1)

            def add_tiles(name):
                dve.wait_ge(unit_evac, unit0(name))
                for k in range(KT):
                    u = unit0(name) + k
                    dve.wait_ge(unit_done, u + 1)
                    xk = h2(X[:, k])
                    tt(xk, halves(2 * (k % 2)), xk, A).then_inc(unit_evac, 1)

            def add_halves(name):
                u0 = unit0(name)
                dve.wait_ge(unit_evac, u0)
                with dve.Fori(0, KT) as i:
                    for j in range(2):
                        dve.wait_ge(unit_done, 2 * i + (u0 + j + 1))
                        xk = X[:, bass.ds(i, 1), j * HALF:(j + 1) * HALF].rearrange("p a t -> p (a t)")
                        tt(xk, PS[:, 2 * j, 0:HALF], xk, A).then_inc(unit_evac, 1)

            def hidden(name, hidx):
                u0, b = unit0(name), FF_TILES * hidx
                with dve.Fori(0, FF_TILES // 2) as i:
                    for j in range(2):
                        dve.wait_ge(unit_evac, 2 * i + (u0 + j + 1))
                        tt(SC[:, 2 + j], SC[:, j], SC[:, j], M).then_inc(h_sq, 1)
                        dve.wait_ge(h_hi, 2 * i + (b + j + 1))
                        m = bass.ds(2 * i + j, 1)
                        tt(HL[:, m].rearrange("p a t -> p (a t)"), SC[:, 2 + j],
                           HH[:, m].rearrange("p a t -> p (a t)").bitcast(F32), S_).then_inc(h_lo, 1)

            def attention():
                dve.wait_ge(unit_done, unit0("qkv"))
                v.memset(VP[:, :, 0:CH], 0.0).then_inc(v_pad, 1)
                for j in range(10):
                    src = Q[:, j] if j < 8 else KR[:, j - 8]
                    dve.wait_ge(qk_rms, j + 1)
                    r = SC[:, 2 + j % 2]
                    o(v.reciprocal(r, r))
                    stt(src, src, prm_col("qn" if j < 8 else "kn"), r, M, M).then_inc(qk_ready, 1)
                dve.wait_ge(qk_ready, 10)
                for kv in range(4):
                    i, src = kv // 2, slice(64 * (kv % 2), 64 * (kv % 2) + 64)
                    for half in range(2):
                        r = slice(64 * half, 64 * half + 64)
                        v.tensor_copy(KD[r, kv], KR[src, i, 0:NP_TOK])
                        v.tensor_copy(KS[r, kv, :, CH:KEYS], KR[src, i, NP_TOK:T].rearrange("p (b t) -> p b t", b=NB))
                    last = v.tensor_copy(QSV[:, kv].rearrange("p b a t -> p a b t"),
                                         Q[:, 2 * kv:2 * kv + 2, NP_TOK:T].rearrange("p a (b t) -> p a b t", b=NB))
                last.then_inc(kd_ready, 1)
                for u in range(18):
                    t, kv = u // 4, u % 4
                    dve.wait_ge(sc_done, u + 1)
                    if u < 16:
                        g1, kk, ng = 2, P, 4
                        sink = SK[:, 4 * kv:4 * kv + 4].rearrange("p (a b) -> p a b", a=2)
                        if t == 0:
                            for half in range(2):
                                pv = PS[0:64, half, 0:256].rearrange("p (a k) -> p a k", a=2)
                                last = v.memset(pv[:, :, 0:64], -1e30)
                            o(last)
                    else:
                        g1, kk, ng = 4, KEYS, 8
                        sink = SK[:, 16:18].unsqueeze(2).broadcast_to((P, 2, 4))
                    ps = PS[:, 0:2, 0:g1 * kk].rearrange("p h (a k) -> p h a k", a=g1)
                    sm = [SM[:, a, 0:ng].rearrange("p (h a) -> p h a", h=2) for a in range(6)]
                    e = EE[:, u % 2, 0:ng * kk].rearrange("p (h a k) -> p h a k", h=2, a=g1)
                    o(v.tensor_reduce(sm[0], ps, AX.X, ALU.max))
                    o(tt(sm[1], sm[0], sink, ALU.max))
                    tt(sm[2], sink, sm[1], S_)
                    tt(e, ps, sm[1].unsqueeze(3).broadcast_to((P, 2, g1, kk)), S_).then_inc(sm_sub, 1)
                    dve.wait_ge(sm_exp, u + 1)
                    o(v.tensor_reduce(sm[4], e, AX.X, A))
                    o(tt(sm[4], sm[4], sm[3], A))
                    o(v.reciprocal(sm[5], sm[4]))
                    tt(e, e, sm[5].unsqueeze(3).broadcast_to((P, 2, g1, kk)), M).then_inc(sm_p, 1)
                    dve.wait_ge(o_hi, u + 1)
                    ps, dst = o_tiles(u, XL)
                    _, hi = o_tiles(u, XH)
                    tt(dst, ps, hi.bitcast(F32), S_).then_inc(o_lo, 1)

            dve.wait_ge(z_edge, 16)
            v.tensor_copy(Z[:, :, 0:1], ZL[:, :, 0:1])
            zt = Z[:, :, 1 + NP_TOK:ZW].rearrange("p a (b t) -> p a b t", b=NB)
            v.tensor_copy(zt[:, :, :, 0], ZL[:, :, 1:1 + NB])
            dve.wait_ge(params_in, 32)
            o(ts(HP[:, :], PR[:, PRM["w0"][0]:PRM["w0"][0] + 8], 0.5, None, M))
            o(ts(SK[:, :], PR[:, PRM["sinkp"][0]:PRM["sinkp"][0] + 18], 8.0, None, M))
            norm(0, 0)
            s5_scalars()
            for j in range(4):
                s5(j)
            dve.wait_ge(unit_evac, 2 * N_IN)
            v.tensor_copy(ZL[:, :, 0:1], Z[:, :, NP_TOK:NP_TOK + 1])
            o(v.tensor_copy(ZL[:, :, 1:1 + NB], Z[:, :, 1 + NP_TOK:ZW].rearrange("p a (b t) -> p a b t", b=NB)[:, :, :, ST]))
            v.engine_nop().then_inc(zl_ready, 1)
            glu()
            rwkv()
            ab_low()
            add_tiles("out")
            norm(1, 2)
            for hf in range(2):
                hidden(f"up0{hf}", hf)
                add_halves(f"dn0{hf}")
            norm(2, 3)
            attention()
            add_tiles("ao")
            norm(3, 4)
            for hf in range(2):
                hidden(f"up1{hf}", 2 + hf)
                add_halves(f"dn1{hf}")


SHAPES = [(P, KT, T), (P, A_TILES, 1 + NB), (NPAIR, P, NB, P), (NPAIR, P, P), (P, 2, NPR5), (P, 2, NPR5, NB),
          (P, 2, 2, 256), (NB, 112 * 256), (NB, 112 * 256)]


def constants():
    import numpy as np
    r, c = np.arange(P)[:, None], np.arange(P)[None, :]
    tiles = [r == c, r >= 0 * c, r // 64 == c // 64]
    for ch in (CH, ST):
        same = r // ch == c // ch
        tiles += [same & (r < c), same & (r <= c)]
    pair = (r // 2 == c // 2)
    tiles += [pair & (r > c), pair & (r < c)]
    for m in (2, 4, 8, 16, 32):
        tiles.append((r // (2 * m) == c // (2 * m)) & (r % (2 * m) >= m) & (c % (2 * m) < m))
    tiles = [np.broadcast_to(x, (P, P)) for x in tiles]
    tiles.append(r // ST == np.arange(NB)[None, :])
    return np.concatenate(tiles, axis=1).astype(np.float32)


def cols(a):
    return a.reshape(-1, P).T


def kernel(**inputs):
    import numpy as np
    import concourse.bacc as bacc
    from concourse.bass_utils import run_bass_kernel_spmd

    x = {k: np.asarray(v) for k, v in inputs.items()}
    f = np.float32
    tok = np.concatenate([x["x_prompt"].reshape(NP_TOK, D), x["x_sample"].reshape(NB * ST, D)], axis=0)

    def up(wm):
        n = wm.shape[1] // 256
        return wm.reshape(KT, P, n, 256).transpose(2, 1, 0, 3).reshape(n, P, SLOT)

    def down(wm):
        n = wm.shape[1] // P
        return wm.reshape(FF_TILES, P, n, P).transpose(2, 1, 0, 3).reshape(n, P, SLOT)

    w_in = up(x["ab_w_in"][0])[[6, 7, 8, 0, 2, 4, 1, 3, 5]]
    slots = [w_in, up(x["ab_w_out"][0])]
    for l in range(2):
        if l:
            slots += [up(x["att_w_qkv"][0]), up(x["att_w_out"][0])]
        for h in range(2):
            slots += [up(x["ffn_w1"][l][:, h * 2048:(h + 1) * 2048]), down(x["ffn_w2"][l][h * 2048:(h + 1) * 2048])]
    w = np.concatenate(slots, axis=0)

    def pairs(a):
        return np.moveaxis(a.reshape((NPR5, P) + a.shape[2:]), 1, 0)

    def const(v):
        return np.full((P, 1), v, f)

    d5 = np.broadcast_to(x["s5_d"][0].reshape(NPR5, 1, 32), (NPR5, 4, 32)).reshape(NPR5, P).T
    sinks = x["att_sinks"][0].reshape(4, 2, 2)
    parts = [cols(x["ab_mu"][0])]
    parts += [cols(x[n][0]) for n in ("rwkv_w0", "rwkv_a0", "rwkv_k_k", "rwkv_k_a")]
    parts += [cols(x["rwkv_r_k"][0].reshape(-1)), cols(x["rwkv_lnx_w"][0]), cols(x["rwkv_lnx_b"][0])]
    parts += [cols(x[n][l]) for l in range(2) for n in ("norm_mix", "norm_ffn")]
    parts += [np.tile(x["att_q_norm"][0], 2)[:, None], np.tile(x["att_k_norm"][0], 2)[:, None]]
    parts += [const(1e-6), const(64e-5), const(np.pi / 2), d5, pairs(x["s5_lam_re"][0]), pairs(x["s5_lam_im"][0]),
              pairs(np.broadcast_to(x["s5_log_dt"][0][:, None], (32, 64)))]
    parts += [np.broadcast_to(sinks.transpose(0, 2, 1).reshape(1, 16), (P, 16)),
              np.broadcast_to(sinks[:, :, None, :], (4, 2, ST, 2)).reshape(P, 2)]
    prm = np.concatenate(parts, axis=1)
    bc5 = np.stack([pairs(x["s5_b_re"][0]), pairs(x["s5_b_im"][0]), pairs(x["s5_c_re"][0].transpose(0, 2, 1)),
                    pairs(x["s5_c_im"][0].transpose(0, 2, 1))], axis=1)
    h05 = np.stack([pairs(x[n][0].transpose(1, 2, 0)) for n in ("state_ssm_re", "state_ssm_im")], axis=1)
    s0 = np.zeros((NPAIR, 2, 64, NB, 2, 64), f)
    st = x["state_rwkv"][0].reshape(NB, NPAIR, 2, 64, 64)
    for hh in range(2):
        s0[:, hh, :, :, hh] = st[:, :, hh].transpose(1, 3, 0, 2)
    shift = np.zeros((P, A_TILES, 1 + NB), f)
    shift[:, :, 1:] = x["state_shift"][0].reshape(NB, A_TILES, P).transpose(2, 1, 0)
    ck, cv = x["cache_k"][0], x["cache_v"][0]
    ckT = np.tile(ck[:, 64:].transpose(3, 2, 0, 1), (2, 1, 1, 1))
    arrays = dict(
        xT=tok.T.reshape(KT, P, T).transpose(1, 0, 2), w=w, prm=prm, cst=constants(), shift=shift,
        w2a2=np.concatenate([x["rwkv_w2"][0], x["rwkv_a2"][0]], axis=0), g2=x["rwkv_g2"][0],
        wglu=x["s5_w_glu"][0].reshape(4, P, 512).transpose(1, 0, 2), bc5=bc5, h05=h05,
        s0=s0.reshape(NPAIR, P, NB, P), ckT=ckT, cv=cv[:, 64:].reshape(NB, 64, 256).transpose(1, 0, 2),
        cko=ck[:, ST:].reshape(NB, 112 * 256), cvo=cv[:, ST:].reshape(NB, 112 * 256))

    nc = bacc.Bacc("TRN2", target_bir_lowering=False, num_devices=1)
    ins = {f"in_{n}": np.ascontiguousarray(a) for n, a in arrays.items()}
    args = [nc.dram_tensor(n, a.shape, mybir.dt.from_np(a.dtype), kind="ExternalInput").ap() for n, a in ins.items()]
    args += [nc.dram_tensor(f"out_{i}", s, F32, kind="ExternalOutput").ap() for i, s in enumerate(SHAPES)]
    hybrid_step(nc, *args)
    r = run_bass_kernel_spmd(nc, [ins], core_ids=[0])
    y, shift_o, srw, prw, s5p, s5s, kv, cko, cvo = [r.results[0][f"out_{i}"] for i in range(len(SHAPES))]

    yt = y.transpose(1, 0, 2).reshape(D, T).T
    sh = shift_o.transpose(2, 1, 0).reshape(1 + NB, A_TILES * P)

    def heads(a):
        a = a.reshape(NPAIR, 2, 64, -1, 2, 64)
        d = np.stack([a[:, h, :, :, h] for h in range(2)], axis=1)
        return d.transpose(3, 0, 1, 4, 2).reshape(-1, 8, 64, 64)

    def ungroup(a):
        return np.moveaxis(a, 1, 0).reshape((32, 64) + a.shape[2:])

    def frames(i, lo, n):
        return kv[:, i, :, lo:lo + n].transpose(2, 1, 0).reshape(n, 4, 64)

    def cache(old, i):
        return np.concatenate([old.reshape(NB, 112, 4, 64), frames(i, 128, 128).reshape(NB, ST, 4, 64)], axis=1)[None]

    return (yt[:NP_TOK].reshape(1, NP_TOK, D), yt[NP_TOK:].reshape(NB, ST, D),
            heads(prw)[None], sh[None, 0:1], ungroup(s5p[:, 0])[None, None], ungroup(s5p[:, 1])[None, None],
            frames(0, 0, 128)[None, None], frames(1, 0, 128)[None, None],
            heads(srw)[None], sh[None, 1:], ungroup(s5s[:, 0]).transpose(2, 0, 1)[None],
            ungroup(s5s[:, 1]).transpose(2, 0, 1)[None], cache(cko, 0), cache(cvo, 1))
```

```python
from contextlib import ExitStack

import concourse.bass as bass
from concourse import mybir

F32 = mybir.dt.float32
F32R = mybir.dt.float32r
ALU = mybir.AluOpType
ACT = mybir.ActivationFunctionType
AX = mybir.AxisListType

P = 128
D = 1024
KT = D // P
NP_TOK, NB, ST = 512, 8, 16
T = NP_TOK + NB * ST
HALF = T // 2
NPAIR = 4
A_TILES = 14
ZW = 1 + NP_TOK + NB * (1 + ST)
CH = 64
NCH = NP_TOK // CH
L5 = 8
NC5 = T // L5
NCP = NP_TOK // L5
NPR5 = 16
SLOT = 2048
FF_TILES = 16
KEYS = 80
EXPM05 = 0.6065306597126334
GELU_C = 0.7978845608028654
TWO_PI_HI, TWO_PI_LO = 6.28125, 0.0019353071795864769
ROUND = 12582912.0

N_IN, N_OUT, N_FF, N_QKV = 9, 4, 8, 6
SLOTS = N_IN + N_OUT + 4 * N_FF + N_QKV + N_OUT + 4 * N_FF
AB_ORDER = [4, 5, 6, 0, 1, 2, 7, 3]
QKV_TILES = [8, 9, 0, 1, 2, 3, 4, 5, 10, 11, 6, 7]
NORM_TILES = [t for t in QKV_TILES if t < 10]
UNITS = 18
IN_TILES = [12, 13, 14, 15, 16, 17, 0, 1, 4, 5, 8, 9, 2, 3, 6, 7, 10, 11]

PRM = {}
_at = 0
for _name, _n in (("mu", 14), ("w0", 4), ("a0", 4), ("k_k", 4), ("k_a", 4), ("r_k", 4), ("lnw", 4), ("lnb", 4),
                  ("g", 32), ("qn", 1), ("kn", 1), ("eps", 1), ("eps_ln", 1), ("halfpi", 1), ("d5", 16), ("lre", 16),
                  ("lim", 16), ("ldt", 16), ("sinkp", 16), ("sinks", 2)):
    PRM[_name] = (_at, _n)
    _at += _n
PRM_COLS = _at
C_ID, C_ONE, C_BD, C_PS, C_SS, C_L1, C_U1, C_LV = 0, 1, 2, 3, 5, 7, 8, 9
CST_COLS = 14 * P + NB


def hybrid_step(nc, xT, w, prm, cst, shift, w2a2, g2, wglu, bc5, h05, s0, ckT, cv, cko, cvo,
                y, o_shift, o_srw, o_prw, o_s5p, o_s5s, o_kv, o_ck, o_cv):
    with ExitStack() as ctx:
        def sb(name, shape, dt=F32, c=ctx):
            return c.enter_context(nc.sbuf_tensor(name, shape, dt))

        PS = ctx.enter_context(nc.psum_tensor("PS", [P, 8, 512], F32))

        X = sb("X", [P, KT, T])
        WR = sb("WR", [P, 2, SLOT])
        PR = sb("PR", [P, PRM_COLS])
        CS = sb("CS", [P, CST_COLS])
        SC = sb("SC", [P, 4, T])
        ZL = sb("ZL", [P, A_TILES, 1 + NB])
        HP = sb("HP", [P, 8])
        SK = sb("SK", [P, 18])
        KN = sb("KN", [P, 20])
        with ExitStack() as c0:
            GM = sb("GM", [P, 5, 2, 4, P], F32, c0)
            TT = sb("TT", [P, 5, 2, 2, P], F32, c0)
            W2 = sb("W2", [P, 512], F32, c0)
        with ExitStack() as c8:
            M1T = sb("M1T", [P, 2, 4, L5, 32], F32, c8)
            GT = sb("GT", [P, 4, 2 * NC5], F32, c8)
        WH = sb("WH", [P, 2, SLOT], F32R)
        WL = sb("WL", [P, 2, SLOT], F32R)
        with ExitStack() as c1:
            HH = sb("HH", [P, FF_TILES, T], F32R, c1)
            HL = sb("HL", [P, FF_TILES, T], F32R, c1)
            XH = sb("XH", [P, KT, T], F32R, c1)
            XL = sb("XL", [P, KT, T], F32R, c1)
        with ExitStack() as c3:
            Z = sb("Z", [P, A_TILES, ZW], F32, c3)
            UF = sb("UF", [P, 4, L5, NC5], F32, c3)
            with ExitStack() as c4:
                UR = sb("UR", [P, 4, 4, 2 * NC5], F32, c4)
                TM = sb("TM", [P, 4, 576], F32, c4)
                PW = sb("PW", [P, 2, NPR5, L5 + 1], F32, c4)
                PV = sb("PV", [P, 2, NPR5, L5], F32, c4)
                BC = sb("BC", [P, 4, NPR5, 16], F32, c4)
                BB = sb("BB", [P, 2, NPR5, 16], F32, c4)
                S5 = sb("S5", [P, 16, NPR5], F32, c4)
                RHO = sb("RHO", [P, 4, NCP], F32, c4)
                HE = sb("HE", [P, 2, NPR5], F32, c4)
                HB = sb("HB", [P, 2, 3, NPR5, NB], F32, c4)
                M1 = sb("M1", [P, 2, 2, 4, P], F32, c4)
                CL2 = sb("CL", [P, 2, 2, 4, L5 + 1, 32], F32, c4)
                TOE = sb("TOE", [P, 2, 4, P], F32, c4)
                GQ = sb("GQ", [P, 4, 2 * NC5], F32, c4)[:, :, :]
                TS = sb("TS", [P, 4, 4, NB], F32, c4)
                XS = sb("XS", [P, 2, 4, NC5], F32, c4)
                HS = sb("HS", [P, 2, 4, NC5], F32, c4)
            ET = SC[:, :, :].rearrange("p a c -> p (a c)")[:, 0:2 * NPR5 * NCP].rearrange("p (a b c) -> p a b c", a=2, b=NPR5)
            HS4 = TM[:, 0:2, 4 * NCP:8 * NCP].rearrange("p a (j c) -> p a j c", j=4)
            with ExitStack() as c5:
                GH = sb("GH", [P, 2, 8, P], F32, c5)
                G2 = sb("G2", [P, 512], F32, c5)
                RKV = sb("RKV", [P, 3, T], F32, c5)
                TP = sb("TP", [P, 5, T], F32, c5)
                SG = sb("SG", [P, NCH + 1, P], F32, c5)
                AR = sb("AR", [P, 5, 2, 2, P], F32, c5)
                BETA = sb("BETA", [P, T], F32, c5)[:, :]
                TOK = sb("TOK", [P, 5, 3, P], F32, c5)
                AW = sb("AW", [P, 5, 2, 2, 64], F32, c5)
                AU = sb("AU", [P, 5, 2, 2, 64], F32, c5)
                XM = sb("XM", [P, 5, 2, P], F32, c5)
                S0 = sb("S0", [P, NB, P], F32, c5)
                PEND = sb("PEND", [P, 2, 16], F32, c5)
            TL, BO, O0 = SC[:, 0:2], [SC[:, 2], Z[:, 12, 0:T]], SC[:, 3]
            TM3 = TP[:, :, :].rearrange("p a t -> p (a t)")[:, 0:3072].rearrange("p (a b t) -> p a b t", a=3, b=8)

            WG = WR[:, 0].rearrange("p (k c) -> p k c", k=4)
            GO = [Z[:, n, 0:T] for n in (13, 4, 8, 5)]
            GO5 = [g.rearrange("p (t c) -> p t c", t=L5) for g in GO]

            def RT(p):
                return Z[:, 4 + p, 0:T]

            def KAPPA(p):
                return Z[:, 8 + p, 0:T]
        with ExitStack() as c7:
            Q = sb("Q", [P, 8, T], F32, c7)
            KR = sb("KR", [P, 2, T], F32, c7)
            VP = sb("VP", [P, 2, CH + T], F32, c7)
            KD = sb("KD", [P, 4, NP_TOK], F32, c7)
            KS = sb("KS", [P, 4, NB, KEYS], F32, c7)
            VW = sb("VW", [P, NCH, 256], F32, c7)
            VS = sb("VS", [P, NB, 256], F32, c7)
            EE = sb("EE", [P, 2, 4 * KEYS * 2], F32, c7)
            PT = sb("PT", [P, 8, P], F32, c7)
            SM = sb("SM", [P, 2, 6, 16], F32, c7)

        qs_flat = SC[:, 2:4].rearrange("p a t -> p (a t)")[:, 0:1024]
        QS = qs_flat.rearrange("p (k b c) -> p k b c", k=4, b=NB)
        QSV = qs_flat.rearrange("p (k b a t) -> p k b a t", k=4, b=NB, a=2)

        def o_tiles(u, x):
            bank = (3, 7)[u % 2]
            if u < 16:
                t, kv = u % 4, u // 4
                return PS[:, bank, 0:256].rearrange("p (a q) -> p a q", a=2), x[:, 2 * kv:2 * kv + 2, t * P:(t + 1) * P]
            a = NP_TOK + 64 * (u - 16)
            return PS[:, bank, :].rearrange("p (a q) -> p a q", a=8), x[:, :, a:a + 64]

        def prm_col(name, i=0):
            return PR[:, PRM[name][0] + i:PRM[name][0] + i + 1]

        def prm_cols(name):
            return PR[:, PRM[name][0]:PRM[name][0] + PRM[name][1]]

        def cstt(i):
            return CS[:, i * P:(i + 1) * P]

        IDN, ONES, BD = cstt(C_ID), cstt(C_ONE), cstt(C_BD)
        ROWM = CS[:, 14 * P:14 * P + NB]

        def prompt_cols(ap2d):
            return ap2d[:, 0:NP_TOK].rearrange("p (c t) -> p t c", t=L5)

        def sample_cols(ap2d, h):
            return ap2d[:, NP_TOK:T].rearrange("p (b h t) -> p h t b", h=2, t=L5)[:, h]

        def sem(name):
            return ctx.enter_context(nc.semaphore(name))

        params_in = sem("params_in")
        x_in = [sem(f"x_in{k}") for k in range(KT)]
        w_in = [sem("w_in0"), sem("w_in1")]
        w_split = sem("w_split")
        unit_done = sem("unit_done")
        unit_evac = sem("unit_evac")
        sq_added = sem("sq_added")
        sq_ready, norm_sum, rms_ready = sem("sq_ready"), sem("norm_sum"), sem("rms_ready")
        xn_t, xn_hi, xn_lo = sem("xn_t"), sem("xn_hi"), sem("xn_lo")
        h_sq, h_hi, h_lo = sem("h_sq"), sem("h_hi"), sem("h_lo")
        dve_seq, act_seq = sem("dve_seq"), sem("act_seq")
        u_relayout, glu_w_in, s5_in = sem("u_relayout"), sem("glu_w_in"), sem("s5_in")
        y_relayout = [sem(f"y_relayout{a}") for a in range(4)]
        s5_arg, s5_fn = sem("s5_arg"), sem("s5_fn")
        m1t_ready, m1_transposed, m1_ready = sem("m1t_ready"), sem("m1_transposed"), sem("m1_ready")
        cl_ready, toe_done, toe_ready = sem("cl_ready"), sem("toe_done"), sem("toe_ready")
        xs_done, xs_evac, hs_ready = sem("xs_done"), sem("xs_evac"), sem("hs_ready")
        y5_done, y5_sum, g_sq, g_arg, g_tanh, g_out = (sem("y5_done"), sem("y5_sum"), sem("g_sq"), sem("g_arg"),
                                                       sem("g_tanh"), sem("g_out"))
        glu_done, glu_tanh, glu_out = sem("glu_done"), sem("glu_tanh"), sem("glu_out")
        z_edge, zl_ready, lora_w_in, s0_in = sem("z_edge"), sem("zl_ready"), sem("lora_w_in"), sem("s0_in")
        srw_stored, prw_stored = sem("srw_stored"), sem("prw_stored")
        ln_inv, ln_spread, ln_scaled = sem("ln_inv"), sem("ln_spread"), sem("ln_scaled")
        rwkv_zeros, bonus_in = sem("rwkv_zeros"), sem("bonus_in")
        mixed, lora_act, wa_done, wa_act = sem("mixed"), sem("lora_act"), sem("wa_done"), sem("wa_act")
        kk_sq, kk_sum, kk_norm = sem("kk_sq"), sem("kk_sum"), sem("kk_norm")
        kk_inv, kk_spread, b_ready, bk_ready = sem("kk_inv"), sem("kk_spread"), sem("b_ready"), sem("bk_ready")
        rms_inv, rms_spread = sem("rms_inv"), sem("rms_spread")
        s5_zeros, sm_inv = sem("s5_zeros"), sem("sm_inv")
        pool_seq, g2_in = sem("pool_seq"), sem("g2_in")
        cs_ready, decay_exp, feat_ready = sem("cs_ready"), sem("decay_exp"), sem("feat_ready")
        bonus_sum, bonus_ready = sem("bonus_sum"), sem("bonus_ready")
        tr_done, tok_ready, gram_done, gm_ready = sem("tr_done"), sem("tok_ready"), sem("gram_done"), sem("gm_ready")
        lv_done = sem("lv_done")
        lx_done, xm_ready, lt_done = sem("lx_done"), sem("xm_ready"), sem("lt_done")
        tt_first, tt_ready = sem("tt_first"), sem("tt_ready")
        au_done, au_ready, ro_done, rt_ready, o0_ready = (sem("au_done"), sem("au_ready"), sem("ro_done"),
                                                          sem("rt_ready"), sem("o0_ready"))
        um_ready, gh_done, ghs_ready, gh_ready = sem("um_ready"), sem("gh_done"), sem("ghs_ready"), sem("gh_ready")
        st_done, st_ready = sem("st_done"), sem("st_ready")
        oo_done, o_ready, ln_sum, oc_ready, ln_sq, ln_sd, ab_out = (sem("oo_done"), sem("o_ready"), sem("ln_sum"),
                                                                   sem("oc_ready"), sem("ln_sq"), sem("ln_sd"),
                                                                   sem("ab_out"))
        qk_inv, qk_spread = sem("qk_inv"), sem("qk_spread")
        qk_sq, qk_sum, qk_rms, qk_ready = sem("qk_sq"), sem("qk_sum"), sem("qk_rms"), sem("qk_ready")
        v_pad, kd_ready, cache_in, vw_tr, vw_ready = (sem("v_pad"), sem("kd_ready"), sem("cache_in"), sem("vw_tr"),
                                                      sem("vw_ready"))
        qs_ready = sem("qs_ready")
        sc_done, sm_sub, sm_exp, sm_p = sem("sc_done"), sem("sm_sub"), sem("sm_exp"), sem("sm_p")
        pt_tr, pt_ready, pv_done, o_hi, o_lo = sem("pt_tr"), sem("pt_ready"), sem("pv_done"), sem("o_hi"), sem("o_lo")
        stored = sem("stored")

        AO = N_IN + N_OUT + 4 * N_FF + N_QKV
        block = ctx.enter_context(nc.Block())

        def sequencer(eng, s):
            n = [0]

            def o(ins):
                n[0] += 1
                ins.then_inc(s, 1)
                eng.wait_ge(s, n[0])
            return o

        stages, at = {}, 0
        for name, n in (("in", N_IN), ("out", N_OUT), ("up00", N_FF), ("dn00", N_FF), ("up01", N_FF), ("dn01", N_FF),
                        ("qkv", N_QKV), ("ao", N_OUT), ("up10", N_FF), ("dn10", N_FF), ("up11", N_FF), ("dn11", N_FF)):
            stages[name] = (at, n)
            at += n
        assert at == SLOTS

        def unit0(name):
            return 2 * stages[name][0]

        def end_unit(name):
            return 2 * sum(stages[name])

        NORM_UNIT = {1: lambda k: unit0("out") + k + 1, 2: lambda k: unit0("dn01") + 2 * k + 2,
                     3: lambda k: unit0("ao") + k + 1}
        ORDER = [4, 0, 1, 2, 3]

        def levels(t):
            return [2, 4, 8] if t == 4 else [2, 4, 8, 16, 32]

        LEVELS = [3, 5, 5, 5, 5]
        LV_PAIR = sum(LEVELS)
        GH_PAIR = 4 + 2 * 4

        def wa_bank(p, low):
            return 2 * low if p == 0 else 5

        def ln_bank(p):
            return 4 if p == NPAIR - 1 else 5

        def active(l):
            return [i for i in range(5) if LEVELS[i] > l]

        def lvn(p, l, i):
            return p * LV_PAIR + sum(len(active(m)) for m in range(l)) + active(l).index(i)

        @block.sync
        def _(sp):
            for k in range(KT):
                if k == KT - 2:
                    sp.dma_start(PR[:, :], prm).then_inc(params_in, 16)
                    sp.dma_start(CS[:, :], cst).then_inc(params_in, 16)
                sp.dma_start(X[:, k], xT[:, k]).then_inc(x_in[k], 16)
            for n in range(2):
                sp.dma_start(WR[:, n], w[n]).then_inc(w_in[n], 16)
            def load(i):
                for r in range(2):
                    sp.wait_ge(w_split, 4 * i + (2 * r - 2))
                    sp.dma_start(WR[:, r], w[bass.ds(2 * i + r, 1)].rearrange("a p c -> p (a c)")).then_inc(w_in[r], 16)

            with sp.Fori(1, (N_IN + 1) // 2) as i:
                load(i)
            sp.wait_ge(w_split, 2 * N_IN)
            sp.dma_start(WG, wglu).then_inc(glu_w_in, 16)
            for a in range(4):
                sp.wait_ge(g_out, a + 1)
                for t4 in range(4):
                    for j in range(4):
                        dst = UF[32 * j:32 * j + 32, a].rearrange("p (b t) c -> p b t c", t=4)[:, :, t4]
                        src = UR[32 * t4:32 * t4 + 32, j, a].rearrange("p (b c) -> p b c", b=2)
                        sp.dma_start(dst, src).then_inc(y_relayout[a], 16)
            sp.wait_ge(glu_done, 4)
            sp.dma_start(WR[:, 0], w[N_IN + 1]).then_inc(w_in[0], 16)
            sp.wait_ge(w_split, 2 * N_IN + 2)
            sp.dma_start(WR[:, 1], w[N_IN + 2]).then_inc(w_in[1], 16)
            with sp.Fori((N_IN + 3) // 2, SLOTS // 2) as i:
                load(i)
            if SLOTS % 2:
                sp.wait_ge(w_split, 2 * (SLOTS - 2))
                sp.dma_start(WR[:, 0], w[SLOTS - 1]).then_inc(w_in[0], 16)

        @block.gpsimd
        def _(pool):
            def split(r, k, reused):
                pool.wait_ge(w_in[r], 16 * k + 16)
                if reused:
                    pool.wait_ge(unit_done, 4 * k + (2 * r - 2))
                nc.gpsimd.tensor_tensor(WH[:, r].rearrange("p (a c) -> p a c", c=P),
                                        WR[:, r].rearrange("p (a c) -> p a c", c=P),
                                        ONES.unsqueeze(1).broadcast_to((P, SLOT // P, P)), ALU.mult).then_inc(w_split, 1)
                pool.wait_ge(w_split, 4 * k + (2 * r + 1))
                nc.gpsimd.tensor_tensor(WL[:, r], WR[:, r], WH[:, r].bitcast(F32), ALU.subtract).then_inc(w_split, 1)

            o = sequencer(pool, pool_seq)
            gt, M, A, S_ = nc.gpsimd.tensor_tensor, ALU.mult, ALU.add, ALU.subtract

            def mix(tile, dst):
                zp = Z[:, tile, 1 + NP_TOK:ZW].rearrange("p (b t) -> p b t", b=NB)
                ds_ = dst[:, NP_TOK:T].rearrange("p (b t) -> p b t", b=NB)
                gt(dst[:, 0:NP_TOK], Z[:, tile, 0:NP_TOK], Z[:, tile, 1:1 + NP_TOK], S_)
                o(gt(ds_, zp[:, :, 0:ST], zp[:, :, 1:1 + ST], S_))
                o(gt(dst, dst, prm_col("mu", tile).broadcast_to((P, T)), M))
                gt(dst[:, 0:NP_TOK], dst[:, 0:NP_TOK], Z[:, tile, 1:1 + NP_TOK], A)
                return gt(ds_, ds_, zp[:, :, 1:1 + ST], A)

            def s5_samples(j5):
                pr = slice(4 * j5, 4 * j5 + 4)
                pool.wait_ge(xs_evac, 2 * j5 + 2)
                p8 = [PW[:, ri, pr, L5:L5 + 1].broadcast_to((P, 4, NB)) for ri in range(2)]
                t = [TS[:, a_] for a_ in range(4)]
                one = ONES[:, 0:4 * NB].rearrange("p (a b) -> p a b", a=4)
                for ri in range(2):
                    gt(HS[:, ri, :, NCP:NCP + NB], HB[:, ri, 0, pr], one, M)
                for h in range(2):
                    hin = [HB[:, ri, h, pr] for ri in range(2)]
                    gt(t[0], p8[0], hin[0], M)
                    gt(t[1], p8[1], hin[1], M)
                    gt(t[2], p8[0], hin[1], M)
                    o(gt(t[3], p8[1], hin[0], M))
                    gt(t[0], t[0], t[1], S_)
                    o(gt(t[2], t[2], t[3], A))
                    c = slice(NCP + h * NB, NCP + (h + 1) * NB)
                    for ri in range(2):
                        if h == 0:
                            gt(HS[:, ri, :, NCP + NB:NCP + 2 * NB], t[2 * ri], XS[:, ri, :, c], A)
                        last = gt(HB[:, ri, h + 1, pr], t[2 * ri], XS[:, ri, :, c], A)
                    if h == 0:
                        o(last)
                last.then_inc(hs_ready, 1)

            def beta_kappa(p):
                pool.wait_ge(b_ready, p + 1)
                pool.wait_ge(decay_exp, p + 1)
                gt(BETA, TP[:, 3], TP[:, 1], M).then_inc(bk_ready, 1)
                gt(KAPPA(p), RKV[:, 1], TP[:, 1], M).then_inc(bk_ready, 1)

            def masked(a, src):
                return gt(TM3[:, a], src.unsqueeze(1).broadcast_to((P, NB, P)),
                          ROWM.unsqueeze(2).broadcast_to((P, NB, P)), M)

            def rwkv():
                pool.wait_ge(mixed, 2)
                mix(0, RKV[:, 0])
                mix(8, RKV[:, 2]).then_inc(mixed, 1)
                pool.wait_ge(y5_done, 4)
                pool.wait_ge(stored, 16 * 5)
                pool.wait_ge(mixed, 3)
                nc.gpsimd.memset(AR[0:64, :, 1], 0.0).then_inc(rwkv_zeros, 1)
                nc.gpsimd.memset(AR[64:P, :, 0], 0.0).then_inc(rwkv_zeros, 1)
                pool.wait_ge(rwkv_zeros, 2)
                nc.gpsimd.memset(SG[:, 0], 0.0).then_inc(rwkv_zeros, 1)
                beta_kappa(0)
                for p in range(NPAIR):
                    if p + 1 < NPAIR:
                        pool.wait_ge(bonus_ready, p + 1)
                        pool.wait_ge(tr_done, 5 * p + 5)
                        mix(4 + p + 1, RKV[:, 1]).then_inc(mixed, 1)
                        mix(p + 1, RKV[:, 0])
                        mix(8 + p + 1, RKV[:, 2]).then_inc(mixed, 1)
                    if p > 0:
                        pool.wait_ge(ab_out, p)
                    pool.wait_ge(bonus_ready, p + 1)
                    pool.wait_ge(tok_ready, 5 * p + 1)
                    masked(0, TOK[:, 0, 0])
                    masked(2, TOK[:, 0, 2])
                    pool.wait_ge(au_ready, 5 * p + 1)
                    masked(1, AU[:, 0, 1].rearrange("p h k -> p (h k)")).then_inc(um_ready, 1)
                    if p + 1 < NPAIR:
                        beta_kappa(p + 1)

            pool.wait_ge(params_in, 32)
            split(0, 0, False)
            split(1, 0, False)
            with pool.Fori(1, N_IN // 2) as i:
                for r in range(2):
                    split(r, i, True)
            split(0, N_IN // 2, True)
            pool.wait_ge(unit_done, 2 * N_IN)
            nc.gpsimd.memset(CL2[:, 0], 0.0)
            nc.gpsimd.memset(HS[:, :, :, 0:1], 0.0).then_inc(s5_zeros, 1)
            nc.gpsimd.memset(TOE[:, :, :, :], 0.0).then_inc(s5_zeros, 1)
            nc.gpsimd.memset(CL2[:, 1], 0.0).then_inc(s5_zeros, 1)
            for j5 in range(4):
                s5_samples(j5)
            rwkv()
            pool.wait_ge(gh_done, GH_PAIR * NPAIR)
            split(1, N_IN // 2, True)
            with pool.Fori(N_IN // 2 + 1, AO // 2) as i:
                for r in range(2):
                    split(r, i, True)
            for r in range(AO % 2 + 2):
                split(r % 2, AO // 2 + r // 2, True)
            for u in range(UNITS):
                ng, kk = (4, P) if u < 16 else (8, KEYS)
                e = EE[:, u % 2, 0:ng * kk].rearrange("p (g k) -> p g k", g=ng)
                pool.wait_ge(sm_inv, u + 1)
                gt(e, e, SM[:, u % 2, 5, 0:ng].unsqueeze(2).broadcast_to((P, ng, kk)), M).then_inc(sm_p, 1)
            if AO % 2:
                split(1, AO // 2 + 1, True)
            with pool.Fori(AO // 2 + 1 + AO % 2, SLOTS // 2) as i:
                for r in range(2):
                    split(r, i, True)
            if SLOTS % 2:
                split(0, SLOTS // 2, True)

        @block.tensor
        def _(pe):
            mm, tr = nc.tensor.matmul, nc.tensor.transpose

            def norm(L):
                if L == 0:
                    pe.wait_ge(params_in, 32)
                pe.wait_ge(sq_added, (KT - 1) * (L + 1))
                for t in range(5):
                    last = mm(PS[:, 4, t:t + 1], SC[:, 3, t * P:(t + 1) * P], ONES[:, 0:1], start=True, stop=True)
                last.then_inc(norm_sum, 1)
                pe.wait_ge(rms_inv, L + 1)
                for t in range(5):
                    last = mm(PS[:, 4 + t // 4, (t % 4) * P:(t % 4 + 1) * P], SC[:, 2, t * P:(t + 1) * P], IDN,
                              start=True, stop=True)
                last.then_inc(rms_spread, 1)

            def xn_wait(n):
                def wait(k):
                    pe.wait_ge(xn_hi, n * KT + k + 1)
                    pe.wait_ge(xn_lo, n * KT + k + 1)
                return wait

            def slot_as_ready(name, xh, xl, kt, wait, order):
                s0 = stages[name][0]
                pe.wait_ge(w_split, 2 * s0 + 2)
                wh = WH[:, s0 % 2].rearrange("p (k c) -> p k c", k=kt)
                wl = WL[:, s0 % 2].rearrange("p (k c) -> p k c", k=kt)
                if s0 > 0:
                    pe.wait_ge(unit_evac, 2 * s0)
                for n, k in enumerate(order):
                    wait(n)
                    for j in range(2):
                        for h in (range(2) if kt == KT else [j]):
                            out = PS[:, 2 * j + (h if kt == KT else 0), 0:HALF]
                            cols = slice(h * HALF, (h + 1) * HALF)
                            wc = slice(j * P, (j + 1) * P) if kt == KT else slice(0, P)
                            mm(out, wh[:, k, wc], xh[:, k, cols], start=(n == 0), stop=False)
                            mm(out, wh[:, k, wc], xl[:, k, cols], start=False, stop=False)
                            last = mm(out, wl[:, k, wc], xh[:, k, cols], start=False, stop=(n == kt - 1))
                        if n == kt - 1:
                            last.then_inc(unit_done, 1)

            def slot(name, i, u, xh, xl, kt):
                s0 = stages[name][0]
                par = (s0 + u) % 2
                pe.wait_ge(w_split, 2 * i + 2 * (s0 + 1))
                wh = WH[:, par].rearrange("p (k c) -> p k c", k=kt)
                wl = WL[:, par].rearrange("p (k c) -> p k c", k=kt)
                for j in range(2):
                    if not isinstance(i, int) or 2 * (s0 + i) + j > 1:
                        pe.wait_ge(unit_evac, 2 * i + (2 * s0 + j - 1))
                    for h in (range(2) if kt == KT else [j]):
                        out = PS[:, 2 * j + (h if kt == KT else 0), 0:HALF]
                        cols = slice(h * HALF, (h + 1) * HALF)
                        wc = slice(j * P, (j + 1) * P) if kt == KT else slice(0, P)
                        for k in range(kt):
                            mm(out, wh[:, k, wc], xh[:, k, cols], start=(k == 0), stop=False)
                            mm(out, wh[:, k, wc], xl[:, k, cols], start=False, stop=False)
                            last = mm(out, wl[:, k, wc], xh[:, k, cols], start=False, stop=(k == kt - 1))
                    last.then_inc(unit_done, 1)

            def stage(name, xh, xl, kt, wait=None, order=None):
                if wait:
                    slot_as_ready(name, xh, xl, kt, wait, order or range(kt))
                    slot(name, 1, 1, xh, xl, kt)
                with pe.Fori(1 if wait else 0, stages[name][1] // 2) as i:
                    for u in range(2):
                        slot(name, 2 * i + u, u, xh, xl, kt)

            def s5_front(j5):
                pe.wait_ge(m1t_ready, j5 + 1)
                for i in range(4):
                    ri, t2 = i // 2, i % 2
                    if i < 2 and j5 > 0:
                        pe.wait_ge(xs_evac, 2 * j5)
                    if i >= 2:
                        pe.wait_ge(m1_ready, 4 * j5 + i - 1)
                    for j in range(4):
                        last = tr(PS[:, 4 + t2, j * P:(j + 1) * P],
                                  M1T[:, ri, j, 4 * t2:4 * t2 + 4, :].rearrange("p a b -> p (a b)"), IDN)
                    last.then_inc(m1_transposed, 1)
                if j5 == 0:
                    pe.wait_ge(u_relayout, 16 * 16)
                pe.wait_ge(m1_ready, 4 * j5 + 4)
                for ri in range(2):
                    for j in range(4):
                        for t2 in range(2):
                            last = mm(PS[:, 4 + ri, j * NC5:(j + 1) * NC5], M1[:, ri, t2, j],
                                      UR[:, j, j5, t2 * NC5:(t2 + 1) * NC5], start=(t2 == 0), stop=(t2 == 1))
                    last.then_inc(xs_done, 1)

            def s5_toeplitz(j5):
                CL = CL2[:, j5 % 2]
                pe.wait_ge(cl_ready, j5 + 1)
                if j5 > 0:
                    pe.wait_ge(y5_sum, j5)
                for j in range(4):
                    for ri in range(2):
                        mm(PS[:, 6, j * P:(j + 1) * P], M1T[:, ri, j, 4:8, :].rearrange("p a b -> p (a b)"),
                           CL[:, ri, j, 1:5, :].rearrange("p a b -> p (a b)"), start=(ri == 0), stop=(ri == 1))
                    for s in range(4):
                        for ri in range(2):
                            last = mm(PS[32 * s:32 * s + 32, 7, j * P + 32 * s:(j + 1) * P], M1T[:, ri, j, 7, :],
                                      CL[:, ri, j, 0:4 - s, :].rearrange("p a b -> p (a b)"),
                                      start=(ri == 0), stop=(ri == 1))
                last.then_inc(toe_done, 1)

            def s5_y(j5):
                CL = CL2[:, j5 % 2]
                pe.wait_ge(toe_ready, j5 + 1)
                pe.wait_ge(hs_ready, 2 * (j5 + 1))
                for j in range(4):
                    at = (j % 2) * 2 * NC5
                    mm(PS[:, 6 + j // 2, at:at + 2 * NC5], TOE[:, 1, j], UR[:, j, j5, :], start=True, stop=False)
                    mm(PS[:, 6 + j // 2, at + NC5:at + 2 * NC5], TOE[:, 0, j], UR[:, j, j5, 0:NC5], start=False, stop=False)
                    for t2 in range(2):
                        for ri in range(2):
                            last = mm(PS[:, 6 + j // 2, at + t2 * NC5:at + (t2 + 1) * NC5],
                                      CL[:, ri, j, 1 + 4 * t2:5 + 4 * t2, :].rearrange("p a b -> p (a b)"),
                                      HS[:, ri, j, :], start=False, stop=(t2 == 1 and ri == 1))
                last.then_inc(y5_done, 1)

            def glu(j, ks):
                if ks[0] == 0 and j > 0:
                    pe.wait_ge(ab_out, j)
                if j == 0:
                    pe.wait_ge(glu_w_in, 16)
                for k in ks:
                    if j == 0:
                        pe.wait_ge(y_relayout[k], 16 * 16)
                    for h in range(2):
                        last = mm(PS[:, 6 + h, 0:HALF], WG[:, k, j * P:(j + 1) * P],
                                  UF[:, k, 4 * h:4 * h + 4, :].rearrange("p t c -> p (t c)"),
                                  start=(k == 0), stop=(k == 3))
                if 3 in ks:
                    last.then_inc(glu_done, 1)

            def s5():
                s5_front(0)
                s5_toeplitz(0)
                for j5 in range(4):
                    s5_y(j5)
                    if j5 + 1 < 4:
                        s5_front(j5 + 1)
                        s5_toeplitz(j5 + 1)

            def halves(bank, a, x):
                for h in range(2):
                    last = mm(PS[:, bank + h, 0:HALF], a, x[:, h * HALF:(h + 1) * HALF], start=True, stop=True)
                return last

            def wa(p, low):
                if p == 0 and low == 0:
                    pe.wait_ge(lora_act, 2)
                    pe.wait_ge(lora_w_in, 16)
                if p > 1 and low == 0:
                    pe.wait_ge(ab_out, p - 1)
                if p > 0 and low == 1:
                    pe.wait_ge(wa_act, 2 * p + 1)
                r = slice(64 * low, 64 * low + 64)
                halves(wa_bank(p, low), W2[r, p * P:(p + 1) * P], TL[r, 0]).then_inc(wa_done, 1)

            def kk(p):
                pe.wait_ge(kk_sq, p + 1)
                pe.wait_ge(wa_act, 2 * p + 2)
                for t in range(5):
                    last = mm(PS[:, 5, 2 * t:2 * t + 2], TP[:, 4, t * P:(t + 1) * P], BD[:, 0:P:64], start=True, stop=True)
                last.then_inc(kk_sum, 1)

            def kk_back(p):
                pe.wait_ge(kk_inv, p + 1)
                for t in range(5):
                    last = mm(PS[:, t // 4, (t % 4) * P:(t % 4 + 1) * P], TP[:, 4, t * P:(t + 1) * P], IDN,
                              start=True, stop=True)
                last.then_inc(kk_spread, 1)

            def ln_squares(p):
                pe.wait_ge(ln_sq, p + 1)
                for t in range(5):
                    last = mm(PS[:, ln_bank(p), 2 * t:2 * t + 2], TP[:, 2, t * P:(t + 1) * P], BD[:, 0:P:64],
                              start=True, stop=True)
                last.then_inc(ln_sum, 1)

            def ln_back(p):
                pe.wait_ge(ln_inv, p + 1)
                for t in range(5):
                    last = mm(PS[:, ln_bank(p) + t // 4, (t % 4) * P:(t % 4 + 1) * P], TP[:, 3, t * P:(t + 1) * P], IDN,
                              start=True, stop=True)
                last.then_inc(ln_spread, 1)

            def gate(p):
                pe.wait_ge(ln_scaled, p + 1)
                pe.wait_ge(g2_in, 16)
                halves(ln_bank(p), G2[:, p * P:(p + 1) * P], TL[:, 1]).then_inc(ln_sum, 1)

            def bonus(p):
                pe.wait_ge(bonus_in, p + 1)
                halves(2, BD, BO[p % 2]).then_inc(bonus_sum, 1)

            def chain(p, c):
                if c == 0:
                    pe.wait_ge(gh_ready, 5 * p + 5)
                    pe.wait_ge(kk_norm, min(p + 2, NPAIR))
                pe.wait_ge(st_ready, p * (NCH + 1) + 1 + c)
                mm(PS[:, (5, 4)[c % 2], 0:P], GH[:, 0, c], SG[:, c], start=True, stop=True).then_inc(st_done, 1)

            def outputs(p):
                pe.wait_ge(st_ready, (p + 1) * (NCH + 1))
                for c in range(NCH):
                    mm(PS[:, 4 + c // 5, (c % 5) * CH:(c % 5 + 1) * CH], SG[:, c], RT(p)[:, c * CH:(c + 1) * CH],
                       start=True, stop=True)
                for s in range(NB):
                    a = NP_TOK + s * ST
                    last = mm(PS[:, 5, a - HALF:a - HALF + ST], S0[:, s], RT(p)[:, a:a + ST], start=True, stop=True)
                last.then_inc(oo_done, 1)

            def tile_au(p, i):
                pe.wait_ge(tt_ready, lvn(p, LEVELS[i] - 1, i) + 1)
                for hh in range(2):
                    last = mm(PS[:, i, hh * P:(hh + 1) * P], TT[:, i, 1, hh], AW[:, i, hh].rearrange("p a k -> p (a k)"),
                              start=True, stop=True)
                last.then_inc(au_done, 1)

            def tile_ro(p, i):
                pe.wait_ge(au_ready, 5 * p + i + 1)
                for hh in range(2):
                    r = slice(64 * hh, 64 * hh + 64)
                    mm(PS[r, i, 0:P], AU[:, i, 0, hh], GM[:, i, hh, 1], start=True, stop=True)
                    mm(PS[r, i, P:2 * P], AU[:, i, 1, hh], GM[:, i, hh, 1], start=True, stop=False)
                    last = mm(PS[r, i, P:2 * P], TOK[:, i, 2, 64 * hh:64 * hh + 64], GM[:, i, hh, 3],
                              start=False, stop=True)
                last.then_inc(ro_done, 1)

            def level(p, l):
                for i in active(l):
                    pe.wait_ge(*((tt_first, 5 * p + i + 1) if l == 0 else (tt_ready, lvn(p, l - 1, i) + 1)))
                    for hh in range(2):
                        last = mm(PS[:, i, hh * P:(hh + 1) * P], GM[:, i, hh, 0], TT[:, i, 0, hh], start=True, stop=True)
                    last.then_inc(lx_done, 1)
                for i in active(l):
                    pe.wait_ge(xm_ready, lvn(p, l, i) + 1)
                    for hh in range(2):
                        if l + 1 < LEVELS[i]:
                            mm(PS[:, i, hh * P:(hh + 1) * P], TT[:, i, 1, hh], XM[:, i, hh], start=True, stop=True)
                        last = mm(PS[:, i, 256 + hh * P:256 + (hh + 1) * P], XM[:, i, hh], TT[:, i, 1, hh],
                                  start=True, stop=True)
                    last.then_inc(lt_done, 1)

            def tiles(p):
                pe.wait_ge(bk_ready, 2 * (p + 1))
                pe.wait_ge(feat_ready, p + 1)
                for i, t in enumerate(ORDER):
                    cols = slice(t * P, (t + 1) * P)
                    if i == 2:
                        pe.wait_ge(bonus_ready, p + 1)
                    if i == 4 and p > 0:
                        pe.wait_ge(o_ready, p)
                    tr(PS[:, i, 0:P], BETA[:, cols], IDN)
                    tr(PS[:, i, P:2 * P], KAPPA(p)[:, cols], IDN)
                    tr(PS[:, i, 2 * P:3 * P], RKV[:, 2, cols], IDN)
                    for hh in range(2):
                        last = mm(PS[:, i, 3 * P + 64 * hh:3 * P + 64 * hh + 64], AR[:, t, hh, 0],
                                  IDN[:, 64 * hh:64 * hh + 64], start=True, stop=True)
                    last.then_inc(tr_done, 1)
                if p > 0:
                    pe.wait_ge(glu_tanh, p)
                    halves(5, BD, TP[:, 2]).then_inc(ln_sum, 1)
                for hh in range(2):
                    for i, t in enumerate(ORDER):
                        cols = slice(t * P, (t + 1) * P)
                        if hh == 0:
                            pe.wait_ge(tok_ready, 5 * p + i + 1)
                        else:
                            pe.wait_ge(gm_ready, 10 * p + i + 1)
                        ar = AR[:, t, hh].rearrange("p a t -> p (a t)")
                        mm(PS[:, i, 0:2 * P], BETA[:, cols], ar, start=True, stop=True)
                        mm(PS[:, i, 2 * P:4 * P], KAPPA(p)[:, cols], ar, start=True, stop=True).then_inc(gram_done, 1)
                if p > 0:
                    ln_squares(p - 1)
                for i, t in enumerate(ORDER):
                    cols = slice(t * P, (t + 1) * P)
                    pe.wait_ge(gm_ready, 10 * p + 5 + i + 1)
                    for hh in range(2):
                        mm(PS[:, i, hh * P:(hh + 1) * P], AR[:, t, hh, 0], BETA[:, cols], start=True, stop=True)
                        last = mm(PS[:, i, 256 + hh * 64:256 + hh * 64 + 64], GM[:, i, hh, 2],
                                  TOK[:, i, 2, 64 * hh:64 * hh + 64], start=True, stop=True)
                    last.then_inc(lv_done, 1)
                level(p, 0)
                if p > 0:
                    ln_back(p - 1)
                level(p, 1)
                if p > 0:
                    gate(p - 1)
                level(p, 2)
                tile_au(p, 0)
                level(p, 3)
                tile_ro(p, 0)
                level(p, 4)
                pe.wait_ge(um_ready, p + 1)
                At = [AU[:, i, 0].rearrange("p h k -> p (h k)") for i in range(5)]
                Ut = [AU[:, i, 1].rearrange("p h k -> p (h k)") for i in range(5)]
                masked = [[TM3[:, a, 4 * h:4 * h + 4].rearrange("p b k -> p (b k)") for a in range(3)] for h in range(2)]
                mm(PS[:, 7, :], At[0], masked[0][0], start=True, stop=True).then_inc(gh_done, 1)
                pe.wait_ge(rt_ready, 5 * p + 1)
                pe.wait_ge(o0_ready, 5 * p + 1)
                mm(PS[:, 0, :], At[0], masked[1][0], start=True, stop=True).then_inc(gh_done, 1)
                for i in range(1, 5):
                    tile_au(p, i)
                for h in range(2):
                    pe.wait_ge(ghs_ready, 4 * p + h + 1)
                    mm(PS[:, (7, 0)[h], :], TOK[:, 0, 0], masked[h][1], start=True, stop=False)
                    mm(PS[:, (7, 0)[h], :], TOK[:, 0, 1], masked[h][2], start=False, stop=True).then_inc(gh_done, 1)
                for i in range(1, 5):
                    tile_ro(p, i)
                if p + 1 < NPAIR:
                    wa(p + 1, 0)
                pe.wait_ge(s0_in, 16 * (p + 1))
                for s in range(NB):
                    if s % 4 == 0:
                        pe.wait_ge(ghs_ready, 4 * p + 2 + s // 4 + 1)
                    last = mm(PS[:, (7, 0)[s // 4], (s % 4) * P:(s % 4 + 1) * P], GH[:, 0, s], S0[:, s],
                              start=True, stop=True)
                last.then_inc(st_done, 1)
                for c in range(2):
                    r, at = slice(64 * c, 64 * c + 64), 256 * c
                    for i in range(1, 5):
                        if c == 0:
                            pe.wait_ge(rt_ready, 5 * p + i + 1)
                            pe.wait_ge(o0_ready, 5 * p + i + 1)
                        else:
                            pe.wait_ge(gh_done, GH_PAIR * p + 4 + i)
                        mm(PS[:, i, at:at + P], At[i][r], TOK[r, i, 0], start=True, stop=True)
                        mm(PS[:, i, at + P:at + 2 * P], TOK[r, i, 0], Ut[i][r], start=True, stop=False)
                        mm(PS[:, i, at + P:at + 2 * P], TOK[r, i, 1], TOK[r, i, 2], start=False,
                           stop=True).then_inc(gh_done, 1)
                    if p + 1 < NPAIR:
                        if c == 0:
                            wa(p + 1, 1)
                        else:
                            kk(p + 1)

            def rwkv():
                wa(0, 0)
                wa(0, 1)
                kk(0)
                kk_back(0)
                bonus(0)
                for p in range(NPAIR):
                    tiles(p)
                    pe.wait_ge(gh_ready, 5 * p + 1)
                    glu(p, (0, 1))
                    for c in range(NCH):
                        chain(p, c)
                        if c == 1 and p + 1 < NPAIR:
                            kk_back(p + 1)
                    outputs(p)
                    glu(p, (2, 3))
                    if p + 1 < NPAIR:
                        bonus(p + 1)
                pe.wait_ge(o_ready, NPAIR)
                halves(4, BD, TP[:, 2]).then_inc(ln_sum, 1)

            def qk_sums(m):
                pe.wait_ge(qk_sq, m + 1)
                if m >= 2:
                    pe.wait_ge(qk_rms, m - 1)
                halves(4 + 2 * (m % 2), BD, SC[:, m % 2]).then_inc(qk_sum, 1)

            def qkv():
                slot_as_ready("qkv", XH, XL, KT, xn_wait(3), range(KT))
                for i in range(1, N_QKV):
                    slot("qkv", i, i, XH, XL, KT)
                    if i in (1, 2, 3, 4):
                        qk_sums(2 * i - 2)
                        qk_sums(2 * i - 1)
                pe.wait_ge(v_pad, 1)
                pe.wait_ge(unit_evac, unit0("qkv") + 10)
                pe.wait_ge(qk_rms, 8)
                for n in range(NCH + NB):
                    if n >= 4:
                        pe.wait_ge(vw_ready, n - 3)
                    for i in range(2):
                        if n < NCH:
                            last = tr(PS[:, 4 + n % 4, i * P:(i + 1) * P], VP[:, i, n * CH:n * CH + P], IDN)
                        else:
                            a = CH + NP_TOK + (n - NCH) * ST
                            last = tr(PS[0:ST, 4 + n % 4, i * P:(i + 1) * P], VP[:, i, a:a + ST], IDN)
                    last.then_inc(vw_tr, 1)
                pe.wait_ge(vw_ready, NCH + NB)
                pe.wait_ge(qk_sq, 10)
                for m in range(2):
                    for t in range(5):
                        at = 10 * m + 2 * t
                        last = mm(PS[:, 4, at:at + 2], SC[:, m, t * P:(t + 1) * P], BD[:, 0:P:64], start=True, stop=True)
                last.then_inc(qk_sum, 1)

            def qk_back():
                pe.wait_ge(qk_inv, 1)
                for m in range(2):
                    for t in range(5):
                        last = mm(PS[:, 4 + 2 * m + t // 4, (t % 4) * P:(t % 4 + 1) * P], SC[:, 2 + m, t * P:(t + 1) * P],
                                  IDN, start=True, stop=True)
                    last.then_inc(qk_spread, 1)

            def scores(u):
                b0 = (0, 4)[u % 2]
                if u == 0:
                    pe.wait_ge(unit_evac, end_unit("qkv"))
                    pe.wait_ge(kd_ready, 1)
                elif u == 1:
                    pe.wait_ge(qk_ready, 10)
                else:
                    pe.wait_ge(sm_sub, u - 1)
                if u < 16:
                    t, kv = u % 4, u // 4
                    pe.wait_ge(qk_ready, 2 * kv + 4)
                    for c in range(2):
                        n = 2 * t + c
                        for g in range(4):
                            half, t2 = g % 2, g // 2
                            r = slice(64 * half, 64 * half + 64)
                            q = Q[r, 2 * kv + t2, n * CH:(n + 1) * CH]
                            if n == 0:
                                last = mm(PS[0:64, b0 + half, t2 * P + 64:t2 * P + P], q, KD[r, kv, 0:CH],
                                          start=True, stop=True)
                            else:
                                last = mm(PS[64 * c:64 * c + 64, b0 + half, t2 * P:(t2 + 1) * P], q,
                                          KD[r, kv, (n - 1) * CH:(n + 1) * CH], start=True, stop=True)
                else:
                    if u == 16:
                        pe.wait_ge(qs_ready, 1)
                        pe.wait_ge(cache_in, 32)
                    for half in range(2):
                        r = slice(64 * half, 64 * half + 64)
                        for b4 in range(4):
                            sq = 4 * (u - 16) + b4
                            for kv in range(4):
                                last = mm(PS[32 * kv:32 * kv + 32, b0 + half, b4 * KEYS:(b4 + 1) * KEYS],
                                          QS[r, kv, sq], KS[r, kv, sq], start=True, stop=True)
                last.then_inc(sc_done, 1)

            def transposes(u):
                pe.wait_ge(sm_p, u + 1)
                if u < 16:
                    if u >= 2:
                        pe.wait_ge(pt_ready, u - 1)
                    for g in range(4):
                        last = tr(PS[:, (2, 6)[u % 2], g * P:(g + 1) * P], EE[:, u % 2, g * P:(g + 1) * P], IDN)
                else:
                    pe.wait_ge(pt_ready, u)
                    for g in range(8):
                        last = tr(PS[0:KEYS, (2, 6)[g // 4], (g % 4) * P:(g % 4 + 1) * P],
                                  EE[:, u % 2, g * KEYS:(g + 1) * KEYS], IDN)
                last.then_inc(pt_tr, 1)

            def values(u):
                bank = (3, 7)[u % 2]
                pe.wait_ge(pt_ready, u + 1)
                if u >= 2:
                    pe.wait_ge(o_lo, u - 1)
                if u < 16:
                    t, kv = u % 4, u // 4
                    for c in range(2):
                        for half in range(2):
                            out = PS[64 * half:64 * half + 64, bank, 0:256].rearrange("p (a c q) -> p a c q", a=2, c=2)
                            g = 4 * (u % 2) + 2 * half
                            last = mm(out[:, :, c], VW[:, 2 * t + c, kv * 64:kv * 64 + 64],
                                      PT[:, g:g + 2, c * 64:c * 64 + 64], start=True, stop=True)
                else:
                    for b4 in range(4):
                        for half in range(2):
                            out = PS[64 * half:64 * half + 64, bank, :].rearrange("p (a b q) -> p a b q", a=8, b=4)
                            for kv in range(4):
                                last = mm(out[:, 2 * kv:2 * kv + 2, b4], VS[0:KEYS, 4 * (u - 16) + b4, kv * 64:kv * 64 + 64],
                                          PT[0:KEYS, half * 4 + b4, 32 * kv:32 * kv + 32], start=True, stop=True)
                last.then_inc(pv_done, 1)

            def attention():
                scores(0)
                qk_back()
                for i in range(UNITS + 2):
                    if i + 1 < UNITS:
                        scores(i + 1)
                    if i >= 2:
                        values(i - 2)
                    if 0 <= i - 1 < UNITS:
                        transposes(i - 1)

            def mlp(l, n):
                stage(f"up{l}0", XH, XL, KT, xn_wait(n))
                for hf in range(2):
                    if hf:
                        stage(f"up{l}1", XH, XL, KT)
                    b = FF_TILES * (2 * l + hf)

                    def h_wait(k):
                        pe.wait_ge(h_hi, b + k + 1)
                        pe.wait_ge(h_lo, b + k + 1)
                    stage(f"dn{l}{hf}", HH, HL, FF_TILES, h_wait)

            norm(0)
            slot_as_ready("in", XH, XL, KT, xn_wait(0), range(KT))
            for i in range(1, N_IN):
                slot("in", i, i, XH, XL, KT)
            s5()
            rwkv()

            def ab_wait(n):
                if n in (1, 3, 5):
                    {1: ln_squares, 3: ln_back, 5: gate}[n](NPAIR - 1)
                xn_wait(1)(n)
            stage("out", XH, XL, KT, ab_wait, AB_ORDER)
            norm(1)
            mlp(0, 2)
            norm(2)
            qkv()
            attention()

            def o_wait(k):
                if k == 0:
                    pe.wait_ge(o_lo, 18)
            stage("ao", XH, XL, KT, o_wait)
            norm(3)
            mlp(1, 4)

        @block.scalar
        def _(act):
            o = sequencer(act, act_seq)
            fn = nc.scalar.activation

            def halves(bank):
                return PS[:, bank:bank + 2, 0:HALF]

            def h2(ap):
                return ap.rearrange("p (h t) -> p h t", h=2)

            def norm(L, n):
                for k in range(KT):
                    if L == 0:
                        act.wait_ge(x_in[k], 16)
                    else:
                        act.wait_ge(unit_evac, NORM_UNIT[L](k))
                    if k >= 2:
                        act.wait_ge(sq_added, (KT - 1) * L + max(1, k - 2))
                    fn(SC[:, k % 2], X[:, k], ACT.Square).then_inc(sq_ready, 1)
                act.wait_ge(norm_sum, L + 1)
                if L == 0:
                    act.wait_ge(params_in, 32)
                fn(KN[:, 0:5], PS[:, 4, 0:5], ACT.Sqrt, bias=prm_col("eps"), scale=1.0 / D).then_inc(rms_ready, 1)
                for k in range(KT):
                    act.wait_ge(xn_t, L * KT + k + 1)
                    fn(XH[:, k], SC[:, (3, 0)[k % 2]], ACT.Copy).then_inc(xn_hi, 1)

            def evac_in():
                for n in range(N_IN):
                    for j in range(2):
                        act.wait_ge(unit_done, 2 * n + j + 1)
                        tile = IN_TILES[2 * n + j]
                        ps = [PS[:, 2 * j, 0:HALF], PS[:, 2 * j + 1, 0:HALF]]
                        if tile < A_TILES:
                            fn(Z[:, tile, 1:1 + HALF], ps[0], ACT.Copy)
                            fn(Z[:, tile, 1 + HALF:1 + NP_TOK], ps[1][:, 0:NP_TOK - HALF], ACT.Copy)
                            zs = Z[:, tile, 1 + NP_TOK:ZW].rearrange("p (b t) -> p b t", b=NB)
                            last = fn(zs[:, :, 1:1 + ST], ps[1][:, NP_TOK - HALF:HALF].rearrange("p (b t) -> p b t", b=NB),
                                      ACT.Copy)
                        else:
                            uf = UF[:, tile - A_TILES]
                            c0 = HALF // L5
                            fn(uf[:, :, 0:c0], ps[0].rearrange("p (c t) -> p t c", t=L5), ACT.Copy)
                            fn(uf[:, :, c0:NCP], ps[1][:, 0:NP_TOK - HALF].rearrange("p (c t) -> p t c", t=L5), ACT.Copy)
                            us = ps[1][:, NP_TOK - HALF:HALF].rearrange("p (b h t) -> p h t b", h=2, t=L5)
                            for h in range(2):
                                last = fn(uf[:, :, NCP + h * NB:NCP + (h + 1) * NB], us[:, h], ACT.Copy)
                        last.then_inc(unit_evac, 1)
                    if n == 0:
                        s5_scalars()
                    if n == 2:
                        act.wait_ge(unit_evac, 6)
                        for t4 in range(4):
                            for j in range(4):
                                src = UF[32 * j:32 * j + 32].rearrange("p a (b t) c -> p a b t c", t=4)[:, :, :, t4]
                                dst = UR[32 * t4:32 * t4 + 32, j].rearrange("p a (b c) -> p a b c", b=2)
                                act.dma_start(dst, src).then_inc(u_relayout, 16)

            def s5_scalars():
                act.wait_ge(params_in, 32)
                fn(S5[:, 0], prm_cols("ldt"), ACT.Exp).then_inc(s5_fn, 1)
                act.wait_ge(s5_arg, 1)
                fn(S5[:, 4], S5[:, 2], ACT.Exp)
                fn(S5[:, 10], S5[:, 2], ACT.Exp, scale=float(L5))
                fn(S5[:, 8], S5[:, 6], ACT.Sin)
                fn(S5[:, 9], S5[:, 7], ACT.Sin, bias=prm_col("halfpi"), scale=-1.0).then_inc(s5_fn, 1)

            def s5_front(j5):
                for i in range(4):
                    ri, t2 = i // 2, i % 2
                    act.wait_ge(m1_transposed, 4 * j5 + i + 1)
                    if j5 > 0:
                        act.wait_ge(xs_done, 2 * j5)
                    fn(M1[:, ri, t2].rearrange("p j c -> p (j c)"), PS[:, 4 + t2, :], ACT.Copy).then_inc(m1_ready, 1)
                for ri in range(2):
                    act.wait_ge(xs_done, 2 * j5 + ri + 1)
                    if j5 > 0:
                        act.wait_ge(hs_ready, 2 * j5)
                    fn(XS[:, ri].rearrange("p j c -> p (j c)"), PS[:, 4 + ri, 0:4 * NC5], ACT.Copy).then_inc(xs_evac, 1)

            def s5_toeplitz(j5):
                act.wait_ge(toe_done, j5 + 1)
                if j5 == 0:
                    act.wait_ge(s5_zeros, 2)
                fn(TOE[:, 0].rearrange("p j c -> p (j c)"), PS[:, 6, :], ACT.Copy)
                for s in range(4):
                    r = slice(32 * s, 32 * s + 32)
                    last = fn(TOE[r, 1, :, 32 * s:P], PS[r, 7, :].rearrange("p (j c) -> p j c", j=4)[:, :, 32 * s:P], ACT.Copy)
                last.then_inc(toe_ready, 1)

            def gelu_square(j5):
                act.wait_ge(y5_sum, j5 + 1)
                fn(GQ, UR[:, :, j5], ACT.Square).then_inc(g_sq, 1)

            def gelu_tanh(j5):
                act.wait_ge(g_arg, j5 + 1)
                fn(GT[:, :, :], GQ, ACT.Tanh, scale=GELU_C).then_inc(g_tanh, 1)

            def low_ranks():
                act.wait_ge(mixed, 1)
                fn(TL[0:64, 0], TL[0:64, 0], ACT.Tanh).then_inc(lora_act, 1)
                o(fn(TL[:, 1], TL[:, 1], ACT.Tanh, scale=0.5))
                fn(TL[:, 1], TL[:, 1], ACT.Copy, bias=0.5, scale=0.5).then_inc(lora_act, 1)

            def s5():
                act.wait_ge(unit_evac, 2 * N_IN)
                act.dma_start(W2[:, :], w2a2).then_inc(lora_w_in, 16)
                s5_front(0)
                s5_toeplitz(0)
                for j5 in range(4):
                    if j5 + 1 < 4:
                        s5_front(j5 + 1)
                    else:
                        act.wait_ge(hs_ready, 8)
                        act.dma_start(o_s5p, HE[:, :, :]).then_inc(stored, 16)
                        act.dma_start(o_s5s, HB[:, :, 2]).then_inc(stored, 16)
                        act.wait_ge(zl_ready, 1)
                        act.dma_start(o_shift, ZL[:, :, :]).then_inc(stored, 16)
                        low_ranks()
                        squares(0)
                    gelu_square(j5)
                    if j5 == 3:
                        low_rank(0, 0)
                        low_rank(0, 1)
                    if j5 + 1 < 4:
                        s5_toeplitz(j5 + 1)
                    gelu_tanh(j5)

            def glu(j):
                act.wait_ge(glu_done, j + 1)
                fn(h2(GO[j]), halves(6), ACT.Tanh, scale=0.25).then_inc(glu_tanh, 1)

            def squares(p):
                act.wait_ge(mixed, 2 * p + 2)
                if p == 0:
                    act.wait_ge(stored, 16 * 5)
                else:
                    act.wait_ge(gh_done, GH_PAIR * (p - 1) + 4)
                fn(TP[:, 4], RKV[:, 1], ACT.Square, scale=prm_col("k_k", p)).then_inc(kk_sq, 1)

            def low_rank(p, low):
                act.wait_ge(wa_done, 2 * p + low + 1)
                fn(h2(TP[:, 2 + low]), halves(wa_bank(p, low)), ACT.Tanh, bias=HP[:, 4 * low + p:4 * low + p + 1],
                   scale=0.5).then_inc(wa_act, 1)

            def kk_root(p):
                act.wait_ge(kk_sum, p + 1)
                fn(KN[:, 0:10], PS[:, 5, 0:10], ACT.Sqrt).then_inc(kk_norm, 1)

            def decays(p):
                act.wait_ge(cs_ready, p + 1)
                fn(TP[:, 0], TP[:, 0], ACT.Exp)
                o(fn(TP[:, 2], TP[:, 1], ACT.Exp))
                fn(TP[:, 1], TP[:, 1], ACT.Exp, scale=-1.0).then_inc(decay_exp, 1)

            def tile_au(p, i):
                act.wait_ge(au_done, 5 * p + i + 1)
                fn(AU[:, i].rearrange("p a h k -> p h a k"), PS[:, i, 0:2 * P].rearrange("p (h a k) -> p h a k", h=2, a=2),
                   ACT.Copy).then_inc(au_ready, 1)

            def tile_o0(p, i):
                t = ORDER[i]
                act.wait_ge(rt_ready, 5 * p + i + 1)
                fn(O0[:, t * P:(t + 1) * P], PS[:, i, P:2 * P], ACT.Copy).then_inc(o0_ready, 1)

            def finish_sq(p):
                act.wait_ge(oc_ready, p + 1)
                fn(TP[:, 2], TP[:, 1], ACT.Square).then_inc(ln_sq, 1)

            def finish_sd(p):
                act.wait_ge(ln_sum, 3 * p + 2)
                fn(KN[:, 0:10], PS[:, ln_bank(p), 0:10], ACT.Sqrt, bias=prm_col("eps_ln"), scale=1.0 / 64).then_inc(ln_sd, 1)

            def tiles(p):
                if p > 0:
                    act.wait_ge(oo_done, p)
                act.dma_start(S0[:, :, :], s0[p]).then_inc(s0_in, 16)
                if p == 0:
                    for a in range(4):
                        act.wait_ge(y_relayout[a], 16 * 16)
                    act.dma_start(G2[:, :], g2).then_inc(g2_in, 16)
                for i in range(5):
                    act.wait_ge(tr_done, 5 * p + i + 1)
                    fn(AW[:, i, :, 0], PS[:, i, 3 * P:4 * P].rearrange("p (h k) -> p h k", h=2), ACT.Copy)
                    fn(TOK[:, i].rearrange("p a c -> p (a c)"), PS[:, i, 0:3 * P], ACT.Copy).then_inc(tok_ready, 1)
                if p > 0:
                    finish_sq(p - 1)
                    finish_sd(p - 1)
                tile_au(p, 0)
                tile_o0(p, 0)
                for i in range(1, 5):
                    tile_au(p, i)
                if p + 1 < NPAIR:
                    squares(p + 1)
                tile_o0(p, 1)
                if p + 1 < NPAIR:
                    low_rank(p + 1, 0)
                for i in range(2, 5):
                    tile_o0(p, i)
                act.wait_ge(st_ready, p * (NCH + 1) + 1)
                act.dma_start(o_srw[p], TM3[:, 0]).then_inc(srw_stored, 16)
                if p + 1 < NPAIR:
                    low_rank(p + 1, 1)
                    kk_root(p + 1)

            def rwkv():
                kk_root(0)
                decays(0)
                for p in range(NPAIR):
                    tiles(p)
                    if p + 1 < NPAIR:
                        decays(p + 1)
                        glu(p)
                    act.wait_ge(st_ready, (p + 1) * (NCH + 1))
                    act.dma_start(o_prw[p], SG[:, NCH]).then_inc(prw_stored, 16)
                act.wait_ge(srw_stored, 16 * NPAIR)
                act.wait_ge(prw_stored, 16 * NPAIR)
                act.wait_ge(oo_done, NPAIR)
                for k in (4, 5, 6, 0, 1):
                    ab_high(k)
                glu(NPAIR - 1)
                finish_sq(NPAIR - 1)
                ab_high(2)
                ab_high(7)
                finish_sd(NPAIR - 1)
                ab_high(3)

            def ab_high(k):
                if k < 4:
                    act.wait_ge(ab_out, k + 1)
                    fn(XH[:, k], Z[:, k, 0:T], ACT.Copy).then_inc(xn_hi, 1)
                else:
                    act.wait_ge(glu_out, k - 3)
                    fn(prompt_cols(XH[:, k]), GO5[k - 4][:, :, 0:NCP], ACT.Copy, scale=0.25)
                    for h in range(2):
                        last = fn(sample_cols(XH[:, k], h), GO5[k - 4][:, :, NCP + h * NB:NCP + (h + 1) * NB], ACT.Copy,
                                  scale=0.25)
                    last.then_inc(xn_hi, 1)

            def hidden(name, hidx):
                u0, b = unit0(name), FF_TILES * hidx
                if hidx % 2 == 1:
                    act.wait_ge(unit_done, u0)
                act.wait_ge(unit_evac, u0)
                with act.Fori(0, FF_TILES // 2) as i:
                    for j in range(2):
                        act.wait_ge(unit_done, 2 * i + (u0 + j + 1))
                        fn(h2(SC[:, j]), halves(2 * j), ACT.Relu).then_inc(unit_evac, 1)
                        act.wait_ge(h_sq, 2 * i + (b + j + 1))
                        fn(HH[:, bass.ds(2 * i + j, 1)].rearrange("p a t -> p (a t)"), SC[:, 2 + j], ACT.Copy).then_inc(h_hi, 1)

            def qkv():
                u0 = unit0("qkv")
                act.wait_ge(unit_done, u0)
                act.dma_start(KS[:, :, :, 0:CH], ckT).then_inc(cache_in, 16)
                act.dma_start(VS[0:CH, :, :], cv).then_inc(cache_in, 16)
                act.wait_ge(unit_evac, u0)

                def rms(m):
                    act.wait_ge(qk_sum, m + 1)
                    if m >= 2:
                        act.wait_ge(qk_ready, m - 1)
                    fn(h2(SC[:, 2 + m % 2]), halves(4 + 2 * (m % 2)), ACT.Sqrt, bias=prm_col("eps"),
                       scale=1.0 / 64).then_inc(qk_rms, 1)

                def square(m):
                    t = NORM_TILES[m]
                    if m >= 2:
                        act.wait_ge(qk_sum, m - 1)
                    fn(SC[:, m % 2], Q[:, t] if t < 8 else KR[:, t - 8], ACT.Square).then_inc(qk_sq, 1)

                for j, tile in enumerate(QKV_TILES):
                    act.wait_ge(unit_done, u0 + j + 1)
                    dst = Q[:, tile] if tile < 8 else (KR[:, tile - 8] if tile < 10 else VP[:, tile - 10, CH:CH + T])
                    fn(h2(dst), halves(2 * (j % 2)), ACT.Copy).then_inc(unit_evac, 1)
                    if j % 2 == 1:
                        if j == 1:
                            act.wait_ge(xn_lo, 4 * KT)
                        act.wait_ge(unit_evac, u0 + j + 1)
                        i = j // 2
                        if i in (1, 2, 3, 4):
                            rms(2 * i - 2)
                            rms(2 * i - 1)
                        if i < 4:
                            square(2 * i)
                            square(2 * i + 1)
                        if i == 5:
                            square(8)
                            square(9)
                for n in range(NCH + NB):
                    act.wait_ge(vw_tr, n + 1)
                    if n < NCH:
                        fn(VW[:, n], PS[:, 4 + n % 4, 0:256], ACT.Copy).then_inc(vw_ready, 1)
                    else:
                        fn(VS[CH:KEYS, n - NCH], PS[0:ST, 4 + n % 4, 0:256], ACT.Copy).then_inc(vw_ready, 1)
                act.wait_ge(qk_sum, 9)
                fn(KN[:, :], PS[:, 4, 0:20], ACT.Sqrt, bias=prm_col("eps"), scale=1.0 / 64).then_inc(qk_rms, 1)
                act.dma_start(o_kv[:, 0], KR[:, :, T - 256:T]).then_inc(stored, 16)
                act.dma_start(o_kv[:, 1], VP[:, :, CH + T - 256:CH + T]).then_inc(stored, 16)

            def exps(u):
                w_, ng = (512, 4) if u < 16 else (8 * KEYS, 8)
                act.wait_ge(sm_sub, u + 1)
                fn(SM[:, u % 2, 3, 0:ng], SM[:, u % 2, 2, 0:ng], ACT.Exp, scale=0.125)
                fn(EE[:, u % 2, 0:w_], EE[:, u % 2, 0:w_], ACT.Exp, scale=0.125).then_inc(sm_exp, 1)

            def transposed(u):
                act.wait_ge(pt_tr, u + 1)
                if u < 16:
                    g = 4 * (u % 2)
                    if u >= 2:
                        act.wait_ge(pv_done, u - 1)
                    fn(PT[:, g:g + 4].rearrange("p g q -> p (g q)"), PS[:, (2, 6)[u % 2], :], ACT.Copy).then_inc(pt_ready, 1)
                else:
                    act.wait_ge(pv_done, u)
                    fn(PT[0:KEYS, 0:4].rearrange("p g q -> p (g q)"), PS[0:KEYS, 2, :], ACT.Copy)
                    fn(PT[0:KEYS, 4:8].rearrange("p g q -> p (g q)"), PS[0:KEYS, 6, :], ACT.Copy).then_inc(pt_ready, 1)

            def out_high(u):
                act.wait_ge(pv_done, u + 1)
                ps, dst = o_tiles(u, XH)
                fn(dst, ps, ACT.Copy).then_inc(o_hi, 1)

            def attention():
                for i in range(UNITS + 2):
                    if i < UNITS:
                        exps(i)
                    if i >= 2:
                        out_high(i - 2)
                    if 0 <= i - 1 < UNITS:
                        transposed(i - 1)

            act.dma_start(ZL[:, :, :], shift).then_inc(z_edge, 16)
            act.dma_start(BC[:, :, :, :], bc5).then_inc(s5_in, 16)
            act.dma_start(HB[:, :, 0], h05).then_inc(s5_in, 16)
            norm(0, 0)
            act.dma_start(o_ck, cko).then_inc(stored, 16)
            act.dma_start(o_cv, cvo).then_inc(stored, 16)
            evac_in()
            s5()
            rwkv()
            norm(1, 2)
            hidden("up00", 0)
            hidden("up01", 1)
            norm(2, 3)
            qkv()
            attention()
            norm(3, 4)
            act.wait_ge(stored, 16 * 7)
            hidden("up10", 2)
            hidden("up11", 3)
            for k in range(KT):
                act.wait_ge(unit_evac, unit0("dn11") + 2 * k + 2)
                act.dma_start(y[:, k], X[:, k]).then_inc(stored, 16)
            act.wait_ge(stored, 16 * (KT + 2 + 2 + 2 + 1))

        @block.vector
        def _(dve):
            o = sequencer(dve, dve_seq)
            v = nc.vector
            tt, ts, stt = v.tensor_tensor, v.tensor_scalar, v.scalar_tensor_tensor
            M, A, S_ = ALU.mult, ALU.add, ALU.subtract

            def h2(ap):
                return ap.rearrange("p (h t) -> p h t", h=2)

            def halves(bank):
                return PS[:, bank:bank + 2, 0:HALF]

            def norm(L, n):
                dve.wait_ge(rms_ready, L + 1)
                o(v.reciprocal(KN[:, 0:5], KN[:, 0:5]))
                v.tensor_copy(SC[:, 2].rearrange("p (a c) -> p a c", c=P),
                              KN[:, 0:5].unsqueeze(2).broadcast_to((P, 5, P))).then_inc(rms_inv, 1)
                rstd = PS[:, 4:6, :].rearrange("p a c -> p (a c)")[:, 0:T]

                def low(k):
                    dve.wait_ge(xn_hi, n * KT + k + 1)
                    tt(XL[:, k], SC[:, (3, 0)[k % 2]], XH[:, k].bitcast(F32), S_).then_inc(xn_lo, 1)
                for k in range(KT):
                    if k >= 2:
                        dve.wait_ge(xn_lo, n * KT + k - 1)
                    if k == 0:
                        dve.wait_ge(rms_spread, L + 1)
                    stt(SC[:, (3, 0)[k % 2]], X[:, k], prm_col("g", 8 * L + k), rstd, M, M).then_inc(xn_t, 1)
                    if k > 0:
                        low(k - 1)
                low(KT - 1)

            def add_square(L, k):
                dve.wait_ge(sq_ready, L * KT + k + 1)
                if k == 1:
                    tt(SC[:, 3], SC[:, 0], SC[:, 1], A).then_inc(sq_added, 1)
                if k > 1:
                    dve.wait_ge(sq_added, (KT - 1) * L + k - 1)
                    tt(SC[:, 3], SC[:, 3], SC[:, k % 2], A).then_inc(sq_added, 1)

            def cmul(outs, a, b, tmp):
                tt(tmp[0], a[0], b[0], M)
                tt(tmp[1], a[1], b[1], M)
                tt(tmp[2], a[0], b[1], M)
                o(tt(tmp[3], a[1], b[0], M))
                for r_out, i_out, pick in outs:
                    tt(r_out, pick(tmp[0]), pick(tmp[1]), S_)
                    o(tt(i_out, pick(tmp[2]), pick(tmp[3]), A))

            def tmps(shape):
                n = 1
                for x in shape:
                    n *= x
                out = []
                for a in range(4):
                    ap = TM[:, a, 0:n]
                    if len(shape) == 2:
                        ap = ap.rearrange("p (a b) -> p a b", a=shape[0])
                    if len(shape) == 3:
                        ap = ap.rearrange("p (a b c) -> p a b c", a=shape[0], b=shape[1])
                    out.append(ap)
                return out

            ident = lambda ap: ap

            def s5_scalars():
                s = [S5[:, i] for i in range(16)]
                dve.wait_ge(params_in, 32)
                dve.wait_ge(s5_in, 32)
                dve.wait_ge(s5_fn, 1)
                o(ts(s[1], prm_cols("lre"), -1e-4, None, ALU.min))
                o(tt(s[2], s[1], s[0], M))
                o(tt(s[3], prm_cols("lim"), s[0], M))
                o(ts(s[5], s[3], 1.0 / 6.283185307179586, ROUND, M, A))
                o(ts(s[5], s[5], -ROUND, None, A))
                o(stt(s[6], s[5], -TWO_PI_HI, s[3], M, A))
                o(stt(s[6], s[5], -TWO_PI_LO, s[6], M, A))
                o(ts(s[6], s[6], 3.1415925, -3.1415925, ALU.min, ALU.max))
                stt(s[7], s[6], -1.0, s[6], M, ALU.max).then_inc(s5_arg, 1)
                dve.wait_ge(s5_fn, 2)
                v.memset(PW[:, 0, :, 0:1], 1.0)
                o(v.memset(PW[:, 1, :, 0:1], 0.0))
                o(tt(PW[:, 0, :, 1], s[4], s[9], M))
                o(tt(PW[:, 1, :, 1], s[4], s[8], M))
                for k in (1, 2, 4):
                    a = [PW[:, ri, :, 1:k + 1] for ri in range(2)]
                    b = [PW[:, ri, :, k:k + 1].broadcast_to((P, NPR5, k)) for ri in range(2)]
                    cmul([(PW[:, 0, :, k + 1:2 * k + 1], PW[:, 1, :, k + 1:2 * k + 1], ident)], a, b, tmps((NPR5, k)))
                for ri in range(2):
                    for n in range(L5):
                        v.tensor_copy(PV[:, ri, :, n:n + 1], PW[:, ri, :, L5 - 1 - n:L5 - n])
                o(ts(s[11], PW[:, 0, :, 1], -1.0, None, A))
                ni, lr, li = PW[:, 1, :, 1], s[1], prm_cols("lim")
                tt(s[12], lr, lr, M)
                o(tt(s[13], li, li, M))
                o(tt(s[12], s[12], s[13], A))
                o(v.reciprocal(s[12], s[12]))
                tt(s[13], s[11], lr, M)
                o(tt(s[14], ni, li, M))
                o(tt(s[13], s[13], s[14], A))
                tt(s[14], ni, lr, M)
                o(tt(s[15], s[11], li, M))
                o(tt(s[14], s[14], s[15], S_))
                tt(s[13], s[13], s[12], M)
                o(tt(s[14], s[14], s[12], M))
                coef = [s[13].unsqueeze(2).broadcast_to((P, NPR5, 16)), s[14].unsqueeze(2).broadcast_to((P, NPR5, 16))]
                cmul([(BB[:, 0], BB[:, 1], ident)], coef, [BC[:, 0], BC[:, 1]], tmps((NPR5, 16)))
                for _ in range(3):
                    cmul([(s[9], s[8], ident)], [s[9], s[8]], [s[9], s[8]], tmps((NPR5,)))
                v.memset(ET[:, 0, :, 0:1], 1.0)
                o(v.memset(ET[:, 1, :, 0:1], 0.0))
                k = 1
                while k < NCP:
                    b = [x.unsqueeze(2).broadcast_to((P, NPR5, k)) for x in (s[9], s[8])]
                    cmul([(ET[:, 0, :, k:2 * k], ET[:, 1, :, k:2 * k], ident)], [ET[:, ri, :, 0:k] for ri in range(2)], b,
                         tmps((NPR5, k)))
                    cmul([(s[9], s[8], ident)], [s[9], s[8]], [s[9], s[8]], tmps((NPR5,)))
                    k *= 2

            def blocks(dst):
                return [(dst[64 * g:64 * g + 64, 0, :, :, 16 * g:16 * g + 16],
                         dst[64 * g:64 * g + 64, 1, :, :, 16 * g:16 * g + 16],
                         lambda ap, g=g: ap[64 * g:64 * g + 64]) for g in range(2)]

            def s5_powers(j5):
                pr = slice(4 * j5, 4 * j5 + 4)
                if j5 > 0:
                    dve.wait_ge(toe_done, j5)
                shape = (P, 4, L5, 16)
                a = [PV[:, ri, pr].unsqueeze(3).broadcast_to(shape) for ri in range(2)]
                b = [BB[:, ri, pr].unsqueeze(2).broadcast_to(shape) for ri in range(2)]
                cmul(blocks(M1T), a, b, tmps((4, L5, 16)))
                v.engine_nop().then_inc(m1t_ready, 1)

            def s5_outs(j5):
                pr = slice(4 * j5, 4 * j5 + 4)
                CL = CL2[:, j5 % 2]
                if j5 < 2:
                    dve.wait_ge(s5_zeros, 1 + 2 * j5)
                shape = (P, 4, L5 + 1, 16)
                a = [PW[:, ri, pr].unsqueeze(3).broadcast_to(shape) for ri in range(2)]
                b = [BC[:, 2 + ri, pr].unsqueeze(2).broadcast_to(shape) for ri in range(2)]
                t = tmps((4, L5 + 1, 16))
                tt(t[0], a[0], b[0], M)
                tt(t[1], a[1], b[1], M)
                tt(t[2], a[0], b[1], M)
                o(tt(t[3], a[1], b[0], M))
                o(tt(t[2], t[2], t[3], A))
                for g in range(2):
                    q = slice(64 * g, 64 * g + 64)
                    tt(CL[q, 0, :, :, 16 * g:16 * g + 16], t[0][q], t[1][q], S_)
                    last = ts(CL[q, 1, :, :, 16 * g:16 * g + 16], t[2][q], -1.0, None, M)
                last.then_inc(cl_ready, 1)
                dve.wait_ge(cl_ready, j5 + 1)

            def s5_states(j5):
                pr = slice(4 * j5, 4 * j5 + 4)
                v.tensor_copy(RHO[:, :, 1:NCP], S5[:, 10, pr].unsqueeze(2).broadcast_to((P, 4, NCP - 1)))
                v.memset(RHO[:, :, 0:1], 0.0)
                dve.wait_ge(xs_evac, 2 * j5 + 2)
                t = tmps((4, NCP))
                e = [ET[:, ri, pr] for ri in range(2)]
                x = [XS[:, ri, :, 0:NCP] for ri in range(2)]
                tt(t[0], x[0], e[0], M)
                tt(t[1], x[1], e[1], M)
                tt(t[2], x[1], e[0], M)
                o(tt(t[3], x[0], e[1], M))
                tt(t[0], t[0], t[1], A)
                o(tt(t[2], t[2], t[3], S_))
                rho = RHO[:, :, :].rearrange("p j c -> p (j c)")
                for a_ in (0, 2):
                    last = v.tensor_tensor_scan(TM[:, a_ + 1, 0:4 * NCP], rho, TM[:, a_, 0:4 * NCP], 0.0, M, A)
                o(last)
                tt(t[0], t[1], e[0], M)
                tt(t[2], t[3], e[1], M)
                o(tt(HS4[:, 0], t[1], e[1], M))
                o(tt(HS4[:, 1], t[3], e[0], M))
                tt(t[0], t[0], t[2], S_)
                o(tt(t[1], HS4[:, 0], HS4[:, 1], A))
                for ri in range(2):
                    v.tensor_copy(HS[:, ri, :, 1:NCP], t[ri][:, :, 0:NCP - 1])
                    last = v.tensor_copy(HE[:, ri, pr], t[ri][:, :, NCP - 1])
                o(last)
                v.engine_nop().then_inc(hs_ready, 1)

            def s5_sum(j5):
                dve.wait_ge(y5_done, j5 + 1)
                for j in range(4):
                    a_ = (j % 2) * 2 * NC5
                    last = stt(UR[:, j, j5], UR[:, j, j5], prm_col("d5", 4 * j5 + j),
                               PS[:, 6 + j // 2, a_:a_ + 2 * NC5], M, A)
                last.then_inc(y5_sum, 1)

            def mix(tile, dst):
                zp = Z[:, tile, 1 + NP_TOK:ZW].rearrange("p (b t) -> p b t", b=NB)
                ds_ = dst[:, NP_TOK:T].rearrange("p (b t) -> p b t", b=NB)
                tt(dst[:, 0:NP_TOK], Z[:, tile, 0:NP_TOK], Z[:, tile, 1:1 + NP_TOK], S_)
                o(tt(ds_, zp[:, :, 0:ST], zp[:, :, 1:1 + ST], S_))
                stt(dst[:, 0:NP_TOK], dst[:, 0:NP_TOK], prm_col("mu", tile), Z[:, tile, 1:1 + NP_TOK], M, A)
                return stt(ds_, ds_, prm_col("mu", tile), zp[:, :, 1:1 + ST], M, A)

            def mix_first():
                dve.wait_ge(unit_evac, 2 * N_IN)
                v.tensor_copy(ZL[:, :, 0:1], Z[:, :, NP_TOK:NP_TOK + 1])
                o(v.tensor_copy(ZL[:, :, 1:1 + NB], Z[:, :, 1 + NP_TOK:ZW].rearrange("p a (b t) -> p a b t", b=NB)[:, :, :, ST]))
                v.engine_nop().then_inc(zl_ready, 1)
                mix(12, TL[:, 0])
                mix(13, TL[:, 1]).then_inc(mixed, 1)
                mix(4, RKV[:, 1]).then_inc(mixed, 1)

            def gelu_arg(j5):
                dve.wait_ge(g_sq, j5 + 1)
                o(ts(GQ, GQ, 0.044715, 1.0, M, A))
                tt(GQ, GQ, UR[:, :, j5], M).then_inc(g_arg, 1)

            def gelu_out(j5):
                dve.wait_ge(g_tanh, j5 + 1)
                stt(UR[:, :, j5], GT[:, :, :], 1.0, UR[:, :, j5], A, M).then_inc(g_out, 1)

            def s5():
                dve.wait_ge(unit_done, 2 * N_IN)
                o(v.memset(M1T[:, :, :, :, :], 0.0))
                s5_powers(0)
                s5_outs(0)
                for j5 in range(4):
                    s5_states(j5)
                    if j5 > 0:
                        gelu_arg(j5 - 1)
                    if j5 + 1 < 4:
                        s5_powers(j5 + 1)
                    if j5 > 0:
                        gelu_out(j5 - 1)
                    if j5 + 1 < 4:
                        s5_outs(j5 + 1)
                    if j5 == 3:
                        mix_first()
                    s5_sum(j5)
                gelu_arg(3)
                gelu_out(3)

            def glu(j):
                dve.wait_ge(glu_tanh, j + 1)
                stt(GO[j], GO[j], 1.0, UF[:, j].rearrange("p t c -> p (t c)"), A, M).then_inc(glu_out, 1)

            def features(p, between):
                R, K, kappa = RKV[:, 0], RKV[:, 1], KAPPA(p)
                T1, T2, T3, T4, T5 = [TP[:, a] for a in range(5)]
                between()
                dve.wait_ge(kk_norm, p + 1)
                o(ts(KN[:, 0:10], KN[:, 0:10], 1e-12, None, ALU.max))
                o(v.reciprocal(KN[:, 0:10], KN[:, 0:10]))
                v.tensor_copy(T5.rearrange("p (a c) -> p a c", c=64),
                              KN[:, 0:10].unsqueeze(2).broadcast_to((P, 10, 64))).then_inc(kk_inv, 1)
                between()
                if p > 0:
                    dve.wait_ge(srw_stored, 16 * p)
                o(ts(T1, T3, 1.0, -0.5 * EXPM05, A, M))
                between()
                for c in range(NCH + NB):
                    a = slice(c * CH, (c + 1) * CH) if c < NCH else slice(NP_TOK + (c - NCH) * ST, NP_TOK + (c - NCH + 1) * ST)
                    last = v.tensor_tensor_scan(T2[:, a], ONES[:, 0:a.stop - a.start], T1[:, a], 0.0, M, A)
                    if c in (3, 7, 15):
                        between()
                o(last)
                tt(T1, T2, T1, S_).then_inc(cs_ready, 1)
                between()
                dve.wait_ge(wa_act, 2 * p + 2)
                o(ts(T4, T4, 0.5, 0.5, M, A))
                between()
                dve.wait_ge(mixed, 2 * p + 3)
                ts(kappa, K, prm_col("k_k", p), None, M)
                o(ts(BETA, T4, -1.0, prm_col("k_a", p), A, M))
                o(stt(K, BETA, 1.0, K, A, M))
                stt(BO[p % 2], R, prm_col("r_k", p), K, M, M).then_inc(bonus_in, 1)
                between()
                dve.wait_ge(kk_spread, p + 1)
                o(tt(T5, PS[:, 0:2, :].rearrange("p a c -> p (a c)")[:, 0:T], kappa, M))
                tt(T4, T5, T4, M).then_inc(b_ready, 1)
                if p == 0:
                    dve.wait_ge(rwkv_zeros, 3)
                dve.wait_ge(decay_exp, p + 1)
                five = lambda ap: ap.rearrange("p (a t) -> p a t", a=5)
                for hh in range(2):
                    r = slice(64 * hh, 64 * hh + 64)
                    stt(AR[r, :, hh, 0], five(T5)[r], -1.0, five(T1)[r], M, M)
                    last = tt(AR[r, :, hh, 1], five(R)[r], five(T3)[r], M)
                o(last)
                v.tensor_copy(PEND[:, p % 2, 0:NCH], T3[:, CH - 1:NP_TOK:CH])
                v.tensor_copy(PEND[:, p % 2, NCH:NCH + NB], T3[:, NP_TOK + ST - 1:T:ST]).then_inc(feat_ready, 1)

            def bonus(p):
                dve.wait_ge(bonus_sum, p + 1)
                tt(h2(BO[p % 2]), halves(2), h2(RKV[:, 2]), M).then_inc(bonus_ready, 1)

            def finish_1(p):
                T3 = TP[:, 2]
                dve.wait_ge(feat_ready, min(p + 2, NPAIR))
                dve.wait_ge(oo_done, p + 1)
                dve.wait_ge(o0_ready, 5 * p + 5)
                tt(h2(T3), halves(4), h2(O0), A).then_inc(o_ready, 1)

            def finish_2(p):
                dve.wait_ge(ln_sum, 3 * p + 1)
                stt(h2(TP[:, 1]), halves(ln_bank(p)), -1.0 / 64, h2(TP[:, 2]), M, A).then_inc(oc_ready, 1)

            def finish_3(p):
                dve.wait_ge(ln_sd, p + 1)
                o(v.reciprocal(KN[:, 0:10], KN[:, 0:10]))
                v.tensor_copy(TP[:, 3].rearrange("p (a c) -> p a c", c=64),
                              KN[:, 0:10].unsqueeze(2).broadcast_to((P, 10, 64))).then_inc(ln_inv, 1)

            def finish_4(p):
                T2 = TP[:, 1]
                dve.wait_ge(ln_spread, p + 1)
                tt(T2, T2, PS[:, ln_bank(p):ln_bank(p) + 2, :].rearrange("p a c -> p (a c)")[:, 0:T], M).then_inc(ln_scaled, 1)
                dve.wait_ge(ln_scaled, p + 1)
                o(ts(T2, T2, prm_col("lnw", p), prm_col("lnb", p), M, A))
                o(tt(T2, T2, BO[p % 2], A))

            def finish_5(p):
                dve.wait_ge(ln_sum, 3 * p + 3)
                tt(Z[:, p, 0:T].rearrange("p (h t) -> p h t", h=2), halves(ln_bank(p)), h2(TP[:, 1]), M).then_inc(ab_out, 1)

            def tile_gm(p, i, hh):
                dve.wait_ge(gram_done, 10 * p + 5 * hh + i + 1)
                mask = CS[:, (C_SS if i == 0 else C_PS) * P:((C_SS if i == 0 else C_PS) + 2) * P]
                tt(GM[:, i, hh].rearrange("p (a c) t -> p a (c t)", a=2), PS[:, i, :].rearrange("p (a c) -> p a c", a=2),
                   mask.unsqueeze(1).broadcast_to((P, 2, 2 * P)), M).then_inc(gm_ready, 1)

            def tile_first(p, i):
                dve.wait_ge(lv_done, 5 * p + i + 1)
                tt(TT[:, i, 0], PS[:, i, 0:256].rearrange("p (h t) -> p h t", h=2),
                   cstt(C_L1).unsqueeze(1).broadcast_to((P, 2, P)), M)
                tt(TT[:, i, 1], GM[:, i, :, 0], cstt(C_U1).unsqueeze(1).broadcast_to((P, 2, P)), M)
                o(v.tensor_copy(AW[:, i, :, 1], PS[:, i, 256:384].rearrange("p (h k) -> p h k", h=2)))
                tv = TT[:, i].rearrange("p a h t -> p (a h) t")
                tt(tv, tv, IDN.unsqueeze(1).broadcast_to((P, 4, P)), A).then_inc(tt_first, 1)

            def level(p, l):
                for i in active(l):
                    dve.wait_ge(lx_done, lvn(p, l, i) + 1)
                    tt(XM[:, i], PS[:, i, 0:256].rearrange("p (h t) -> p h t", h=2),
                       cstt(C_LV + l).unsqueeze(1).broadcast_to((P, 2, P)), M).then_inc(xm_ready, 1)
                for i in active(l):
                    dve.wait_ge(lt_done, lvn(p, l, i) + 1)
                    if l + 1 < LEVELS[i]:
                        tf = TT[:, i].rearrange("p a h t -> p (a h t)")
                        tt(tf, tf, PS[:, i, :], A).then_inc(tt_ready, 1)
                    else:
                        tf = TT[:, i, 1].rearrange("p h t -> p (h t)")
                        tt(tf, tf, PS[:, i, 256:512], A).then_inc(tt_ready, 1)

            def tile_rt(p, i):
                t = ORDER[i]
                dve.wait_ge(ro_done, 5 * p + i + 1)
                for hh in range(2):
                    r = slice(64 * hh, 64 * hh + 64)
                    last = tt(RT(p)[r, t * P:(t + 1) * P], PS[r, i, 0:P], AR[r, t, hh, 1], A)
                last.then_inc(rt_ready, 1)

            def tiles(p):
                for i in range(5):
                    tile_gm(p, i, 0)
                if p > 0:
                    finish_2(p - 1)
                    glu(p - 1)
                for i in range(5):
                    tile_gm(p, i, 1)
                for i in range(5):
                    tile_first(p, i)
                if p > 0:
                    finish_3(p - 1)
                level(p, 0)
                if p > 0:
                    finish_4(p - 1)
                level(p, 1)
                level(p, 2)
                if p > 0:
                    finish_5(p - 1)
                level(p, 3)
                tile_rt(p, 0)
                level(p, 4)

                def quarter(h):
                    q = slice(4 * h, 4 * h + 4)
                    pend = PEND[:, p % 2, NCH + 4 * h:NCH + 4 * h + 4].unsqueeze(2).broadcast_to((P, 4, P))
                    return q, PS[:, (7, 0)[h], :].rearrange("p (b c) -> p b c", b=4), pend
                four = (P, 4, P)
                if p == 0:
                    for a in range(4):
                        dve.wait_ge(y_relayout[a], 16 * 16)
                for h in range(2):
                    q, ps, pend = quarter(h)
                    dve.wait_ge(gh_done, GH_PAIR * p + h + 1)
                    o(tt(GH[:, 0, q], ps, BD.unsqueeze(1).broadcast_to(four), M))
                    tt(GH[:, 0, q], GH[:, 0, q], IDN.unsqueeze(1).broadcast_to(four), A).then_inc(ghs_ready, 1)
                for h in range(2):
                    q, ps, pend = quarter(h)
                    dve.wait_ge(gh_done, GH_PAIR * p + 2 + h + 1)
                    o(tt(GH[:, 1, q], ps, pend, M))
                    tt(GH[:, 1, q], GH[:, 1, q], BD.unsqueeze(1).broadcast_to(four), M).then_inc(ghs_ready, 1)
                for i in range(1, 5):
                    tile_rt(p, i)
                dve.wait_ge(st_done, p * (NCH + 1) + 1)
                dve.wait_ge(ghs_ready, 4 * p + 4)
                for h in range(2):
                    q, ps, pend = quarter(h)
                    o(tt(TM3[:, 0, q], ps, pend, M))
                o(tt(TM3[:, 0], TM3[:, 0], GH[:, 1], A))
                v.engine_nop().then_inc(st_ready, 1)
                v.engine_nop().then_inc(gh_ready, 1)
                for i in range(1, 5):
                    ch = 2 * ORDER[i]
                    ps = PS[:, i, :].rearrange("p (c a k) -> p c a k", c=2, a=2)
                    two = (P, 2, P)
                    dve.wait_ge(gh_done, GH_PAIR * p + 8 + i)
                    tt(GH[:, 0, ch:ch + 2], ps[:, :, 0], BD.unsqueeze(1).broadcast_to(two), M)
                    for c in range(2):
                        last = stt(GH[:, 1, ch + c], ps[:, c, 1], PEND[:, p % 2, ch + c:ch + c + 1], BD, M, M)
                    o(last)
                    tt(GH[:, 0, ch:ch + 2], GH[:, 0, ch:ch + 2], IDN.unsqueeze(1).broadcast_to(two), A).then_inc(gh_ready, 1)

            def chain(p, c):
                if c == 0 and p > 0:
                    dve.wait_ge(prw_stored, 16 * p)
                dve.wait_ge(st_done, p * (NCH + 1) + 2 + c)
                stt(SG[:, c + 1], PS[:, (5, 4)[c % 2], 0:P], PEND[:, p % 2, c:c + 1], GH[:, 1, c], M, A).then_inc(st_ready, 1)

            def rwkv():
                features(0, lambda: None)
                for p in range(NPAIR):
                    if p > 0:
                        finish_1(p - 1)
                    bonus(p)
                    tiles(p)
                    left = list(range(NCH))
                    if p + 1 < NPAIR:
                        features(p + 1, lambda: left and chain(p, left.pop(0)))
                    while left:
                        chain(p, left.pop(0))
                dve.wait_ge(srw_stored, 16 * NPAIR)
                finish_1(NPAIR - 1)
                for k in (4, 5, 6, 0, 1):
                    ab_low(k)
                finish_2(NPAIR - 1)
                glu(NPAIR - 1)
                ab_low(2)
                ab_low(7)
                finish_3(NPAIR - 1)
                finish_4(NPAIR - 1)
                finish_5(NPAIR - 1)
                ab_low(3)

            def ab_low(k):
                dve.wait_ge(xn_hi, KT + AB_ORDER.index(k) + 1)
                if k < 4:
                    tt(XL[:, k], Z[:, k, 0:T], XH[:, k].bitcast(F32), S_).then_inc(xn_lo, 1)
                else:
                    hi = XH[:, k].bitcast(F32)
                    stt(prompt_cols(XL[:, k]), GO5[k - 4][:, :, 0:NCP], 0.25, prompt_cols(hi), M, S_)
                    for h in range(2):
                        last = stt(sample_cols(XL[:, k], h), GO5[k - 4][:, :, NCP + h * NB:NCP + (h + 1) * NB], 0.25,
                                   sample_cols(hi, h), M, S_)
                    last.then_inc(xn_lo, 1)

            def add_tiles(name, L):
                dve.wait_ge(unit_evac, unit0(name))
                for k in range(KT):
                    u = unit0(name) + k
                    dve.wait_ge(unit_done, u + 1)
                    xk = h2(X[:, k])
                    tt(xk, halves(2 * (k % 2)), xk, A).then_inc(unit_evac, 1)
                    if k > 0:
                        add_square(L, k - 1)
                add_square(L, KT - 1)

            def add_halves_norm(name, L):
                u0 = unit0(name)
                dve.wait_ge(unit_evac, u0)
                for k in range(KT):
                    for j in range(2):
                        dve.wait_ge(unit_done, u0 + 2 * k + j + 1)
                        xk = X[:, k, j * HALF:(j + 1) * HALF]
                        tt(xk, PS[:, 2 * j, 0:HALF], xk, A).then_inc(unit_evac, 1)
                    if k > 0:
                        add_square(L, k - 1)
                add_square(L, KT - 1)

            def add_halves(name):
                u0 = unit0(name)
                dve.wait_ge(unit_evac, u0)
                with dve.Fori(0, KT) as i:
                    for j in range(2):
                        dve.wait_ge(unit_done, 2 * i + (u0 + j + 1))
                        xk = X[:, bass.ds(i, 1), j * HALF:(j + 1) * HALF].rearrange("p a t -> p (a t)")
                        tt(xk, PS[:, 2 * j, 0:HALF], xk, A).then_inc(unit_evac, 1)

            def hidden(name, hidx):
                u0, b = unit0(name), FF_TILES * hidx
                with dve.Fori(0, FF_TILES // 2) as i:
                    for j in range(2):
                        dve.wait_ge(unit_evac, 2 * i + (u0 + j + 1))
                        tt(SC[:, 2 + j], SC[:, j], SC[:, j], M).then_inc(h_sq, 1)
                        dve.wait_ge(h_hi, 2 * i + (b + j + 1))
                        m = bass.ds(2 * i + j, 1)
                        tt(HL[:, m].rearrange("p a t -> p (a t)"), SC[:, 2 + j],
                           HH[:, m].rearrange("p a t -> p (a t)").bitcast(F32), S_).then_inc(h_lo, 1)

            def qk_norm(m):
                t = NORM_TILES[m]
                src = Q[:, t] if t < 8 else KR[:, t - 8]
                dve.wait_ge(qk_rms, m + 1)
                r = SC[:, 2 + m % 2]
                o(v.reciprocal(r, r))
                stt(src, src, prm_col("qn" if t < 8 else "kn"), r, M, M).then_inc(qk_ready, 1)

            def last_norms_inv():
                dve.wait_ge(qk_ready, 8)
                dve.wait_ge(qk_rms, 9)
                o(v.reciprocal(KN[:, :], KN[:, :]))
                v.tensor_copy(SC[:, 2:4].rearrange("p m (a c) -> p (m a) c", c=64),
                              KN[:, :].unsqueeze(2).broadcast_to((P, 20, 64))).then_inc(qk_inv, 1)

            def last_norms():
                for m in range(2):
                    t = NORM_TILES[8 + m]
                    dve.wait_ge(qk_spread, m + 1)
                    stt(Q[:, t], Q[:, t], prm_col("qn"), PS[:, 4 + 2 * m:6 + 2 * m, :].rearrange("p a c -> p (a c)")[:, 0:T],
                        M, M).then_inc(qk_ready, 1)

            def qkv():
                dve.wait_ge(unit_done, unit0("qkv"))
                v.memset(VP[:, :, 0:CH], 0.0).then_inc(v_pad, 1)
                qk_norm(0)
                qk_norm(1)
                dve.wait_ge(qk_ready, 2)
                for kv in range(4):
                    i, src = kv // 2, slice(64 * (kv % 2), 64 * (kv % 2) + 64)
                    for half in range(2):
                        r = slice(64 * half, 64 * half + 64)
                        v.tensor_copy(KD[r, kv], KR[src, i, 0:NP_TOK])
                        last = v.tensor_copy(KS[r, kv, :, CH:KEYS], KR[src, i, NP_TOK:T].rearrange("p (b t) -> p b t", b=NB))
                last.then_inc(kd_ready, 1)
                for m in range(2, 8):
                    qk_norm(m)
                last_norms_inv()
                last_norms()

            def sample_queries():
                dve.wait_ge(qk_ready, 10)
                for kv in range(4):
                    last = v.tensor_copy(QSV[:, kv].rearrange("p b a t -> p a b t"),
                                         Q[:, 2 * kv:2 * kv + 2, NP_TOK:T].rearrange("p a (b t) -> p a b t", b=NB))
                last.then_inc(qs_ready, 1)

            def unit_views(u):
                b0 = (0, 4)[u % 2]
                g1, kk, ng = (2, P, 4) if u < 16 else (4, KEYS, 8)
                kv = u // 4
                sink = (SK[:, 4 * kv:4 * kv + 4].rearrange("p (a b) -> p a b", a=2) if u < 16
                        else SK[:, 16:18].unsqueeze(2).broadcast_to((P, 2, 4)))
                ps = PS[:, b0:b0 + 2, 0:g1 * kk].rearrange("p h (a k) -> p h a k", a=g1)
                sm = [SM[:, u % 2, a, 0:ng].rearrange("p (h a) -> p h a", h=2) for a in range(6)]
                e = EE[:, u % 2, 0:ng * kk].rearrange("p (h a k) -> p h a k", h=2, a=g1)
                return ps, sink, sm, e, (P, 2, g1, kk)

            def less_max(u):
                ps, sink, sm, e, shape = unit_views(u)
                dve.wait_ge(sc_done, u + 1)
                if u < 16 and u % 4 == 0:
                    for half in range(2):
                        pv = PS[0:64, (0, 4)[u % 2] + half, 0:256].rearrange("p (a k) -> p a k", a=2)
                        last = v.memset(pv[:, :, 0:64], -1e30)
                    o(last)
                o(v.tensor_reduce(sm[0], ps, AX.X, ALU.max))
                o(tt(sm[1], sm[0], sink, ALU.max))
                tt(sm[2], sink, sm[1], S_)
                if u >= 2:
                    dve.wait_ge(pt_tr, u - 1)
                tt(e, ps, sm[1].unsqueeze(3).broadcast_to(shape), S_).then_inc(sm_sub, 1)

            def over_sum(u):
                ps, sink, sm, e, shape = unit_views(u)
                dve.wait_ge(sm_exp, u + 1)
                o(v.tensor_reduce(sm[4], e, AX.X, A))
                o(tt(sm[4], sm[4], sm[3], A))
                v.reciprocal(sm[5], sm[4]).then_inc(sm_inv, 1)

            def out_low(u):
                dve.wait_ge(o_hi, u + 1)
                ps, dst = o_tiles(u, XL)
                _, hi = o_tiles(u, XH)
                tt(dst, ps, hi.bitcast(F32), S_).then_inc(o_lo, 1)

            def attention():
                for i in range(UNITS + 2):
                    if i < UNITS:
                        less_max(i)
                    if 0 <= i - 1 < UNITS:
                        over_sum(i - 1)
                    if i >= 2:
                        out_low(i - 2)
                    if i == 5:
                        sample_queries()

            dve.wait_ge(z_edge, 16)
            v.tensor_copy(Z[:, :, 0:1], ZL[:, :, 0:1])
            zt = Z[:, :, 1 + NP_TOK:ZW].rearrange("p a (b t) -> p a b t", b=NB)
            v.tensor_copy(zt[:, :, :, 0], ZL[:, :, 1:1 + NB])
            for k in range(KT):
                add_square(0, k)
            dve.wait_ge(params_in, 32)
            o(ts(HP[:, :], PR[:, PRM["w0"][0]:PRM["w0"][0] + 8], 0.5, None, M))
            o(ts(SK[:, :], PR[:, PRM["sinkp"][0]:PRM["sinkp"][0] + 18], 8.0, None, M))
            norm(0, 0)
            s5_scalars()
            s5()
            rwkv()
            add_tiles("out", 1)
            norm(1, 2)
            hidden("up00", 0)
            add_halves("dn00")
            hidden("up01", 1)
            add_halves_norm("dn01", 2)
            norm(2, 3)
            qkv()
            attention()
            add_tiles("ao", 3)
            norm(3, 4)
            for hf in range(2):
                hidden(f"up1{hf}", 2 + hf)
                add_halves(f"dn1{hf}")


SHAPES = [(P, KT, T), (P, A_TILES, 1 + NB), (NPAIR, P, NB, P), (NPAIR, P, P), (P, 2, NPR5), (P, 2, NPR5, NB),
          (P, 2, 2, 256), (NB, 112 * 256), (NB, 112 * 256)]


def constants():
    import numpy as np
    r, c = np.arange(P)[:, None], np.arange(P)[None, :]
    tiles = [r == c, r >= 0 * c, r // 64 == c // 64]
    for ch in (CH, ST):
        same = r // ch == c // ch
        tiles += [same & (r < c), same & (r <= c)]
    pair = (r // 2 == c // 2)
    tiles += [pair & (r > c), pair & (r < c)]
    for m in (2, 4, 8, 16, 32):
        tiles.append((r // (2 * m) == c // (2 * m)) & (r % (2 * m) >= m) & (c % (2 * m) < m))
    tiles = [np.broadcast_to(x, (P, P)) for x in tiles]
    tiles.append(r // ST == np.arange(NB)[None, :])
    return np.concatenate(tiles, axis=1).astype(np.float32)


def cols(a):
    return a.reshape(-1, P).T


def kernel(**inputs):
    import numpy as np
    import concourse.bacc as bacc
    from concourse.bass_utils import run_bass_kernel_spmd

    x = {k: np.asarray(v) for k, v in inputs.items()}
    f = np.float32
    tok = np.concatenate([x["x_prompt"].reshape(NP_TOK, D), x["x_sample"].reshape(NB * ST, D)], axis=0)

    def up(wm):
        n = wm.shape[1] // 256
        return wm.reshape(KT, P, n, 256).transpose(2, 1, 0, 3).reshape(n, P, SLOT)

    def down(wm):
        n = wm.shape[1] // P
        return wm.reshape(FF_TILES, P, n, P).transpose(2, 1, 0, 3).reshape(n, P, SLOT)

    w_qkv = up(x["att_w_qkv"][0])[[4, 0, 1, 2, 5, 3]]
    w_in = up(x["ab_w_in"][0])[[6, 7, 8, 0, 2, 4, 1, 3, 5]]
    slots = [w_in, up(x["ab_w_out"][0])]
    for l in range(2):
        if l:
            slots += [w_qkv, up(x["att_w_out"][0])]
        for h in range(2):
            slots += [up(x["ffn_w1"][l][:, h * 2048:(h + 1) * 2048]), down(x["ffn_w2"][l][h * 2048:(h + 1) * 2048])]
    w = np.concatenate(slots, axis=0)

    def pairs(a):
        return np.moveaxis(a.reshape((NPR5, P) + a.shape[2:]), 1, 0)

    def const(v):
        return np.full((P, 1), v, f)

    d5 = np.broadcast_to(x["s5_d"][0].reshape(NPR5, 1, 32), (NPR5, 4, 32)).reshape(NPR5, P).T
    sinks = x["att_sinks"][0].reshape(4, 2, 2)
    parts = [cols(x["ab_mu"][0])]
    parts += [cols(x[n][0]) for n in ("rwkv_w0", "rwkv_a0", "rwkv_k_k", "rwkv_k_a")]
    parts += [cols(x["rwkv_r_k"][0].reshape(-1)), cols(x["rwkv_lnx_w"][0]), cols(x["rwkv_lnx_b"][0])]
    parts += [cols(x[n][l]) for l in range(2) for n in ("norm_mix", "norm_ffn")]
    parts += [np.tile(x["att_q_norm"][0], 2)[:, None], np.tile(x["att_k_norm"][0], 2)[:, None]]
    parts += [const(1e-6), const(64e-5), const(np.pi / 2), d5, pairs(x["s5_lam_re"][0]), pairs(x["s5_lam_im"][0]),
              pairs(np.broadcast_to(x["s5_log_dt"][0][:, None], (32, 64)))]
    parts += [np.broadcast_to(sinks.transpose(0, 2, 1).reshape(1, 16), (P, 16)),
              np.broadcast_to(sinks[:, :, None, :], (4, 2, ST, 2)).reshape(P, 2)]
    prm = np.concatenate(parts, axis=1)
    bc5 = np.stack([pairs(x["s5_b_re"][0]), pairs(x["s5_b_im"][0]), pairs(x["s5_c_re"][0].transpose(0, 2, 1)),
                    pairs(x["s5_c_im"][0].transpose(0, 2, 1))], axis=1)
    h05 = np.stack([pairs(x[n][0].transpose(1, 2, 0)) for n in ("state_ssm_re", "state_ssm_im")], axis=1)
    s0 = np.zeros((NPAIR, 2, 64, NB, 2, 64), f)
    st = x["state_rwkv"][0].reshape(NB, NPAIR, 2, 64, 64)
    for hh in range(2):
        s0[:, hh, :, :, hh] = st[:, :, hh].transpose(1, 3, 0, 2)
    shift = np.zeros((P, A_TILES, 1 + NB), f)
    shift[:, :, 1:] = x["state_shift"][0].reshape(NB, A_TILES, P).transpose(2, 1, 0)
    ck, cv = x["cache_k"][0], x["cache_v"][0]
    ckT = np.tile(ck[:, 64:].transpose(3, 2, 0, 1), (2, 1, 1, 1))
    arrays = dict(
        xT=tok.T.reshape(KT, P, T).transpose(1, 0, 2), w=w, prm=prm, cst=constants(), shift=shift,
        w2a2=np.concatenate([x["rwkv_w2"][0], x["rwkv_a2"][0]], axis=0), g2=x["rwkv_g2"][0],
        wglu=x["s5_w_glu"][0].reshape(4, P, 512).transpose(1, 0, 2), bc5=bc5, h05=h05,
        s0=s0.reshape(NPAIR, P, NB, P), ckT=ckT, cv=cv[:, 64:].reshape(NB, 64, 256).transpose(1, 0, 2),
        cko=ck[:, ST:].reshape(NB, 112 * 256), cvo=cv[:, ST:].reshape(NB, 112 * 256))

    nc = bacc.Bacc("TRN2", target_bir_lowering=False, num_devices=1)
    ins = {f"in_{n}": np.ascontiguousarray(a) for n, a in arrays.items()}
    args = [nc.dram_tensor(n, a.shape, mybir.dt.from_np(a.dtype), kind="ExternalInput").ap() for n, a in ins.items()]
    args += [nc.dram_tensor(f"out_{i}", s, F32, kind="ExternalOutput").ap() for i, s in enumerate(SHAPES)]
    hybrid_step(nc, *args)
    r = run_bass_kernel_spmd(nc, [ins], core_ids=[0])
    y, shift_o, srw, prw, s5p, s5s, kv, cko, cvo = [r.results[0][f"out_{i}"] for i in range(len(SHAPES))]

    yt = y.transpose(1, 0, 2).reshape(D, T).T
    sh = shift_o.transpose(2, 1, 0).reshape(1 + NB, A_TILES * P)

    def heads(a):
        a = a.reshape(NPAIR, 2, 64, -1, 2, 64)
        d = np.stack([a[:, h, :, :, h] for h in range(2)], axis=1)
        return d.transpose(3, 0, 1, 4, 2).reshape(-1, 8, 64, 64)

    def ungroup(a):
        return np.moveaxis(a, 1, 0).reshape((32, 64) + a.shape[2:])

    def frames(i, lo, n):
        return kv[:, i, :, lo:lo + n].transpose(2, 1, 0).reshape(n, 4, 64)

    def cache(old, i):
        return np.concatenate([old.reshape(NB, 112, 4, 64), frames(i, 128, 128).reshape(NB, ST, 4, 64)], axis=1)[None]

    return (yt[:NP_TOK].reshape(1, NP_TOK, D), yt[NP_TOK:].reshape(NB, ST, D),
            heads(prw)[None], sh[None, 0:1], ungroup(s5p[:, 0])[None, None], ungroup(s5p[:, 1])[None, None],
            frames(0, 0, 128)[None, None], frames(1, 0, 128)[None, None],
            heads(srw)[None], sh[None, 1:], ungroup(s5s[:, 0]).transpose(2, 0, 1)[None],
            ungroup(s5s[:, 1]).transpose(2, 0, 1)[None], cache(cko, 0), cache(cvo, 1))
```
